# Optimizing a Trainium2 kernel written in Bass

```python
import jax, jax.numpy as jnp
from jax import lax
import numpy as np

D_MODEL = 1024
BATCH = 1
SEQ = 256
DEPTH = 2

GRID_W = 64
CTX_LEN = 256
N_EVEN = (DEPTH + 1) // 2
N_ODD = DEPTH // 2
HEAD_DIM = 64
ATTN_HEADS = 8
KV_HEADS = 2
GQA_GROUP = ATTN_HEADS // KV_HEADS
WINDOW = 128
ATTN_BLOCK = 128
ROPE_BASE = 10000.0
GMLP_GROUPS = 8
GMLP_DIM = 64
CHUNK = 128
Q_W = ATTN_HEADS * HEAD_DIM
KV_W = KV_HEADS * HEAD_DIM
A_W = GMLP_GROUPS * GMLP_DIM
IN_W = Q_W + 2 * KV_W + 2 * A_W
MIX_W = Q_W + A_W
POOL_WINDOWS = (2, 4, 8, 16)
POOL_GROUPS = 4
POOL_DIM = D_MODEL // POOL_GROUPS
PEER_HEADS = 8
PEER_NKEYS = 128
PEER_EXPERTS = PEER_NKEYS * PEER_NKEYS
PEER_TOPK = 16
PEER_DKEY = 256
PEER_DHALF = PEER_DKEY // 2
PEER_BLOCK = 128
N_MOD = 6
EPS = 1e-6


def rms_norm(x, g):
    xf = x.astype(jnp.float32)
    y = xf * lax.rsqrt(jnp.mean(jnp.square(xf), axis=-1, keepdims=True) + EPS)
    return (y * g).astype(x.dtype)

def axial_rope(t, row, col):
    half = HEAD_DIM // 2
    quarter = half // 2
    inv = jnp.power(ROPE_BASE, -jnp.arange(quarter, dtype=jnp.float32) / quarter)

    def rot(xa, pos):
        ang = pos[:, None] * inv[None, :]
        cos = jnp.cos(ang)[None, :, None, :]
        sin = jnp.sin(ang)[None, :, None, :]
        x1, x2 = xa[..., :quarter], xa[..., quarter:]
        return jnp.concatenate([x1 * cos - x2 * sin, x1 * sin + x2 * cos], axis=-1)

    tf = t.astype(jnp.float32)
    return jnp.concatenate([rot(tf[..., :half], row), rot(tf[..., half:], col)], axis=-1).astype(t.dtype)

def sink_softmax(logits, sink):
    sk = jnp.broadcast_to(sink.astype(jnp.float32).reshape(1, KV_HEADS, GQA_GROUP, 1, 1), logits.shape[:-1] + (1,))
    return jax.nn.softmax(jnp.concatenate([logits, sk], axis=-1), axis=-1)[..., :-1]

def window_attention(q, k, v, k_ctx, v_ctx, sink):
    B_, L_ = q.shape[0], q.shape[1]
    nb = L_ // ATTN_BLOCK
    span = ATTN_BLOCK + 2 * WINDOW
    scale = HEAD_DIM ** -0.5
    pad = ((0, 0), (WINDOW, WINDOW), (0, 0), (0, 0))
    kp = jnp.pad(k, pad)
    vp = jnp.pad(v, pad)
    qb = q.reshape(B_, nb, ATTN_BLOCK, KV_HEADS, GQA_GROUP, HEAD_DIM).swapaxes(0, 1)

    def one_block(args):
        n, qn = args
        start = n * ATTN_BLOCK
        kn = lax.dynamic_slice_in_dim(kp, start, span, axis=1)
        vn = lax.dynamic_slice_in_dim(vp, start, span, axis=1)
        qpos = start + jnp.arange(ATTN_BLOCK)
        kpos = start - WINDOW + jnp.arange(span)
        valid = (jnp.abs(qpos[:, None] - kpos[None, :]) <= WINDOW) & (kpos >= 0)[None, :] & (kpos < L_)[None, :]
        s_loc = jnp.einsum('bqhgd,bkhd->bhgqk', qn, kn).astype(jnp.float32) * scale
        s_loc = jnp.where(valid, s_loc, -jnp.inf)
        s_ctx = jnp.einsum('bqhgd,bkhd->bhgqk', qn, k_ctx).astype(jnp.float32) * scale
        p = sink_softmax(jnp.concatenate([s_loc, s_ctx], axis=-1), sink)
        o = (jnp.einsum('bhgqk,bkhd->bqhgd', p[..., :span], vn.astype(jnp.float32))
             + jnp.einsum('bhgqk,bkhd->bqhgd', p[..., span:], v_ctx.astype(jnp.float32)))
        return o.astype(q.dtype)

    out = lax.map(one_block, (jnp.arange(nb), qb))
    return out.swapaxes(0, 1).reshape(B_, L_, Q_W)

def context_attention(qc, kc, vc, sink):
    B_, C_ = qc.shape[0], qc.shape[1]
    qg = qc.reshape(B_, C_, KV_HEADS, GQA_GROUP, HEAD_DIM)
    s = jnp.einsum('bqhgd,bkhd->bhgqk', qg, kc).astype(jnp.float32) * (HEAD_DIM ** -0.5)
    p = sink_softmax(s, sink)
    o = jnp.einsum('bhgqk,bkhd->bqhgd', p, vc.astype(jnp.float32))
    return o.astype(qc.dtype).reshape(B_, C_, Q_W)

def chunk_gmlp(ua, va, w_s, b_s):
    B_, L_ = ua.shape[0], ua.shape[1]
    u = jax.nn.gelu(ua).reshape(B_, L_, GMLP_GROUPS, GMLP_DIM)
    vf = jax.nn.gelu(va).reshape(B_, L_, GMLP_GROUPS, GMLP_DIM).astype(jnp.float32)
    mu = jnp.mean(vf, axis=-1, keepdims=True)
    var = jnp.mean(jnp.square(vf - mu), axis=-1, keepdims=True)
    v = ((vf - mu) * lax.rsqrt(var + EPS)).astype(ua.dtype)
    vc = v.reshape(B_, L_ // CHUNK, CHUNK, GMLP_GROUPS, GMLP_DIM)
    mixed = jnp.einsum('gpq,bcqgd->bcpgd', w_s, vc) + b_s.T[:, :, None]
    return (u * mixed.reshape(B_, L_, GMLP_GROUPS, GMLP_DIM)).reshape(B_, L_, A_W)

def split_proj(p):
    return jnp.split(p, [Q_W, Q_W + KV_W, Q_W + 2 * KV_W, Q_W + 2 * KV_W + A_W], axis=-1)

def attn_gmlp_mixer(h, hc, w_in, w_out, sink, w_s, b_s, row, col, need_ctx_out):
    B_, L_ = h.shape[0], h.shape[1]
    C_ = hc.shape[1]
    q, k, v, ua, va = split_proj(h @ w_in)
    q = axial_rope(q.reshape(B_, L_, ATTN_HEADS, HEAD_DIM), row, col)
    k = axial_rope(k.reshape(B_, L_, KV_HEADS, HEAD_DIM), row, col)
    v = v.reshape(B_, L_, KV_HEADS, HEAD_DIM)
    if need_ctx_out:
        qc, kc, vc, uac, vac = split_proj(hc @ w_in)
    else:
        kc, vc = jnp.split(hc @ w_in[:, Q_W:Q_W + 2 * KV_W], 2, axis=-1)
    kc = kc.reshape(B_, C_, KV_HEADS, HEAD_DIM)
    vc = vc.reshape(B_, C_, KV_HEADS, HEAD_DIM)
    attn = window_attention(q, k, v, kc, vc, sink)
    mix = chunk_gmlp(ua, va, w_s, b_s)
    y = jnp.concatenate([attn, mix], axis=-1) @ w_out
    yc = None
    if need_ctx_out:
        attn_c = context_attention(qc.reshape(B_, C_, ATTN_HEADS, HEAD_DIM), kc, vc, sink)
        mix_c = chunk_gmlp(uac, vac, w_s, b_s)
        yc = jnp.concatenate([attn_c, mix_c], axis=-1) @ w_out
    return y, yc

def multiscale_pool(h, w_pool, scale):
    B_, L_ = h.shape[0], h.shape[1]
    hf = h.reshape(B_, L_, POOL_GROUPS, POOL_DIM).astype(jnp.float32)
    cs = jnp.pad(lax.cumsum(hf, axis=1), ((0, 0), (1, 0), (0, 0), (0, 0)))
    t = jnp.arange(L_)
    diffs = []
    for g, w in enumerate(POOL_WINDOWS):
        lo = jnp.clip(t - w // 2, 0, L_)
        hi = jnp.clip(t + w // 2, 0, L_)
        mean = (cs[:, hi, g] - cs[:, lo, g]) / (hi - lo).astype(jnp.float32)[None, :, None]
        diffs.append(mean - hf[:, :, g])
    pooled = jnp.stack(diffs, axis=2).astype(h.dtype)
    y = jnp.einsum('blgc,gce->blge', pooled, w_pool).reshape(B_, L_, D_MODEL)
    return y * scale

def peer_ffn(h, w_q, sub_keys, down, up):
    shape = h.shape
    blocks = h.reshape(-1, PEER_BLOCK, D_MODEL)

    def one_block(xb):
        n = xb.shape[0]
        q = (xb @ w_q).reshape(n, PEER_HEADS, 2, PEER_DHALF)
        s = jnp.einsum('thpk,pnk->thpn', q, sub_keys).astype(jnp.float32)
        s_top, i_top = lax.top_k(s, PEER_TOPK)
        cand_s = s_top[:, :, 0, :, None] + s_top[:, :, 1, None, :]
        cand_i = i_top[:, :, 0, :, None] * PEER_NKEYS + i_top[:, :, 1, None, :]
        best_s, best_pos = lax.top_k(cand_s.reshape(n, PEER_HEADS, -1), PEER_TOPK)
        idx = jnp.take_along_axis(cand_i.reshape(n, PEER_HEADS, -1), best_pos, axis=-1)
        gate = jax.nn.softmax(best_s, axis=-1)
        u = jnp.take(down, idx, axis=0)
        act = jax.nn.gelu(jnp.einsum('thkd,td->thk', u, xb))
        v = jnp.take(up, idx, axis=0)
        return jnp.einsum('thk,thkd->td', (gate * act).astype(v.dtype), v)

    return lax.map(one_block, blocks).reshape(shape)

def first_inputs(seed: int = 0) -> dict:
    key = jax.random.key(seed)
    ks = jax.random.split(key, 20)
    D = D_MODEL

    def nrm(k, shape, s):
        return jax.random.normal(k, shape, jnp.float32) * s

    return {
        'x': nrm(ks[0], (BATCH, SEQ, D), 1.0),
        'c': nrm(ks[1], (BATCH, D), 1.0),
        'ctx': nrm(ks[2], (BATCH, CTX_LEN, D), 1.0),
        'c_ctx': nrm(ks[3], (D,), 1.0),
        'mod_w': nrm(ks[4], (DEPTH, D, N_MOD * D), 0.5 * D ** -0.5),
        'mod_b': nrm(ks[5], (DEPTH, N_MOD * D), 0.02),
        'norm1_g': 1.0 + nrm(ks[6], (DEPTH, D), 0.02),
        'norm2_g': 1.0 + nrm(ks[7], (DEPTH, D), 0.02),
        'attn_in_w': nrm(ks[8], (N_EVEN, D, IN_W), D ** -0.5),
        'attn_out_w': nrm(ks[9], (N_EVEN, MIX_W, D), MIX_W ** -0.5),
        'attn_sink': nrm(ks[10], (N_EVEN, ATTN_HEADS), 0.5),
        'gmlp_w_s': nrm(ks[11], (N_EVEN, GMLP_GROUPS, CHUNK, CHUNK), CHUNK ** -0.5),
        'gmlp_b_s': 1.0 + nrm(ks[12], (N_EVEN, GMLP_GROUPS, CHUNK), 0.02),
        'pool_w': nrm(ks[13], (N_ODD, POOL_GROUPS, POOL_DIM, POOL_DIM), POOL_DIM ** -0.5),
        'pool_scale': 1.0 + nrm(ks[14], (N_ODD, D), 0.02),
        'peer_w_q': nrm(ks[15], (DEPTH, D, PEER_HEADS * PEER_DKEY), D ** -0.5),
        'peer_sub_keys': nrm(ks[16], (DEPTH, 2, PEER_NKEYS, PEER_DHALF), PEER_DHALF ** -0.5),
        'peer_down': nrm(ks[17], (DEPTH, PEER_EXPERTS, D), D ** -0.5),
        'peer_up': nrm(ks[18], (DEPTH, PEER_EXPERTS, D), 0.5),
        'final_g': 1.0 + nrm(ks[19], (D,), 0.02),
    }

def first_block(x, c, ctx, c_ctx, mod_w, mod_b, norm1_g, norm2_g, attn_in_w, attn_out_w, attn_sink,
              gmlp_w_s, gmlp_b_s, pool_w, pool_scale, peer_w_q, peer_sub_keys, peer_down, peer_up, final_g):
    L_ = x.shape[1]
    ROWS = L_ // GRID_W
    t = jnp.arange(ROWS * GRID_W)
    row = (t // GRID_W).astype(jnp.float32)
    col = (t % GRID_W).astype(jnp.float32)
    last_reader = ((DEPTH - 1) // 2) * 2
    xc = ctx
    for l in range(DEPTH):
        has_ctx = l <= last_reader
        keep_ctx = l < last_reader
        m = jax.nn.silu(c) @ mod_w[l] + mod_b[l]
        sh1, sc1, g1, sh2, sc2, g2 = jnp.split(m[:, None, :], N_MOD, axis=-1)
        h = rms_norm(x, norm1_g[l]) * (1.0 + sc1) + sh1
        hc = None
        if has_ctx:
            mc = jax.nn.silu(c_ctx) @ mod_w[l] + mod_b[l]
            csh1, csc1, cg1, csh2, csc2, cg2 = jnp.split(mc, N_MOD, axis=-1)
            hc = rms_norm(xc, norm1_g[l]) * (1.0 + csc1) + csh1
        if l % 2 == 0:
            e = l // 2
            y, yc = attn_gmlp_mixer(h, hc, attn_in_w[e], attn_out_w[e], attn_sink[e],
                                    gmlp_w_s[e], gmlp_b_s[e], row, col, keep_ctx)
        else:
            o = l // 2
            y = multiscale_pool(h, pool_w[o], pool_scale[o])
            yc = multiscale_pool(hc, pool_w[o], pool_scale[o]) if keep_ctx else None
        x = x + g1 * y
        h2 = rms_norm(x, norm2_g[l]) * (1.0 + sc2) + sh2
        x = x + g2 * peer_ffn(h2, peer_w_q[l], peer_sub_keys[l], peer_down[l], peer_up[l])
        if keep_ctx:
            xc = xc + cg1 * yc
            hc2 = rms_norm(xc, norm2_g[l]) * (1.0 + csc2) + csh2
            xc = xc + cg2 * peer_ffn(hc2, peer_w_q[l], peer_sub_keys[l], peer_down[l], peer_up[l])
    return rms_norm(x, final_g)


DEPTH_2 = 1

NSA_HEADS = 8
NSA_KV_GROUPS = 2
NSA_HEADS_PER_GROUP = NSA_HEADS // NSA_KV_GROUPS
NSA_HEAD_DIM = 64
CMP_BLOCK = 32
CMP_STRIDE = 16
CMP_RATIO = CMP_BLOCK // CMP_STRIDE
CMP_HIDDEN = 256
SLC_BLOCK = 64
SLC_TOPK = 16
WINDOW_2 = 512
Q_BLOCK = 128
GLA_HEADS = 4
GLA_KEY_DIM = 64
GLA_VAL_DIM = 128
GLA_RANK = 16
GLA_TAU = 16.0
GLA_CHUNK = 64
MOE_GROUPS = 4
MOE_EXPERTS_PER_GROUP = 8
MOE_N_EXPERTS = MOE_GROUPS * MOE_EXPERTS_PER_GROUP
MOE_TOPK = 2
MOE_D_FF = 512

ROPE_THETA = 10000.0
NEG_INF = -1e30
FORCED_SCORE = 1e4

NSA_Q_W = NSA_HEADS * NSA_HEAD_DIM
NSA_KV_W = NSA_KV_GROUPS * NSA_HEAD_DIM
GLA_QK_W = GLA_HEADS * GLA_KEY_DIM
GLA_V_W = GLA_HEADS * GLA_VAL_DIM
IN_SPLITS = (NSA_Q_W,) + (NSA_KV_W,) * 6 + (3 * NSA_HEADS, GLA_QK_W, GLA_QK_W, GLA_V_W, GLA_RANK, GLA_V_W, D_MODEL, D_MODEL)
IN_WIDTH = sum(IN_SPLITS)


def rms_norm_2(x, g):
    xf = x.astype(jnp.float32)
    y = xf * lax.rsqrt(jnp.mean(xf * xf, axis=-1, keepdims=True) + EPS)
    return (y * g.astype(jnp.float32)).astype(x.dtype)

def rope(x, pos):
    half = x.shape[-1] // 2
    inv = 1.0 / (ROPE_THETA ** (jnp.arange(half, dtype=jnp.float32) / half))
    ang = pos.astype(jnp.float32)[..., None] * inv
    cos, sin = jnp.cos(ang), jnp.sin(ang)
    x1 = x[..., :half].astype(jnp.float32)
    x2 = x[..., half:].astype(jnp.float32)
    return jnp.concatenate([x1 * cos - x2 * sin, x2 * cos + x1 * sin], axis=-1).astype(x.dtype)

def _heads(t, n, dh):
    b, s, _ = t.shape
    return t.reshape(b, s, n, dh).transpose(0, 2, 1, 3)

def compress_blocks(t, pos_emb, w1, b1, w2, b2):
    bsz, g, seq, dh = t.shape
    chunks = t.reshape(bsz, g, seq // CMP_STRIDE, CMP_STRIDE, dh)
    n_cmp = seq // CMP_STRIDE - CMP_RATIO + 1
    blocks = jnp.concatenate([chunks[:, :, m:m + n_cmp] for m in range(CMP_RATIO)], axis=3)
    blocks = blocks + pos_emb
    flat = blocks.reshape(bsz, g, n_cmp, CMP_BLOCK * dh)
    return jax.nn.gelu(flat @ w1 + b1) @ w2 + b2

def cmp_to_slc_overlap(n_cmp, n_slc):
    c0 = CMP_STRIDE * jnp.arange(n_cmp)[:, None]
    s0 = SLC_BLOCK * jnp.arange(n_slc)[None, :]
    ov = jnp.clip(jnp.minimum(c0 + CMP_BLOCK, s0 + SLC_BLOCK) - jnp.maximum(c0, s0), 0, None)
    return ov.astype(jnp.float32) / CMP_BLOCK

def nsa_attention(q, k_c, v_c, k_s, v_s, k_w, v_w, gate_logits, positions,
                  cmp_pos_k, cmp_w1_k, cmp_b1_k, cmp_w2_k, cmp_b2_k,
                  cmp_pos_v, cmp_w1_v, cmp_b1_v, cmp_w2_v, cmp_b2_v):
    f32 = jnp.float32
    bsz, seq, _ = q.shape
    G, hpg, dh = NSA_KV_GROUPS, NSA_HEADS_PER_GROUP, NSA_HEAD_DIM
    pos_h = positions[:, None, :]
    q = (rope(_heads(q, NSA_HEADS, dh), pos_h) * dh ** -0.5).reshape(bsz, G, hpg, seq, dh)
    k_cmp = compress_blocks(_heads(k_c, G, dh), cmp_pos_k, cmp_w1_k, cmp_b1_k, cmp_w2_k, cmp_b2_k)
    v_cmp = compress_blocks(_heads(v_c, G, dh), cmp_pos_v, cmp_w1_v, cmp_b1_v, cmp_w2_v, cmp_b2_v)
    n_cmp = k_cmp.shape[2]
    cmp_end = CMP_STRIDE * jnp.arange(n_cmp) + CMP_BLOCK - 1
    k_cmp = rope(k_cmp, jnp.take(positions, cmp_end, axis=1)[:, None, :])
    n_slc = seq // SLC_BLOCK
    top_n = min(SLC_TOPK, n_slc)
    overlap = cmp_to_slc_overlap(n_cmp, n_slc)
    k_blocks = rope(_heads(k_s, G, dh), pos_h).reshape(bsz, G, n_slc, SLC_BLOCK, dh)
    v_blocks = _heads(v_s, G, dh).reshape(bsz, G, n_slc, SLC_BLOCK, dh)
    pad = ((0, 0), (0, 0), (WINDOW_2, 0), (0, 0))
    k_win = jnp.pad(rope(_heads(k_w, G, dh), pos_h), pad)
    v_win = jnp.pad(_heads(v_w, G, dh), pad)
    gates = jax.nn.sigmoid(gate_logits.astype(f32)).reshape(bsz, seq, NSA_HEADS, 3)
    gates = gates.transpose(0, 2, 1, 3).reshape(bsz, G, hpg, seq, 3)
    b_idx = jnp.arange(bsz)[:, None, None, None]
    g_idx = jnp.arange(G)[None, :, None, None]
    blk_ids = jnp.arange(n_slc)

    def query_block(c):
        q0 = c * Q_BLOCK
        t_idx = q0 + jnp.arange(Q_BLOCK)
        qc = lax.dynamic_slice_in_dim(q, q0, Q_BLOCK, axis=3)
        gc = lax.dynamic_slice_in_dim(gates, q0, Q_BLOCK, axis=3)
        s = jnp.einsum('bghqd,bgnd->bghqn', qc, k_cmp).astype(f32)
        cmp_ok = cmp_end[None, :] <= t_idx[:, None]
        p_cmp = jax.nn.softmax(jnp.where(cmp_ok, s, NEG_INF), axis=-1) * cmp_ok
        o_cmp = jnp.einsum('bghqn,bgnd->bghqd', p_cmp.astype(v_cmp.dtype), v_cmp)
        imp = jnp.einsum('bghqn,nj->bgqj', p_cmp, overlap)
        cur = t_idx // SLC_BLOCK
        forced = (blk_ids[None, :] == 0) | (blk_ids[None, :] == cur[:, None]) | (blk_ids[None, :] == cur[:, None] - 1)
        imp = jnp.where(forced, FORCED_SCORE, imp)
        imp = jnp.where(blk_ids[None, :] <= cur[:, None], imp, NEG_INF)
        _, sel = lax.top_k(imp, top_n)
        k_sel = k_blocks[b_idx, g_idx, sel].reshape(bsz, G, Q_BLOCK, top_n * SLC_BLOCK, dh)
        v_sel = v_blocks[b_idx, g_idx, sel].reshape(bsz, G, Q_BLOCK, top_n * SLC_BLOCK, dh)
        key_pos = (sel[..., None] * SLC_BLOCK + jnp.arange(SLC_BLOCK)).reshape(bsz, G, Q_BLOCK, top_n * SLC_BLOCK)
        sel_ok = (key_pos <= t_idx[:, None])[:, :, None]
        s = jnp.einsum('bghqd,bgqkd->bghqk', qc, k_sel).astype(f32)
        p = jax.nn.softmax(jnp.where(sel_ok, s, NEG_INF), axis=-1)
        o_slc = jnp.einsum('bghqk,bgqkd->bghqd', p.astype(v_sel.dtype), v_sel)
        kw = lax.dynamic_slice_in_dim(k_win, q0, Q_BLOCK + WINDOW_2, axis=2)
        vw = lax.dynamic_slice_in_dim(v_win, q0, Q_BLOCK + WINDOW_2, axis=2)
        kpos = q0 - WINDOW_2 + jnp.arange(Q_BLOCK + WINDOW_2)
        win_ok = (kpos[None, :] >= 0) & (kpos[None, :] <= t_idx[:, None]) & (kpos[None, :] > t_idx[:, None] - WINDOW_2)
        s = jnp.einsum('bghqd,bgkd->bghqk', qc, kw).astype(f32)
        p = jax.nn.softmax(jnp.where(win_ok, s, NEG_INF), axis=-1)
        o_win = jnp.einsum('bghqk,bgkd->bghqd', p.astype(vw.dtype), vw)
        o = gc[..., 0:1] * o_cmp + gc[..., 1:2] * o_slc + gc[..., 2:3] * o_win
        return o.astype(q.dtype)

    out = lax.map(query_block, jnp.arange(seq // Q_BLOCK))
    return out.transpose(1, 0, 4, 2, 3, 5).reshape(bsz, seq, NSA_HEADS * dh)

def gla_attention(q, k, v, a_low, r, w_a2, b_a, norm_g):
    f32 = jnp.float32
    bsz, seq, _ = q.shape
    H, dk, dv, C = GLA_HEADS, GLA_KEY_DIM, GLA_VAL_DIM, GLA_CHUNK
    q = _heads(q, H, dk).astype(f32) * dk ** -0.5
    k = _heads(k, H, dk).astype(f32)
    v = _heads(v, H, dv).astype(f32)
    log_a = _heads(jax.nn.log_sigmoid((a_low @ w_a2 + b_a).astype(f32)) / GLA_TAU, H, dk)
    nc = seq // C

    def to_chunks(t):
        return t.reshape(bsz, H, nc, C, t.shape[-1]).transpose(2, 0, 1, 3, 4)

    causal = jnp.tril(jnp.ones((C, C), dtype=bool))[:, :, None]

    def step(state, xs):
        qc, kc, vc, lac = xs
        b = jnp.cumsum(lac, axis=2)
        o_inter = jnp.einsum('bhtd,bhde->bhte', qc * jnp.exp(b), state)
        diff = b[:, :, :, None, :] - b[:, :, None, :, :]
        decay = jnp.where(causal, jnp.exp(jnp.where(causal, diff, 0.0)), 0.0)
        attn = jnp.einsum('bhtd,bhsd,bhtsd->bhts', qc, kc, decay)
        o_intra = jnp.einsum('bhts,bhse->bhte', attn, vc)
        b_last = b[:, :, -1, :]
        k_dec = kc * jnp.exp(b_last[:, :, None, :] - b)
        state = jnp.exp(b_last)[..., None] * state + jnp.einsum('bhsd,bhse->bhde', k_dec, vc)
        return state, o_inter + o_intra

    state0 = jnp.zeros((bsz, H, dk, dv), f32)
    _, o = lax.scan(step, state0, (to_chunks(q), to_chunks(k), to_chunks(v), to_chunks(log_a)))
    o = o.transpose(1, 2, 0, 3, 4).reshape(bsz, H, seq, dv)
    o = o * lax.rsqrt(jnp.mean(o * o, axis=-1, keepdims=True) + EPS)
    o = o.transpose(0, 2, 1, 3).reshape(bsz, seq, H * dv) * norm_g.astype(f32)
    return (o * jax.nn.silu(r.astype(f32))).astype(r.dtype)

def hybrid_mixer(u, positions, w_in,
                 cmp_pos_k, cmp_w1_k, cmp_b1_k, cmp_w2_k, cmp_b2_k,
                 cmp_pos_v, cmp_w1_v, cmp_b1_v, cmp_w2_v, cmp_b2_v,
                 gla_w_a2, gla_b_a, gla_norm_g, w_proj_nsa, w_proj_gla, w_out):
    z = u @ w_in
    (nsa_q, k_c, v_c, k_s, v_s, k_w, v_w, nsa_g,
     g_q, g_k, g_v, g_a, g_r, m_a, m_b) = jnp.split(z, np.cumsum(IN_SPLITS)[:-1].tolist(), axis=-1)
    y_a = nsa_attention(nsa_q, k_c, v_c, k_s, v_s, k_w, v_w, nsa_g, positions,
                        cmp_pos_k, cmp_w1_k, cmp_b1_k, cmp_w2_k, cmp_b2_k,
                        cmp_pos_v, cmp_w1_v, cmp_b1_v, cmp_w2_v, cmp_b2_v) @ w_proj_nsa
    y_b = gla_attention(g_q, g_k, g_v, g_a, g_r, gla_w_a2, gla_b_a, gla_norm_g) @ w_proj_gla
    mixed = jax.nn.sigmoid(m_a) * y_a + jax.nn.sigmoid(m_b) * y_b
    return mixed @ w_out

def hier_moe(v, w_grp, b_grp, w_exp, b_exp, w_gate, w_up, w_down):
    f32 = jnp.float32
    bsz, seq, d = v.shape
    vt = v.reshape(-1, d)
    grp_prob = jax.nn.softmax((vt @ w_grp + b_grp).astype(f32), axis=-1)
    p_grp, g_sel = lax.top_k(grp_prob, 1)
    exp_logits = (vt @ w_exp + b_exp).astype(f32).reshape(-1, MOE_GROUPS, MOE_EXPERTS_PER_GROUP)
    in_grp = jnp.take_along_axis(exp_logits, g_sel[:, :, None], axis=1)[:, 0]
    p_in, e_sel = lax.top_k(jax.nn.softmax(in_grp, axis=-1), MOE_TOPK)
    w = p_grp * p_in / jnp.sum(p_in, axis=-1, keepdims=True)
    expert_id = g_sel * MOE_EXPERTS_PER_GROUP + e_sel
    combine = jnp.einsum('tk,tke->te', w, jax.nn.one_hot(expert_id, MOE_N_EXPERTS, dtype=f32))
    y = jnp.zeros(vt.shape, f32)
    for e in range(MOE_N_EXPERTS):
        hdn = jax.nn.silu(vt @ w_gate[e]) * (vt @ w_up[e])
        y = y + (combine[:, e:e + 1].astype(hdn.dtype) * hdn) @ w_down[e]
    return y.reshape(bsz, seq, d).astype(v.dtype)

def second_inputs(seed: int = 0) -> dict:
    key = jax.random.key(seed)
    ks = jax.random.split(key, 32)
    f32 = jnp.float32
    L, D, dh = DEPTH_2, D_MODEL, NSA_HEAD_DIM

    def nrm(k, shape, scale):
        return jax.random.normal(k, shape, f32) * scale

    start = jax.random.randint(ks[1], (BATCH,), 0, 1024)
    positions = (start[:, None] + jnp.arange(SEQ)[None, :]).astype(jnp.int32)
    return {
        "x": nrm(ks[0], (BATCH, SEQ, D), 1.0),
        "positions": positions,
        "g_mix": 1.0 + nrm(ks[2], (L, D), 0.02),
        "w_in": nrm(ks[3], (L, D, IN_WIDTH), D ** -0.5),
        "cmp_pos_k": nrm(ks[4], (L, CMP_BLOCK, dh), 0.02),
        "cmp_w1_k": nrm(ks[5], (L, CMP_BLOCK * dh, CMP_HIDDEN), (CMP_BLOCK * dh) ** -0.5),
        "cmp_b1_k": nrm(ks[6], (L, CMP_HIDDEN), 0.01),
        "cmp_w2_k": nrm(ks[7], (L, CMP_HIDDEN, dh), CMP_HIDDEN ** -0.5),
        "cmp_b2_k": nrm(ks[8], (L, dh), 0.01),
        "cmp_pos_v": nrm(ks[9], (L, CMP_BLOCK, dh), 0.02),
        "cmp_w1_v": nrm(ks[10], (L, CMP_BLOCK * dh, CMP_HIDDEN), (CMP_BLOCK * dh) ** -0.5),
        "cmp_b1_v": nrm(ks[11], (L, CMP_HIDDEN), 0.01),
        "cmp_w2_v": nrm(ks[12], (L, CMP_HIDDEN, dh), CMP_HIDDEN ** -0.5),
        "cmp_b2_v": nrm(ks[13], (L, dh), 0.01),
        "gla_w_a2": nrm(ks[14], (L, GLA_RANK, GLA_QK_W), GLA_RANK ** -0.5),
        "gla_b_a": nrm(ks[15], (L, GLA_QK_W), 0.1),
        "gla_norm_g": 1.0 + nrm(ks[16], (L, GLA_V_W), 0.02),
        "w_proj_nsa": nrm(ks[17], (L, NSA_Q_W, D), NSA_Q_W ** -0.5),
        "w_proj_gla": nrm(ks[18], (L, GLA_V_W, D), GLA_V_W ** -0.5),
        "w_out": nrm(ks[19], (L, D, D), D ** -0.5),
        "g_ffn": 1.0 + nrm(ks[20], (L, D), 0.02),
        "w_grp": nrm(ks[21], (L, D, MOE_GROUPS), D ** -0.5),
        "b_grp": nrm(ks[22], (L, MOE_GROUPS), 0.01),
        "w_exp": nrm(ks[23], (L, D, MOE_N_EXPERTS), D ** -0.5),
        "b_exp": nrm(ks[24], (L, MOE_N_EXPERTS), 0.01),
        "w_gate": nrm(ks[25], (L, MOE_N_EXPERTS, D, MOE_D_FF), D ** -0.5),
        "w_up": nrm(ks[26], (L, MOE_N_EXPERTS, D, MOE_D_FF), D ** -0.5),
        "w_down": nrm(ks[27], (L, MOE_N_EXPERTS, MOE_D_FF, D), MOE_D_FF ** -0.5),
        "g_final": 1.0 + nrm(ks[28], (D,), 0.02),
    }

def second_block(x, positions, g_mix, w_in,
              cmp_pos_k, cmp_w1_k, cmp_b1_k, cmp_w2_k, cmp_b2_k,
              cmp_pos_v, cmp_w1_v, cmp_b1_v, cmp_w2_v, cmp_b2_v,
              gla_w_a2, gla_b_a, gla_norm_g, w_proj_nsa, w_proj_gla, w_out,
              g_ffn, w_grp, b_grp, w_exp, b_exp, w_gate, w_up, w_down, g_final):
    h = x
    for layer in range(DEPTH_2):
        u = rms_norm_2(h, g_mix[layer])
        h = h + hybrid_mixer(u, positions, w_in[layer],
                             cmp_pos_k[layer], cmp_w1_k[layer], cmp_b1_k[layer], cmp_w2_k[layer], cmp_b2_k[layer],
                             cmp_pos_v[layer], cmp_w1_v[layer], cmp_b1_v[layer], cmp_w2_v[layer], cmp_b2_v[layer],
                             gla_w_a2[layer], gla_b_a[layer], gla_norm_g[layer],
                             w_proj_nsa[layer], w_proj_gla[layer], w_out[layer])
        h = h + hier_moe(rms_norm_2(h, g_ffn[layer]), w_grp[layer], b_grp[layer], w_exp[layer], b_exp[layer],
                         w_gate[layer], w_up[layer], w_down[layer])
    return rms_norm_2(h, g_final)


def setup_inputs(seed=0):
    out = dict(first_inputs(seed))
    for name, value in second_inputs(seed + 1).items():
        if name != "x":
            out[name + "_2"] = value
    return out


def reference(
    x, c, ctx, c_ctx, mod_w, mod_b, norm1_g, norm2_g, attn_in_w, attn_out_w, attn_sink,
    gmlp_w_s, gmlp_b_s, pool_w, pool_scale, peer_w_q, peer_sub_keys, peer_down, peer_up,
    final_g, positions_2, g_mix_2, w_in_2, cmp_pos_k_2, cmp_w1_k_2, cmp_b1_k_2, cmp_w2_k_2,
    cmp_b2_k_2, cmp_pos_v_2, cmp_w1_v_2, cmp_b1_v_2, cmp_w2_v_2, cmp_b2_v_2, gla_w_a2_2,
    gla_b_a_2, gla_norm_g_2, w_proj_nsa_2, w_proj_gla_2, w_out_2, g_ffn_2, w_grp_2, b_grp_2,
    w_exp_2, b_exp_2, w_gate_2, w_up_2, w_down_2, g_final_2,
):
    x = first_block(
        x, c, ctx, c_ctx, mod_w, mod_b, norm1_g, norm2_g, attn_in_w, attn_out_w, attn_sink,
        gmlp_w_s, gmlp_b_s, pool_w, pool_scale, peer_w_q, peer_sub_keys, peer_down, peer_up,
        final_g,
    )
    return second_block(
        x, positions_2, g_mix_2, w_in_2, cmp_pos_k_2, cmp_w1_k_2, cmp_b1_k_2, cmp_w2_k_2,
        cmp_b2_k_2, cmp_pos_v_2, cmp_w1_v_2, cmp_b1_v_2, cmp_w2_v_2, cmp_b2_v_2, gla_w_a2_2,
        gla_b_a_2, gla_norm_g_2, w_proj_nsa_2, w_proj_gla_2, w_out_2, g_ffn_2, w_grp_2, b_grp_2,
        w_exp_2, b_exp_2, w_gate_2, w_up_2, w_down_2, g_final_2,
    )


_drawn_inputs = setup_inputs


def setup_inputs(seed=0):
    import zlib

    import numpy as np

    out = dict(_drawn_inputs(seed))
    spreads = {}
    factors = {'attn_sink': 8.0,
     'gmlp_b_s': 3.473,
     'pool_scale': 3.291,
     'cmp_pos_k_2': 64.0,
     'cmp_b1_k_2': 64.0,
     'cmp_b2_k_2': 64.0,
     'cmp_pos_v_2': 31.231,
     'cmp_b1_v_2': 28.04,
     'cmp_b2_v_2': 28.212,
     'gla_norm_g_2': 7.335,
     'b_grp_2': 28.96,
     'b_exp_2': 14.339,
     'g_final_2': 8.439,
     'cmp_w1_k_2': 3.696,
     'cmp_w2_k_2': 3.507,
     'g_ffn_2': 4.641}
    for name, (base, spread) in spreads.items():
        noise = np.random.default_rng([zlib.crc32(name.encode()), seed]).standard_normal(out[name].shape)
        drawn = base * np.exp(spread * noise) if base else spread * noise
        out[name] = __import__('jax').numpy.asarray(drawn.astype(out[name].dtype))
    for name, factor in factors.items():
        out[name] = (out[name] * factor).astype(out[name].dtype)
    return out
```

```python
from contextlib import ExitStack

import concourse.bass as bass
import numpy as np
from concourse import mybir

F32 = mybir.dt.float32
U32 = mybir.dt.uint32
I32 = mybir.dt.int32
ALU = mybir.AluOpType
ACT = mybir.ActivationFunctionType
AX = mybir.AxisListType.X

P = 128
T = 256
NT = T // P
D = 1024
KT = D // P
NEG = -1e30
EPS = 1e-6
SLOT = 4096
RING = 4
CAP = 64
PICKS = 128
GSLOTS = 8
EXPERTS = 16384

Z_Q, Z_KC, Z_KS, Z_VS, Z_KW, Z_VW, Z_NG = 0, 512, 768, 896, 1024, 1152, 1280
Z_GQ, Z_GK, Z_GV, Z_GA, Z_GR, Z_MA, Z_MB, Z_W = 1304, 1560, 1816, 2328, 2344, 2856, 3880, 4904


def offsets(sizes):
    at, out = 0, {}
    for name, n in sizes:
        out[name] = (at, n)
        at += n
    return out, at


CONST_AT, CONST_W = offsets([
    ("ident", 128), ("ones", 128), ("win", 512), ("causal", 512), ("cmpmask", 64), ("cmpok", 64),
    ("rope", 128), ("inv", 32), ("glamask", 128), ("reset", 256), ("iota", 64), ("tri", 128), ("band", 2048)])
COL_AT, COL_W = offsets([
    ("c", 8), ("cctx", 8), ("b_a", 2), ("bs", 8), ("posk", 16), ("posv", 16), ("wsT", 1024), ("keysT", 512),
    ("w2k", 128), ("w2v", 128), ("wr", 288), ("wa2", 256)])
ROW_AT, ROW_W = offsets([
    ("sink", 8), ("glag", 512), ("brt", 36), ("b1k", 256), ("b1v", 256), ("b2k", 64), ("b2v", 64)])
G_NAMES = ["norm1_0", "norm2_0", "norm1_1", "pool", "norm2_1", "final_1", "mix", "ffn", "final_2"]


NORMS = ["nctx", "n1_0", "n2_0", "n1_1", "n2_1", "nf1", "nmix", "nffn", "nf2"]
TURNS = ["tctx", "t1_0", "tcat", "t2_0", "t2_1", "tmix", "tzy", "tffn"]


def normed(tag, n):
    return NT * NORMS.index(tag) + n


def turned(tag, n):
    return 4 * TURNS.index(tag) + n


OPERANDS = {"pctx": 2, "tq1": 3, "ppool": 8, "tkc": 2, "th1": 1, "tq2": 4, "tnsa": 2, "tgla": 3, "tkd": 2, "tgo": 2}


def operand(tag, n):
    names = list(OPERANDS)
    return sum(OPERANDS[name] for name in names[:names.index(tag)]) + n


def shape_constants():
    c = np.zeros((P, CONST_W), np.float32)

    def put(name, a):
        at, n = CONST_AT[name]
        c[:, at:at + n] = np.asarray(a, np.float32).reshape(P, n)

    t = np.arange(T)
    tile = t.reshape(NT, P)
    put("ident", np.eye(P))
    put("ones", np.ones((P, P)))
    near = np.abs(tile[:, :, None] - t[None, None, :]) <= 128
    put("win", np.where(near, 0, NEG).transpose(1, 0, 2))
    put("causal", np.where(t[None, None, :] <= tile[:, :, None], 0, NEG).transpose(1, 0, 2))
    n = np.arange(32)
    ok = (16 * n + 31)[None, None, :] <= tile[:, :, None]
    ok = ok & (n < 15)[None, None, :]
    put("cmpmask", np.where(ok, 0, NEG).transpose(1, 0, 2))
    put("cmpok", ok.transpose(1, 0, 2))
    inv = np.power(np.float32(10000.0), -np.arange(16, dtype=np.float32) / np.float32(16)).astype(np.float32)
    row, col = (t // 64).astype(np.float32), (t % 64).astype(np.float32)
    ang = np.stack([row[:, None] * inv, col[:, None] * inv], 1)
    rope = np.stack([np.cos(ang), np.sin(ang)], 1)
    put("rope", rope.reshape(NT, P, 64).transpose(1, 0, 2))
    inv2 = (np.float32(1.0) / np.power(np.float32(10000.0), np.arange(32, dtype=np.float32) / np.float32(32)))
    put("inv", np.broadcast_to(inv2, (P, 32)))
    cs, ct = np.arange(P), np.arange(P)
    put("glamask", (cs[:, None] // 64 == ct[None, :] // 64) & (cs[:, None] % 64 <= ct[None, :] % 64))
    put("reset", np.broadcast_to((t % 64 != 0), (P, T)))
    put("iota", np.broadcast_to(np.arange(64), (P, 64)))
    put("tri", cs[:, None] < ct[None, :])
    band = np.zeros((4, T, T), np.float32)
    for g, w in enumerate((2, 4, 8, 16)):
        for i in range(T):
            lo, hi = max(i - w // 2, 0), min(i + w // 2, T)
            band[g, lo:hi, i] += np.float32(1.0) / np.float32(hi - lo)
            band[g, i, i] -= 1.0
    put("band", band.reshape(4, NT, P, T).transpose(2, 1, 0, 3))
    return c


class Chain:

    def __init__(self, eng, sem):
        self.eng, self.sem, self.n = eng, sem, 0

    def __call__(self, ins):
        ins.then_inc(self.sem, 1)
        self.n += 1
        self.eng.wait_ge(self.sem, self.n)


def program(nc, a, out):
    ctx = ExitStack()
    with ctx:
        def sb(name, shape, dt=F32):
            return ctx.enter_context(nc.sbuf_tensor(name, shape, dt))

        class Sems(dict):

            def __missing__(self, name):
                self[name] = ctx.enter_context(nc.semaphore(name))
                return self[name]

        S = Sems()
        moe_rows = nc.dram_tensor("moe_rows", (32 * CAP, D), F32).ap()

        const = sb("const", [P, CONST_W])
        cols = sb("cols", [P, COL_W])
        rows = sb("rows", [P, ROW_W])
        gvec = sb("gvec", [P, 2, D])
        ring = sb("ring", [P, RING, SLOT])
        x = sb("x", [P, NT, D])
        h = sb("h", [P, NT, D])
        hT = sb("hT", [P, KT, T])
        posi = sb("posi", [P, 3], I32)
        stat = sb("stat", [P, 64])
        ARENA = 20480
        arena = sb("arena", [P, ARENA])
        bank = [ctx.enter_context(nc.psum_tensor(f"bank{i}", [P, 512], F32)) for i in range(8)]

        class Carve:

            def __init__(self, at):
                self.at = at

            def __call__(self, *shape):
                n = int(np.prod(shape))
                assert self.at + n <= ARENA, (self.at, n)
                ap = arena[:, self.at:self.at + n]
                self.at += n
                if len(shape) == 2:
                    return ap.rearrange("p (a b) -> p a b", a=shape[0])
                if len(shape) == 3:
                    return ap.rearrange("p (a b c) -> p a b c", a=shape[0], b=shape[1])
                if len(shape) == 4:
                    return ap.rearrange("p (a b c d) -> p a b c d", a=shape[0], b=shape[1], c=shape[2])
                return ap

        def cst(name):
            at, n = CONST_AT[name]
            return const[:, at:at + n]

        def col(name):
            at, n = COL_AT[name]
            return cols[:, at:at + n]

        def rw(name):
            at, n = ROW_AT[name]
            return rows[:, at:at + n]

        ident = cst("ident")
        ones = cst("ones")
        band = cst("band").rearrange("p (k g t) -> p k g t", k=NT, g=4)
        wsT = col("wsT").rearrange("p (g q) -> p g q", g=8)
        keysT = col("keysT").rearrange("p (l s n) -> p l s n", l=2, s=2)
        wr = col("wr").rearrange("p (k n) -> p k n", k=KT)

        cv = Carve(0)
        mod = cv(6, D)
        m1 = Carve(cv.at)
        cB, cB2 = (hT[:, 4 * i:4 * i + 4, :].rearrange("p a (b c) -> p (a b) c", c=P)
                   for i in range(2))
        modc = m1(2, D)
        ctxn = m1(NT, D)
        m1 = Carve(cv.at)
        proj = m1(NT, 1792)
        mixcat = m1(NT, D)
        qk = m1(NT, 640)
        qT = m1(4, T)
        kT = m1(512)
        kvc = m1(NT, 256)
        sc1 = m1(4, 512)
        pT = m1(4, P)
        tmp1 = m1(NT * 320)
        gst = m1(5, NT * 8)
        ast = m1(6, 4)
        pe_ = Carve(cv.at)
        G = pe_(GSLOTS, D)
        idx_all = pe_(NT, PICKS).bitcast(U32)
        gate = pe_(NT, PICKS)
        act = pe_(NT, PICKS)
        diag = pe_(4, P)
        gt = arena[:, ARENA - 1024:ARENA].rearrange("p (a b) -> p a b", a=2)
        idxb = pe_(GSLOTS).bitcast(U32)
        at_topk = pe_.at
        q16 = Carve(cv.at)(16, T)
        s16 = Carve(cv.at + 4096)(NT, 16, P)
        pk = Carve(at_topk)
        v16 = pk(8, 2, 16)
        i16 = pk(16, 16).bitcast(U32)
        i16f = pk(8, 2, 16)
        bv = pk(8, 16)
        bp = pk(8, 16).bitcast(U32)
        ab = pk(2, PICKS).bitcast(U32)
        abf = pk(2, PICKS)
        sel = pk(2, PICKS)
        gsum = pk(2, 8)
        cand = pk(8, 256)
        onehot = [s16[:, i].rearrange("p a (b c) -> p (a b) c", c=16) for i in range(NT)]

        def kn(w, c0, n):
            return w.rearrange("(k p) n -> p k n", p=P)[:, :, c0:c0 + n]

        loads, freed, wat = [], [], {}

        def stream(tag, aps, used):
            wat[tag] = len(loads)
            loads.extend(aps)
            freed.extend(used(c) for c in range(len(aps)))

        stream("mod0", [kn(a["mod_w"][0], 512 * c, 512) for c in range(12)], lambda c: ("modc" if c < 4 else "mod", c + 1))
        INC = [(512, 512), (0, 512), (1024, 512), (1536, 256)]
        stream("in1", [kn(a["attn_in_w"], c0, n) for c0, n in INC], lambda c: ("pin1", 2 * c + 2))
        stream("out1", [kn(a["attn_out_w"], 512 * c, 512) for c in range(2)], lambda c: ("pout1", 2 * c + 2))
        stream("wq0", [kn(a["peer_w_q"][0], 512 * c, 512) for c in range(4)], lambda c: ("pq", 4 * c + 4))
        stream("mod1", [kn(a["mod_w"][1], 512 * c, 512) for c in range(12)], lambda c: ("mod", 12 + c + 1))
        stream("pool", [a["pool_w"].rearrange("g (k p) e -> p (g k) e", p=P)], lambda c: ("py_pool", 4))
        stream("wq1", [kn(a["peer_w_q"][1], 512 * c, 512) for c in range(4)], lambda c: ("pq", 16 + 4 * c + 4))
        ZC = [(512 * c, min(512, Z_W - 512 * c)) for c in range(10)]
        stream("in2", [kn(a["w_in_2"], c0, n) for c0, n in ZC], lambda c: ("pin2", 2 * c + 2))
        stream("w1k", [a["cmp_w1_k_2"].rearrange("(k p) n -> p k n", p=P)], lambda c: ("hid", 1))
        stream("w1v", [a["cmp_w1_v_2"].rearrange("(k p) n -> p k n", p=P)], lambda c: ("hid", 2))
        stream("nsa", [a["w_proj_nsa_2"].rearrange("(k p) n -> p k n", p=P)], lambda c: ("branch", 4))
        stream("gla", [a["w_proj_gla_2"].rearrange("(k p) n -> p k n", p=P)], lambda c: ("branch", 8))
        stream("out2", [kn(a["w_out_2"], 512 * c, 512) for c in range(2)], lambda c: ("pout2", 2 * c + 2))

        def slot(i):
            _, k, n = loads[i].shape
            return ring[:, i % RING, 0:k * n].rearrange("p (k n) -> p k n", k=k)

        w_landed = [S[f"w_landed{i}"] for i in range(RING)]

        def wait_weight(eng, i):
            eng.wait_ge(w_landed[i % RING], 16 * (i // RING + 1))

        g_landed = [S[f"g_landed{i}"] for i in range(2)]

        def wait_gain(eng, name):
            i = G_NAMES.index(name)
            eng.wait_ge(g_landed[i % 2], 16 * (i // 2 + 1))
            return gvec[:, i % 2, :]

        mo = Carve(0)
        w_moe = [ring[:, i, :] for i in range(RING)] + [mo(SLOT) for _ in range(2)]
        moe_landed = [S[f"moe_landed{i}"] for i in range(6)]
        hdn = mo(4, T)
        sg = mo(2, T)
        cmb = mo(NT, 32)
        mst = mo(16, 36)
        pick = mo(NT, 2, 32)
        chosen = mo(NT, 32)
        place = mo(NT, 34)
        wts = mo(NT, 2)
        ptmp = mo(NT, 2, 32)
        prow = mo(NT * 2)
        pidx = mo(NT * 2).bitcast(U32)
        crowd = mo(1).bitcast(I32)
        msel = mo(2, NT, CAP)
        xs = mo(2, KT, CAP)
        hsel = mo(2, 4, CAP)
        ysb = mo(2, D)
        yback = ring[:, 0, :].rearrange("p (n d) -> p n d", n=4)

        b2 = Carve(0)
        z = b2(NT, Z_W)
        zcat = b2(NT, 512)
        zT = b2(4, T)
        zy = h
        at_b2 = b2.at
        trig = b2(3, 2, 32)
        tang = b2(6, 32)
        qr = b2(NT, 768)
        kcd = b2(NT, 4, P)
        rtmp = b2(384)
        kdT = Carve(b2.at)(4, T)
        X = Carve(b2.at + 1024)(2, 16, 64)
        nq = Carve(b2.at)
        nqT = nq(4, T)
        kswT = nq(512)
        kcT = nq(64)
        vcz = nq(2, 64)
        c2 = Carve(nq.at)
        H1 = c2(2, 256)
        H1T = c2(2, 2, 64)
        kc2 = c2(128)
        ctmp = c2(128)
        ns = Carve(nq.at)
        psc = ns(8, T)
        nst = ns(8, 8)
        gsig = ns(NT, 24)
        npT = Carve(at_b2 + 192 + 192)(4, P)
        pcm = Carve(at_b2 + 192 + 192 + 512)(4, 64)
        pcT = Carve(at_b2 + 192 + 192 + 768)(4, P)
        cst2 = Carve(at_b2 + 192 + 192 + 1280)(4, 8)

        gl = Carve(at_b2)
        gqT = gl(2, T)
        gkT = gl(2, T)
        gaT = gl(T)
        bb = gl(2, T)
        gt1 = gl(2, T)
        gt2 = gl(2, T)
        kdn = gl(NT, 256)
        QZ = gl(2, 4, P)
        QM = gl(2, 2, 256)
        zx = z[:, :, Z_MA:Z_MB]
        Ek = [h[:, :, :].rearrange("p a b -> p (a b)"), hT[:, :, :].rearrange("p a b -> p (a b)")]
        AT = gl(4, P)
        st = gl(4, 2, 256)
        gel = gl(8)
        gso = gl(8)

        def flat(ap):
            return ap.rearrange("p a b -> p (a b)")

        block = ctx.enter_context(nc.Block())

        @block.sync
        def _(sp):
            sp.dma_start(cols[:, :], a["cols"]).then_inc(S["in_cols"], 16)
            sp.dma_start(x[:, :, :], a["x"].rearrange("(t p) d -> p t d", p=P)).then_inc(S["in_x"], 16)
            sp.dma_start(ctxn, a["ctx"].rearrange("(t p) d -> p t d", p=P)).then_inc(S["in_ctx"], 16)
            sp.dma_start(posi[:, :], a["pos3"]).then_inc(S["in_pos"], 16)
            sp.dma_start(const[:, :], a["const"]).then_inc(S["in_const"], 16)
            sp.dma_start(rows[:, :], a["rows"].to_broadcast([P, ROW_W])).then_inc(S["in_rows"], 16)

            def load_mod_bias(l):
                sp.dma_start(flat(mod), a["mod_b"][l:l + 1, :].to_broadcast([P, 6 * D])).then_inc(S["in_modb"], 16)
                if l == 0:
                    sp.dma_start(flat(modc), a["mod_b"][0:1, 0:2 * D].to_broadcast([P, 2 * D])).then_inc(S["in_modcb"], 16)

            def load_gain(i):
                if i >= 2:
                    sp.wait_ge(S["gain_used"], i - 1)
                sp.dma_start(gvec[:, i % 2, :], a["gains"][i:i + 1, :].to_broadcast([P, D])).then_inc(g_landed[i % 2], 16)

            def load_weight(i):
                if i >= RING:
                    sem, value = freed[i - RING]
                    sp.wait_ge(S[sem], value)
                sp.dma_start(slot(i), loads[i]).then_inc(w_landed[i % RING], 16)

            def load_weights(tag, n):
                for i in range(wat[tag], wat[tag] + n):
                    load_weight(i)

            load_mod_bias(0)
            load_gain(0)
            load_gain(1)
            load_weights("mod0", 12)
            load_weights("in1", 4)
            load_weights("out1", 2)
            load_weights("wq0", 4)
            load_gain(2)
            sp.wait_ge(S["x_peer"], NT)
            load_mod_bias(1)
            load_weights("mod1", 12)
            load_gain(3)
            load_weights("pool", 1)
            load_gain(4)
            load_weights("wq1", 4)
            load_gain(5)
            load_gain(6)
            load_weights("in2", 10)
            load_weights("w1k", 1)
            load_weights("w1v", 1)
            load_weights("nsa", 1)
            load_gain(7)
            load_weights("gla", 1)
            load_weights("out2", 2)
            load_gain(8)
            sp.wait_ge(S["x_mix"], NT * 3)

            def load_expert(i, k, first):
                for j, w in enumerate(("w_gate_2", "w_up_2", "w_down_2")):
                    if not first:
                        sp.wait_ge(S["moe_u" if j < 2 else "moe_y"], i * 8 + (4 * k - 4))
                    kk = 8 if j < 2 else 4
                    src = a[w].rearrange("(e b) k n -> e b k n", b=2)[bass.ds(i, 1), k]
                    src = src.rearrange("e (k p) n -> p (e k) n", p=P)
                    sp.dma_start(w_moe[3 * k + j].rearrange("p (k n) -> p k n", k=kk), src).then_inc(
                        moe_landed[3 * k + j], 16)

            load_expert(0, 0, True)
            load_expert(0, 1, True)
            with sp.Fori(1, 16) as i:
                for k in range(2):
                    load_expert(i, k, False)

            sp.wait_ge(S["out_ready"], NT)
            sp.dma_start(out.rearrange("(t p) d -> p t d", p=P), h[:, :, :]).then_inc(S["stored"], 16)
            sp.wait_ge(S["stored"], 16)

        @block.gpsimd
        def _(pool):
            def gather_pass(l, n, table, tile):
                done = 4 * l + n

                def group(i, s, first):
                    if first:
                        if n in (1, 2):
                            pool.wait_ge(S["down_used"], PICKS * (2 * l + n) - GSLOTS + s + 4)
                        elif n == 3:
                            pool.wait_ge(S["up_used"], 4 + PICKS * (2 * l + 1) - GSLOTS + s + 4)
                    else:
                        used, before = (S["down_used"], 2 * l + n) if n < 2 else (S["up_used"], 2 * l + n - 2)
                        pool.wait_ge(used, i * GSLOTS + (PICKS * before - GSLOTS + s + 4 + (0 if n < 2 else 4)))
                    turn = done * 32 + 2 * i + s // 4
                    src = idx_all[:, tile, bass.ds(i * GSLOTS + s, 4)]
                    pool.tensor_copy(idxb[:, s:s + 4], src).then_inc(S["idx_copied"], 1)
                    pool.wait_ge(S["idx_copied"], turn + 1)
                    pool.sem_inc(S["idx_seen"], 1)
                    for q in range(s, s + 4):
                        pool.indirect_dma_start(
                            out=G[:, q, :], out_offset=None, in_=table,
                            in_offset=bass.IndirectOffsetOnAxis(ap=idxb[:, q:q + 1], axis=0)).then_inc(S[f"gathered{q}"], 16)

                if n < 2:
                    pool.wait_ge(S["idx_ready"], 2 * l + n + 1)
                for s in (0, 4):
                    group(0, s, True)
                with pool.Fori(1, PICKS // GSLOTS) as i:
                    for s in (0, 4):
                        group(i, s, False)

            for l in range(2):
                pool.wait_ge(S["idx_ready"], 2 * l + 2)
                gather_pass(l, 0, a["down"], 0)
                gather_pass(l, 1, a["down"], 1)
                gather_pass(l, 2, a["up"], 0)
                gather_pass(l, 3, a["up"], 1)
            pool.wait_ge(S["crowd"], 1)
            crowded = pool.value_load(crowd[0:1, 0:1], min_val=0, max_val=1)
            with pool.If(crowded == 0):
                for k in range(2):
                    pool.wait_ge(S[f"rows_stored{k}"], 16 * 17)
                for n in range(4):
                    pool.indirect_dma_start(out=yback[:, n, :], out_offset=None, in_=moe_rows,
                                            in_offset=bass.IndirectOffsetOnAxis(ap=pidx[:, n:n + 1], axis=0)).then_inc(
                        S[f"gathered{n}"], 16)

        @block.scalar
        def _(act_):
            link = Chain(act_, S["act_chain"])

            def evac(tag, dsts, banks, before=0):
                for k, (dst, src) in enumerate(zip(dsts, banks)):
                    if tag in OPERANDS:
                        act_.wait_ge(S["operands"], operand(tag, k + 1))
                    else:
                        act_.wait_ge(S[tag], before + k + 1)
                    act_.activation(dst, src, ACT.Copy).then_inc(S["operands_ev" if tag in OPERANDS else tag + "_ev"], 1)

            def norm(tag, src, junk):
                for t in range(NT):
                    act_.activation(junk[:, t], src[:, t], ACT.Square, accum_out=stat[:, t:t + 1]).then_inc(S["norm_sum"], 1)
                act_.wait_ge(S["norm_mean"], NORMS.index(tag) + 1)
                act_.activation(stat[:, 4:6], stat[:, 2:4], ACT.Sqrt).then_inc(S["norm_root"], 1)

            def transposes_out(tag):
                for g in range(4):
                    act_.wait_ge(S["turned"], turned(tag, g + 1))
                    act_.activation(hT[:, 4 * (g % 2):4 * (g % 2) + 4, P * (g // 2):P * (g // 2) + P],
                                    bank[g][:, :].rearrange("p (k t) -> p k t", k=4), ACT.Copy).then_inc(S["turned_ev"], 1)

            act_.sem_inc(S["rows_stored0"], 16)
            act_.sem_inc(S["rows_stored1"], 16)
            act_.wait_ge(S["in_cols"], 16)
            act_.activation(cols[:, 0:16], cols[:, 0:16], ACT.Silu).then_inc(S["silu_c"], 1)
            act_.wait_ge(S["in_ctx"], 16)
            norm("nctx", ctxn, h)
            transposes_out("tctx")
            evac("pctx", [kvc[:, t, :] for t in range(NT)], [bank[4 + t][:, 0:256] for t in range(NT)])
            act_.wait_ge(S["in_x"], 16)
            act_.wait_ge(S["turned"], turned("tctx", 4))
            norm("n1_0", x, h)
            transposes_out("t1_0")
            evac("pin1", [proj[:, t, c0:c0 + n] for c0, n in INC for t in range(NT)],
                 [bank[4 + k % 4][:, 0:INC[k // 2][1]] for k in range(8)])
            act_.wait_ge(S["pin1_ev"], 8)
            for t in range(NT):
                act_.activation(proj[:, t, 768:1792], proj[:, t, 768:1792], ACT.Gelu_apprx_tanh).then_inc(S["gelu1"], 1)
            act_.wait_ge(S["gmlp_v"], 1)
            act_.activation(gst[:, 2], gst[:, 1], ACT.Sqrt).then_inc(S["g_rt"], 1)
            evac("tq1", [qT[:, :, 0:P], qT[:, :, P:T], kT[:, 0:512]],
                 [bank[0][:, :].rearrange("p (k t) -> p k t", k=4), bank[1][:, :].rearrange("p (k t) -> p k t", k=4), bank[2][:, :]])
            for it in range(4):
                act_.wait_ge(S["a_negm"], it + 1)
                for p in range(4):
                    act_.activation(sc1[:, p], sc1[:, p], ACT.Exp, bias=ast[:, 2, p:p + 1],
                                    accum_out=ast[:, 4, p:p + 1]).then_inc(S["a_exp"], 1)
                act_.activation(ast[:, 3], ast[:, 3], ACT.Exp).then_inc(S["a_exp"], 1)
                for p in range(4):
                    k = 4 * it + p
                    act_.wait_ge(S["a_pt"], k + 1)
                    if k:
                        act_.wait_ge(S["a_pv"], k)
                    act_.activation(flat(pT), bank[4 + k % 2][:, :], ACT.Copy).then_inc(S["a_pt_ev"], 1)
            transposes_out("tcat")

            def peer(l):
                act_.wait_ge(S["x_mix"], NT * (l + 1))
                norm(f"n2_{l}", x, h)
                transposes_out(f"t2_{l}")
                evac("pq", [q16[:, k, :] for k in range(16)], [bank[4 + k % 4][:, 0:T] for k in range(16)], 16 * l)
                evac("ps", [s16[:, k // 4, 4 * (k % 4):4 * (k % 4) + 4, :] for k in range(8)],
                     [bank[k % 4][:, :].rearrange("p (a b) -> p a b", a=4) for k in range(8)], 8 * l)
                for t in range(NT):
                    act_.wait_ge(S["gate_in"], NT * l + t + 1)
                    act_.activation(gate[:, t], gate[:, t], ACT.Exp).then_inc(S["gate_exp"], 1)
                for t in range(NT):
                    act_.wait_ge(S["down_used"], PICKS * (2 * l + t + 1))
                    act_.activation(act[:, t], act[:, t], ACT.Gelu_apprx_tanh).then_inc(S["peer_gelu"], 1)
                for t in range(NT):
                    act_.wait_ge(S["peer_w"], NT * l + t + 1)
                    n0 = PICKS * (NT * l + t)
                    with act_.Fori(0, PICKS // 4) as i:
                        for s in range(4):
                            act_.wait_ge(S["up_used"], i * 4 + (n0 + s + 1))
                            act_.activation(diag[:, s], ident, ACT.Copy,
                                            scale=act[:, t, bass.ds(i * 4 + s, 1)]).then_inc(S["diag_made"], 1)

            peer(0)
            act_.wait_ge(S["x_peer"], NT)
            act_.wait_ge(S["up_used"], 4 + 2 * PICKS)
            norm("n1_1", x, h)
            evac("ppool", [hT[:, k, :] for k in range(8)], [bank[4 + k % 4][:, 0:T] for k in range(8)])
            peer(1)
            act_.wait_ge(S["x_peer"], 2 * NT)
            norm("nf1", x, h)
            act_.wait_ge(S["x_block1"], NT)
            norm("nmix", x, h)
            transposes_out("tmix")
            evac("pin2", [z[:, t, c0:c0 + n] for c0, n in ZC for t in range(NT)],
                 [bank[4 + k % 4][:, 0:ZC[k // 2][1]] for k in range(20)])
            act_.wait_ge(S["angles"], 1)
            act_.activation(trig[:, :, 1, :], tang[:, 0:3, :], ACT.Sin).then_inc(S["trig"], 1)
            act_.activation(trig[:, :, 0, :], tang[:, 3:6, :], ACT.Sin).then_inc(S["trig"], 1)
            evac("tkc", [kdT[:, 2 * g:2 * g + 2, :] for g in range(2)],
                 [bank[g][:, :].rearrange("p (k t) -> p k t", k=2) for g in range(2)])
            act_.wait_ge(S["cmp_v"], 1)
            act_.activation(flat(H1)[0:64], flat(H1)[0:64], ACT.Gelu_apprx_tanh).then_inc(S["h1_gelu"], 1)
            evac("th1", [H1T.rearrange("p a b c -> p (a b c)")], [bank[2][:, 0:256]])
            evac("tq2", [nqT[:, :, 0:P], nqT[:, :, P:T], kswT[:, 0:512]],
                 [bank[4][:, :].rearrange("p (k t) -> p k t", k=4), bank[5][:, :].rearrange("p (k t) -> p k t", k=4),
                  bank[6][:, :]])
            act_.wait_ge(S["operands"], operand("tq2", 4))
            act_.wait_ge(S["cmp_v"], 3)
            act_.activation(kcT[0:64, 0:32], bank[7][0:64, 0:32], ACT.Copy)
            act_.activation(kcT[64:128, 32:64], bank[7][64:128, 32:64], ACT.Copy).then_inc(S["operands_ev"], 1)
            act_.activation(gsig, z[:, :, Z_NG:Z_NG + 24], ACT.Sigmoid).then_inc(S["z_acts"], 1)
            for t in range(NT):
                act_.wait_ge(S["c_sub"], t + 1)
                act_.activation(pcm, pcm, ACT.Exp).then_inc(S["c_exp"], 1)
                act_.wait_ge(S["c_pt"], t + 1)
                act_.activation(pcT[0:64], bank[6][0:64, :].rearrange("p (k t) -> p k t", k=4), ACT.Copy).then_inc(S["c_pt_ev"], 1)
                for j in range(2):
                    it = 2 * t + j
                    act_.wait_ge(S["b_negm"], it + 1)
                    for q in range(8):
                        act_.activation(psc[:, q], psc[:, q], ACT.Exp, bias=nst[:, 1, q:q + 1],
                                        accum_out=nst[:, 2, q:q + 1]).then_inc(S["b_exp"], 1)
                    for p in range(4):
                        k = 4 * it + p
                        act_.wait_ge(S["b_pt"], k + 1)
                        if k:
                            act_.wait_ge(S["b_pv"], k)
                        nb = 2 * (t + 1)
                        act_.activation(npT[:, 0:nb], bank[4 + k % 2][:, 0:P * nb].rearrange("p (k t) -> p k t", k=nb),
                                        ACT.Copy).then_inc(S["b_pt_ev"], 1)
                act_.wait_ge(S["b_pv"], 4 * (2 * t + 2))
                act_.activation(zcat[:, t], bank[7][:, :], ACT.Copy).then_inc(S["nsa_o"], 1)
            evac("tnsa", [zT[:, :, P * t:P * t + P] for t in range(NT)],
                 [bank[t][:, :].rearrange("p (k t) -> p k t", k=4) for t in range(NT)])
            for t in range(NT):
                act_.activation(z[:, t, Z_MA:Z_W], z[:, t, Z_MA:Z_W], ACT.Sigmoid).then_inc(S["z_acts"], 1)
            evac("tgla", [gqT, gkT, gaT[0:16]],
                 [bank[0][:, :].rearrange("p (k t) -> p k t", k=2), bank[1][:, :].rearrange("p (k t) -> p k t", k=2),
                  bank[2][0:16, 0:256]])
            act_.wait_ge(S["gla_v"], 1)
            act_.activation(gt2, gt2, ACT.Exp, scale=-1.0).then_inc(S["gla_a"], 1)
            act_.wait_ge(S["gla_a"], 1)
            act_.activation(gt2, gt2, ACT.Ln, bias=1.0).then_inc(S["gla_a"], 1)
            act_.wait_ge(S["gla_v"], 2)
            act_.activation(gt1, bb, ACT.Exp).then_inc(S["gla_a"], 1)
            act_.activation(gel.rearrange("p (a c) -> p a c", a=2),
                            bb.rearrange("p a (c s) -> p a c s", s=64)[:, :, :, 63], ACT.Exp).then_inc(S["gla_a"], 1)
            act_.wait_ge(S["gla_v"], 3)
            act_.activation(gt2, gt2, ACT.Exp).then_inc(S["gla_a"], 1)
            evac("tkd", [kdn.rearrange("p t (a b) -> p a t b", a=2)[:, k] for k in range(2)],
                 [bank[k][:, 0:256].rearrange("p (t b) -> p t b", t=2) for k in range(2)])
            for k in range(16):
                act_.wait_ge(S["ek_sub"], k + 1)
                act_.activation(Ek[k % 2], Ek[k % 2], ACT.Exp).then_inc(S["ek_exp"], 1)
            act_.wait_ge(S["go_v"], 1)
            act_.activation(gso, gso, ACT.Sqrt).then_inc(S["go_rt"], 1)
            act_.activation(z[:, :, Z_GR:Z_MA], z[:, :, Z_GR:Z_MA], ACT.Silu).then_inc(S["z_acts"], 1)
            evac("tgo", [zT[:, :, P * t:P * t + P] for t in range(NT)],
                 [bank[t][:, :].rearrange("p (k t) -> p k t", k=4) for t in range(NT)])
            transposes_out("tzy")
            act_.wait_ge(S["x_mix"], NT * 3)
            norm("nffn", x, h)
            transposes_out("tffn")
            for t in range(NT):
                act_.wait_ge(S["r_sub"], t + 1)
                act_.activation(mst[:, 6, 0:5], mst[:, 5, 0:5], ACT.Exp).then_inc(S["r_exp"], 1)
            act_.wait_ge(S["crowd"], 1)
            crowded = act_.value_load(crowd[0:1, 0:1], min_val=0, max_val=1)
            with act_.If(crowded == 0):
                def tokens(k, n):
                    act_.wait_ge(S["x_sel"], n)
                    act_.activation(xs[:, k].rearrange("p a b -> p (a b)"), bank[k][:, :], ACT.Copy).then_inc(S["x_sel_ev"], 1)

                tokens(0, 1)
                with act_.Fori(0, 16) as i:
                    for k in range(2):
                        act_.wait_ge(S["moe_u"], i * 8 + (4 * k + 4))
                        act_.activation(sg[:, k], bank[2 + k][:, 0:256], ACT.Silu).then_inc(S["sg_made"], 1)
                        tokens(1 - k, i * 2 + (k + 2))
                        act_.wait_ge(S[f"rows_stored{k}"], i * 16 + 16)
                        for c in range(2):
                            act_.wait_ge(S["moe_y"], i * 8 + (4 * k + 2 * c + 2))
                            act_.activation(ysb[0:CAP, k, 512 * c:512 * c + 512], bank[4 + 2 * k + c][0:CAP, :],
                                            ACT.Copy).then_inc(S["moe_added"], 1)
                        act_.wait_ge(S["moe_added"], i * 4 + (4 + 2 * k + 2))
                        dst = moe_rows.rearrange("(e b c) d -> e b c d", b=2, c=CAP)[bass.ds(i, 1), k]
                        act_.dma_start(dst.rearrange("e c d -> (e c) d"), ysb[0:CAP, k]).then_inc(S[f"rows_stored{k}"], 16)
            with act_.Else():
                with act_.Fori(0, 16) as e:
                    for k in range(2):
                        for f in range(4):
                            act_.wait_ge(S["moe_g"], e * 8 + (4 * k + f + 1))
                            act_.wait_ge(S["hdn_made"], e * 8 + (4 * k + f + 1))
                            act_.activation(sg[:, f % 2], bank[f % 2][:, 0:T], ACT.Silu).then_inc(S["sg_made"], 1)
            act_.wait_ge(S["x_moe"], 1)
            norm("nf2", x, h)

        @block.vector
        def _(v):
            link = Chain(v, S["dve_chain"])

            def bc(ap, axis, n):
                ap = ap.unsqueeze(axis)
                shape = list(ap.shape)
                shape[axis] = n
                return ap.to_broadcast(shape)

            def norm(tag, src, dst, scale, shift=None):
                v.wait_ge(S["norm_sum"], normed(tag, NT))
                v.tensor_scalar(stat[:, 2:4], stat[:, 0:2], 1.0 / D, EPS, ALU.mult, ALU.add).then_inc(S["norm_mean"], 1)
                v.wait_ge(S["norm_root"], NORMS.index(tag) + 1)
                link(v.reciprocal(stat[:, 6:8], stat[:, 4:6]))
                for t in range(NT):
                    ins = v.scalar_tensor_tensor(out=dst[:, t], in0=src[:, t], scalar=stat[:, 6 + t:7 + t], in1=scale,
                                                 op0=ALU.mult, op1=ALU.mult)
                    if shift is not None:
                        link(ins)
                        ins = v.tensor_tensor(dst[:, t], dst[:, t], shift, ALU.add)
                    ins.then_inc(S["normed"], 1)

            def modulation(l):
                v.wait_ge(S["in_modb"], 16 * (l + 1))
                for c in range(12):
                    v.wait_ge(S["mod"], 12 * l + c + 1)
                    part = flat(mod)[:, 512 * c:512 * c + 512]
                    v.tensor_tensor(part, part, bank[c % 4][:, :], ALU.add).then_inc(S["mod_ev"], 1)
                    if l == 0 and c < 4:
                        if c == 0:
                            v.wait_ge(S["in_modcb"], 16)
                        v.wait_ge(S["modc"], c + 1)
                        part = flat(modc)[:, 512 * c:512 * c + 512]
                        v.tensor_tensor(part, part, bank[4 + c][:, :], ALU.add).then_inc(S["modc_ev"], 1)
                v.wait_ge(S["mod_ev"], 12 * l + 12)

            def gain_into(scale, name):
                g = wait_gain(v, name)
                return v.scalar_tensor_tensor(out=scale, in0=scale, scalar=1.0, in1=g, op0=ALU.add, op1=ALU.mult)

            def top16(values, indices, scores, n):
                for r in range(n):
                    ins = v.max(values(r)[:, 0:8], scores(r))
                link(ins)
                for r in range(n):
                    ins = v.max_index(indices(r)[:, 0:8], values(r)[:, 0:8], scores(r))
                link(ins)
                for r in range(n):
                    ins = v.match_replace(scores(r), values(r)[:, 0:8], scores(r), NEG)
                link(ins)
                for r in range(n):
                    ins = v.max(values(r)[:, 8:16], scores(r))
                link(ins)
                for r in range(n):
                    ins = v.max_index(indices(r)[:, 8:16], values(r)[:, 8:16], scores(r))
                link(ins)

            def add_product(dst, products, gain, tag, done):
                for k in range(4):
                    c, t = k // 2, k % 2
                    v.wait_ge(S[tag], k + 1)
                    part = dst[:, t, 512 * c:512 * c + 512]
                    if gain is None:
                        ins = v.tensor_tensor(part, part, products[k][:, :], ALU.add)
                    else:
                        link(v.tensor_tensor(gt[:, k % 2], products[k][:, :], gain[:, 512 * c:512 * c + 512], ALU.mult))
                        ins = v.tensor_tensor(part, part, gt[:, k % 2], ALU.add)
                    if c == 1:
                        ins.then_inc(S[done], 1)
                    else:
                        link(ins)

            v.wait_ge(S["silu_c"], 1)
            v.tensor_copy(cB, bc(cols[:, 0:8], 2, P)).then_inc(S["cB"], 1)
            v.tensor_copy(cB2, bc(cols[:, 8:16], 2, P)).then_inc(S["cB"], 1)
            v.memset(stat[:, 16:17], 0.0).then_inc(S["up_used"], 4)
            modulation(0)
            v.wait_ge(S["modc_ev"], 4)
            link(gain_into(modc[:, 1], "norm1_0"))
            link(gain_into(mod[:, 1], "norm1_0"))
            ins = gain_into(mod[:, 4], "norm2_0")
            ins.then_inc(S["gain_used"], 2)
            v.wait_ge(S["gain_used"], 2)
            norm("nctx", ctxn, h, modc[:, 1], modc[:, 0])
            v.wait_ge(S["in_x"], 16)
            v.wait_ge(S["norm_sum"], normed("n1_0", NT))
            norm("n1_0", x, h, mod[:, 1], mod[:, 0])

            v.wait_ge(S["pin1_ev"], 8)
            v.wait_ge(S["in_const"], 16)
            rope = cst("rope").rearrange("p (t f) -> p t f", t=NT)
            for t in range(NT):
                for n, src, dst in (
                        (4, proj[:, t, 0:512].rearrange("p (j a f) -> p j a f", j=2, a=4),
                         qk[:, t, 0:512].rearrange("p (a j f) -> p j a f", a=4, j=2)),
                        (1, proj[:, t, 512:640].rearrange("p (j a f) -> p j a f", j=2, a=1),
                         qk[:, t, 512:640].rearrange("p (a j f) -> p j a f", a=1, j=2))):
                    tmp = tmp1[:, 0:64 * n].rearrange("p (j a f) -> p j a f", j=2, a=n)
                    for axis in range(2):
                        x1, x2 = (src[:, :, :, 32 * axis + 16 * i:32 * axis + 16 * i + 16] for i in range(2))
                        o1, o2 = (dst[:, :, :, 32 * axis + 16 * i:32 * axis + 16 * i + 16] for i in range(2))
                        u1, u2 = tmp[:, :, :, 0:16], tmp[:, :, :, 16:32]
                        cos = bc(bc(rope[:, t, 16 * axis:16 * axis + 16], 1, n), 1, 2)
                        sin = bc(bc(rope[:, t, 32 + 16 * axis:48 + 16 * axis], 1, n), 1, 2)
                        v.tensor_tensor(u1, x2, sin, ALU.mult)
                        v.tensor_tensor(u2, x2, cos, ALU.mult)
                        v.tensor_tensor(o1, x1, cos, ALU.mult)
                        link(v.tensor_tensor(o2, x1, sin, ALU.mult))
                        v.tensor_tensor(o1, o1, u1, ALU.subtract)
                        link(v.tensor_tensor(o2, o2, u2, ALU.add))
            v.tensor_copy(stat[:, 8:9], stat[:, 6:7]).then_inc(S["rope1"], 1)

            v.wait_ge(S["gelu1"], NT)
            va = proj[:, :, 1280:1792].rearrange("p t (g d) -> p t g d", g=8)
            mu = gst[:, 0].rearrange("p (t g) -> p t g", t=NT)
            var = gst[:, 1].rearrange("p (t g) -> p t g", t=NT)
            sq = mixcat[:, 0, 0:512].rearrange("p (g d) -> p g d", g=8)
            for t in range(NT):
                link(v.tensor_reduce(mu[:, t], va[:, t], AX, ALU.add))
            link(v.tensor_scalar(gst[:, 0], gst[:, 0], 1.0 / 64, None, ALU.mult))
            for t in range(NT):
                link(v.tensor_tensor(va[:, t], va[:, t], bc(mu[:, t], 2, 64), ALU.subtract))
                link(v.tensor_tensor(sq, va[:, t], va[:, t], ALU.mult))
                link(v.tensor_reduce(var[:, t], sq, AX, ALU.add))
            v.tensor_scalar(gst[:, 1], gst[:, 1], 1.0 / 64, EPS, ALU.mult, ALU.add).then_inc(S["gmlp_v"], 1)
            v.wait_ge(S["g_rt"], 1)
            link(v.reciprocal(gst[:, 3], gst[:, 2]))
            for t in range(NT):
                v.tensor_tensor(va[:, t], va[:, t], bc(gst[:, 3, 8 * t:8 * t + 8], 2, 64), ALU.mult).then_inc(S["gmlp_v"], 1)
            bs = col("bs")
            for t in range(NT):
                v.wait_ge(S["gmlp"], t + 1)
                mg = mixcat[:, t, 512:1024].rearrange("p (g d) -> p g d", g=8)
                link(v.tensor_tensor(mg, bank[4 + t][:, :].rearrange("p (g d) -> p g d", g=8), bc(bs, 2, 64), ALU.add))
                v.tensor_tensor(mixcat[:, t, 512:1024], mixcat[:, t, 512:1024], proj[:, t, 768:1280], ALU.mult).then_inc(
                    S["mixed"], 1)

            v.wait_ge(S["in_rows"], 16)
            win = cst("win").rearrange("p (t k) -> p t k", t=NT)
            for it in range(4):
                t, j = it // 2, it % 2
                sink = rw("sink")[:, 4 * j:4 * j + 4]
                if it:
                    v.wait_ge(S["a_pt"], 4 * it)
                for p in range(4):
                    v.wait_ge(S["a_s"], 4 * it + p + 1)
                    v.scalar_tensor_tensor(out=sc1[:, p, 0:256], in0=bank[p][:, 0:256], scalar=0.125, in1=win[:, t],
                                           op0=ALU.mult, op1=ALU.add)
                    v.tensor_scalar(sc1[:, p, 256:512], bank[p][:, 256:512], 0.125, None, ALU.mult).then_inc(S["a_s_ev"], 1)
                v.wait_ge(S["a_s_ev"], 4 * it + 4)
                link(v.tensor_reduce(ast[:, 0], sc1, AX, ALU.max))
                link(v.tensor_tensor(ast[:, 0], ast[:, 0], sink, ALU.max))
                v.tensor_tensor(ast[:, 3], sink, ast[:, 0], ALU.subtract)
                v.tensor_scalar(ast[:, 2], ast[:, 0], -1.0, None, ALU.mult).then_inc(S["a_negm"], 1)
                v.wait_ge(S["a_exp"], 5 * it + 5)
                link(v.tensor_tensor(ast[:, 4], ast[:, 4], ast[:, 3], ALU.add))
                link(v.reciprocal(ast[:, 5], ast[:, 4]))
                v.wait_ge(S["a_pv"], 4 * it + 4)
                v.tensor_tensor(mixcat[:, t, 256 * j:256 * j + 256].rearrange("p (g d) -> p g d", g=4),
                                bank[6 + it % 2][:, 0:256].rearrange("p (g d) -> p g d", g=4),
                                bc(ast[:, 5], 2, 64), ALU.mult).then_inc(S["attn_o"], 1)
            v.wait_ge(S["attn_o"], 4)

            add_product(x, [bank[4 + k] for k in range(4)], mod[:, 2], "pout1", "x_mix")

            def peer(l):
                v.wait_ge(S["x_mix"], NT * (l + 1))
                norm(f"n2_{l}", x, h, mod[:, 4], mod[:, 3])
                v.wait_ge(S["ps_ev"], 8 * l + 8)
                for t in range(NT):
                    top16(lambda r: v16[:, r // 2, r % 2], lambda r: i16[:, r], lambda r: s16[:, t, r], 16)
                    for hh in range(8):
                        ins = v.tensor_tensor(cand[:, hh].rearrange("p (a b) -> p a b", a=16),
                                              bc(v16[:, hh, 0], 2, 16), bc(v16[:, hh, 1], 1, 16), ALU.add)
                    link(ins)
                    top16(lambda r: bv[:, r], lambda r: bp[:, r], lambda r: cand[:, r], 8)
                    if t:
                        v.wait_ge(S["gate_exp"], NT * l + t)
                    v.tensor_tensor(gate[:, t].rearrange("p (g k) -> p g k", g=8), bv, bc(bv[:, :, 0], 2, 16),
                                    ALU.subtract).then_inc(S["gate_in"], 1)
                    v.tensor_single_scalar(ab[:, 0], flat(bp), 4, ALU.logical_shift_right)
                    link(v.tensor_single_scalar(ab[:, 1], flat(bp), 15, ALU.bitwise_and))
                    v.tensor_copy(abf, ab)
                    link(v.tensor_copy(i16f.rearrange("p a b c -> p (a b c)"), flat(i16)))
                    oh = onehot[t]
                    for s in range(2):
                        link(v.tensor_tensor(oh, bc(cst("iota")[:, 0:16], 1, PICKS), bc(abf[:, s], 2, 16), ALU.is_equal))
                        link(v.tensor_tensor(oh.rearrange("p (g k) c -> p g k c", g=8),
                                             oh.rearrange("p (g k) c -> p g k c", g=8),
                                             bc(i16f[:, :, s], 2, 16), ALU.mult))
                        link(v.tensor_reduce(sel[:, s], oh, AX, ALU.add))
                    link(v.scalar_tensor_tensor(out=sel[:, 0], in0=sel[:, 0], scalar=128.0, in1=sel[:, 1],
                                                op0=ALU.mult, op1=ALU.add))
                    v.tensor_scalar(idx_all[:, t], sel[:, 0], float(l * EXPERTS), None, ALU.add).then_inc(S["idx_ready"], 1)
                    v.wait_ge(S["gate_exp"], NT * l + t + 1)
                    g3 = gate[:, t].rearrange("p (g k) -> p g k", g=8)
                    link(v.tensor_reduce(gsum[:, 0], g3, AX, ALU.add))
                    link(v.reciprocal(gsum[:, 1], gsum[:, 0]))
                    link(v.tensor_tensor(g3, g3, bc(gsum[:, 1], 2, 16), ALU.mult))
                for t in range(NT):
                    n = 2 * l + t
                    with v.Fori(0, PICKS // GSLOTS) as i:
                        for s in range(GSLOTS):
                            v.wait_ge(S[f"gathered{s}"], i * 16 + 16 * (16 * (4 * l + t) + 1))
                            v.scalar_tensor_tensor(out=G[:, s], in0=G[:, s], scalar=1.0, in1=h[:, t], op0=ALU.mult,
                                                   op1=ALU.mult, accum_out=act[:, t, bass.ds(i * GSLOTS + s, 1)]).then_inc(
                                S["down_used"], 1)
                for t in range(NT):
                    v.wait_ge(S["peer_gelu"], NT * l + t + 1)
                    v.tensor_tensor(act[:, t], act[:, t], gate[:, t], ALU.mult).then_inc(S["peer_w"], 1)
                for t in range(NT):
                    v.wait_ge(S["up_used"], 4 + PICKS * (NT * l + t + 1))
                    if t:
                        v.wait_ge(S["x_peer"], NT * l + t)
                    for c in range(2):
                        link(v.tensor_tensor(gt[:, c], bank[2 * t + c][:, :], mod[:, 5, 512 * c:512 * c + 512], ALU.mult))
                    v.tensor_tensor(x[:, t], x[:, t], gt.rearrange("p a b -> p (a b)"), ALU.add).then_inc(S["x_peer"], 1)
                v.wait_ge(S["x_peer"], NT * (l + 1))

            peer(0)
            v.tensor_copy(cB, bc(cols[:, 0:8], 2, P)).then_inc(S["cB"], 1)
            modulation(1)
            link(gain_into(mod[:, 1], "norm1_1"))
            v.tensor_copy(stat[:, 8:9], stat[:, 6:7]).then_inc(S["gain_used"], 1)
            norm("n1_1", x, h, mod[:, 1], mod[:, 0])
            g = wait_gain(v, "pool")
            v.tensor_tensor(mod[:, 2], mod[:, 2], g, ALU.mult).then_inc(S["gain_used"], 1)
            v.wait_ge(S["gain_used"], 4)
            gain_into(mod[:, 4], "norm2_1").then_inc(S["gain_used"], 1)
            v.wait_ge(S["gain_used"], 5)
            add_product(x, [bank[k] for k in range(4)], mod[:, 2], "py_pool", "x_mix")
            peer(1)
            g = wait_gain(v, "final_1")
            norm("nf1", x, x, g)
            v.wait_ge(S["normed"], normed("nf1", NT))
            v.tensor_copy(stat[:, 8:10], stat[:, 6:8]).then_inc(S["x_block1"], NT)
            v.tensor_copy(stat[:, 10:11], stat[:, 6:7]).then_inc(S["gain_used"], 1)
            g = wait_gain(v, "mix")
            norm("nmix", x, h, g)
            v.wait_ge(S["normed"], normed("nmix", NT))
            v.tensor_copy(stat[:, 8:9], stat[:, 6:7]).then_inc(S["gain_used"], 1)

            posf = stat[:, 12:15]
            v.wait_ge(S["in_pos"], 16)
            link(v.tensor_copy(posf, posi[:, :]))
            ang = tang[:, 0:3]
            for i in range(3):
                link(v.tensor_scalar(ang[:, i], cst("inv"), posf[:, i:i + 1], None, ALU.mult))
            turns = tang[:, 3:6]
            link(v.tensor_scalar(turns, ang, float(np.float32(1 / (2 * np.pi))), 12582912.0, ALU.mult, ALU.add))
            link(v.tensor_scalar(turns, turns, -12582912.0, None, ALU.add))
            parts, rest = [], 2 * np.pi
            for bits in (7, 10):
                e = 2.0 ** (bits - 3)
                parts.append(np.floor(rest * e) / e if not parts else np.floor(rest * 2.0 ** 17) / 2.0 ** 17)
                rest -= parts[-1]
            parts.append(rest)
            for part in parts:
                link(v.scalar_tensor_tensor(out=ang, in0=turns, scalar=-float(part), in1=ang, op0=ALU.mult, op1=ALU.add))
            PI = 3.1415925
            link(v.tensor_scalar(ang, ang, PI, -PI, ALU.min, ALU.max))
            link(v.scalar_tensor_tensor(out=turns, in0=ang, scalar=-1.0, in1=ang, op0=ALU.mult, op1=ALU.max))
            v.tensor_scalar(turns, turns, -1.0, float(np.pi / 2), ALU.mult, ALU.add).then_inc(S["angles"], 1)

            def rope2(dst, src, tmp, n, row):
                np_ = src.shape[0]
                j = 2 if src.shape[1] > 64 else 1
                src = src.rearrange("p (j a f) -> p j a f", j=j, a=n)
                dst = dst.rearrange("p (a j f) -> p j a f", j=j, a=n)
                u = tmp.rearrange("p (j a f) -> p j a f", j=j, a=n)
                cos, sin = (bc(bc(trig[0:np_, row, i, :], 1, n), 1, j) for i in range(2))
                link(v.tensor_tensor(u, src[:, :, :, 32:64], sin, ALU.mult))
                link(v.tensor_tensor(dst[:, :, :, 0:32], src[:, :, :, 0:32], cos, ALU.mult))
                link(v.tensor_tensor(dst[:, :, :, 0:32], dst[:, :, :, 0:32], u, ALU.subtract))
                link(v.tensor_tensor(u, src[:, :, :, 32:64], cos, ALU.mult))
                link(v.tensor_tensor(dst[:, :, :, 32:64], src[:, :, :, 0:32], sin, ALU.mult))
                return v.tensor_tensor(dst[:, :, :, 32:64], dst[:, :, :, 32:64], u, ALU.add)

            v.wait_ge(S["pin2_ev"], 20)
            for t in range(NT):
                v.tensor_copy(kcd[:, t].rearrange("p a (b d) -> p a b d", b=2),
                              bc(z[:, t, Z_KC:Z_KS].rearrange("p (a d) -> p a d", a=4), 2, 2)).then_inc(S["kcd"], 1)
            v.wait_ge(S["trig"], 2)
            link(v.memset(X, 0.0))
            v.wait_ge(S["operands_ev"], operand("tkc", 2))
            X5 = X.rearrange("p v k (g n) -> p v k g n", g=2)
            for kv in range(2):
                pos = col("posk" if kv == 0 else "posv")
                for g in range(2):
                    raw = kdT[:, 2 * kv + g].rearrange("p (n m b) -> p m n b", m=8, b=2)
                    for b in range(2):
                        q = slice(64 * b, 64 * b + 64)
                        for half in range(2):
                            ins = v.tensor_tensor(X5[q, kv, 8 * half:8 * half + 8, g, 0:15], raw[q, :, half:half + 15, b],
                                                  bc(pos[q, 8 * half:8 * half + 8], 2, 15), ALU.add)
                            ins.then_inc(S["windows"], 1)
            for t in range(NT):
                link(rope2(qr[:, t, 0:512], z[:, t, Z_Q:Z_Q + 512], rtmp[:, 0:256], 4, t))
                link(rope2(qr[:, t, 512:640], z[:, t, Z_KS:Z_KS + 128], rtmp[:, 256:320], 1, t))
                rope2(qr[:, t, 640:768], z[:, t, Z_KW:Z_KW + 128], rtmp[:, 320:384], 1, t).then_inc(S["rope2"], 1)
            v.wait_ge(S["hid"], 2)
            b1 = rows[0:64, ROW_AT["b1k"][0]:ROW_AT["b1k"][0] + 512]
            v.tensor_tensor(flat(H1)[0:64], bank[3][0:64, :], b1, ALU.add).then_inc(S["cmp_v"], 1)
            v.wait_ge(S["cmp"], 2)
            b2k = rows[0:64, ROW_AT["b2k"][0]:ROW_AT["b2k"][0] + 64]
            b2v = rows[0:64, ROW_AT["b2v"][0]:ROW_AT["b2v"][0] + 64]
            link(v.tensor_tensor(ctmp[0:64, 0:64], bank[0][0:64, 0:64], b2k, ALU.add))
            link(rope2(kc2[0:64, 0:64], ctmp[0:64, 0:64], ctmp[0:64, 64:96], 1, 2))
            v.tensor_copy(kc2[0:64, 64:128], kc2[0:64, 0:64]).then_inc(S["cmp_v"], 1)
            v.memset(kcT, 0.0).then_inc(S["cmp_v"], 1)
            link(v.memset(vcz, 0.0))
            for g in range(2):
                q = slice(32 * g, 32 * g + 32)
                v.tensor_tensor(vcz[q, g], bank[1][q, 0:64], rows[q, ROW_AT["b2v"][0]:ROW_AT["b2v"][0] + 64],
                                ALU.add).then_inc(S["cmp_v"], 1)
            cmpmask = cst("cmpmask").rearrange("p (t n) -> p t n", t=NT)
            cmpok = cst("cmpok").rearrange("p (t n) -> p t n", t=NT)
            causal = cst("causal").rearrange("p (t n) -> p t n", t=NT)
            v.wait_ge(S["z_acts"], 1)
            v.wait_ge(S["operands_ev"], operand("tq2", 4))
            for t in range(NT):
                v.wait_ge(S["c_s"], t + 1)
                if t:
                    v.wait_ge(S["c_pt"], t)
                pc4 = pcm.rearrange("p a (j n) -> p a j n", j=2)
                for p in range(4):
                    ins = v.scalar_tensor_tensor(
                        out=pc4[:, p], in0=bank[5][:, 64 * p:64 * p + 64].rearrange("p (j n) -> p j n", j=2),
                        scalar=0.125, in1=bc(cmpmask[:, t], 1, 2), op0=ALU.mult, op1=ALU.add)
                link(ins)
                cm = cst2[:, 0]
                c8 = cst2.rearrange("p a b -> p (a b)")
                link(v.tensor_reduce(c8[:, 0:8], flat(pcm).rearrange("p (a n) -> p a n", a=8), AX, ALU.max))
                p8 = flat(pcm).rearrange("p (a n) -> p a n", a=8)
                v.tensor_tensor(p8, p8, bc(c8[:, 0:8], 2, 32), ALU.subtract).then_inc(S["c_sub"], 1)
                v.wait_ge(S["c_exp"], t + 1)
                link(v.tensor_reduce(c8[:, 8:16], p8, AX, ALU.add))
                link(v.reciprocal(c8[:, 16:24], c8[:, 8:16]))
                gs3 = gsig[:, t].rearrange("p (j a b) -> p a j b", j=2, a=4)
                link(v.tensor_tensor(c8[:, 16:24].rearrange("p (a j) -> p a j", a=4),
                                     c8[:, 16:24].rearrange("p (a j) -> p a j", a=4), gs3[:, :, :, 0], ALU.mult))
                link(v.tensor_tensor(p8, p8, bc(c8[:, 16:24], 2, 32), ALU.mult))
                v.tensor_tensor(p8, p8, bc(cmpok[:, t], 1, 8), ALU.mult).then_inc(S["c_p"], 1)
                for j in range(2):
                    it = 2 * t + j
                    if it:
                        v.wait_ge(S["b_pt"], 4 * it)
                    for p in range(4):
                        v.wait_ge(S["b_s"], 4 * it + p + 1)
                        v.scalar_tensor_tensor(out=psc[:, 2 * p:2 * p + 2], in0=bank[p][:, :].rearrange("p (a k) -> p a k", a=2),
                                               scalar=0.125, in1=bc(causal[:, t], 1, 2), op0=ALU.mult,
                                               op1=ALU.add).then_inc(S["b_s_ev"], 1)
                    v.wait_ge(S["b_s_ev"], 4 * it + 4)
                    link(v.tensor_reduce(nst[:, 0], psc, AX, ALU.max))
                    v.tensor_scalar(nst[:, 1], nst[:, 0], -1.0, None, ALU.mult).then_inc(S["b_negm"], 1)
                    v.wait_ge(S["b_exp"], 8 * it + 8)
                    link(v.reciprocal(nst[:, 3], nst[:, 2]))
                    gs = gsig[:, t, 12 * j:12 * j + 12].rearrange("p (a b) -> p a b", a=4)[:, :, 1:3]
                    n3 = nst[:, 3].rearrange("p (a b) -> p a b", a=4)
                    link(v.tensor_tensor(n3, n3, gs, ALU.mult))
                    v.tensor_tensor(psc, psc, bc(nst[:, 3], 2, T), ALU.mult).then_inc(S["b_p"], 1)
            v.wait_ge(S["z_acts"], 1 + NT)
            for c in range(2):
                for t in range(NT):
                    v.wait_ge(S["branch"], 2 * c + t + 1)
                    v.tensor_tensor(zx[:, t, 512 * c:512 * c + 512], bank[4 + 2 * c + t][:, :],
                                    z[:, t, Z_MA + 512 * c:Z_MA + 512 * c + 512], ALU.mult).then_inc(S["ya"], 1)

            v.wait_ge(S["operands_ev"], operand("tgla", 3))
            v.wait_ge(S["gla_x"], 1)
            ba = col("b_a")
            for q in range(2):
                link(v.tensor_scalar(gt1[:, q], bank[3][:, 256 * q:256 * q + 256], ba[:, q:q + 1], None, ALU.add))
            v.scalar_tensor_tensor(out=gt2, in0=gt1, scalar=-1.0, in1=gt1, op0=ALU.mult, op1=ALU.max).then_inc(S["gla_v"], 1)
            v.wait_ge(S["gla_a"], 2)
            link(v.scalar_tensor_tensor(out=gt1, in0=gt1, scalar=0.0, in1=gt2, op0=ALU.min, op1=ALU.subtract))
            link(v.tensor_scalar(gt1, gt1, 1.0 / 16, None, ALU.mult))
            for q in range(2):
                ins = v.tensor_tensor_scan(bb[:, q], cst("reset"), gt1[:, q], 0.0, ALU.mult, ALU.add)
            ins.then_inc(S["gla_v"], 1)
            v.wait_ge(S["gla_v"], 2)
            b4 = bb.rearrange("p a (c s) -> p a c s", s=64)
            last = b4[:, :, :, 63]
            for q in range(2):
                ins = v.tensor_tensor(gt2[:, q].rearrange("p (c s) -> p c s", s=64), bc(last[:, q], 2, 64), b4[:, q], ALU.subtract)
            ins.then_inc(S["gla_v"], 1)
            link(v.tensor_scalar(gqT, gqT, 0.125, None, ALU.mult))
            v.memset(QM, 0.0)
            v.memset(st, 0.0)
            link(v.memset(QZ, 0.0))
            QM6 = QM.rearrange("p q t (u c g) -> p q t u c g", c=2, g=2)
            for q in range(2):
                for t in range(NT):
                    for g in range(2):
                        pp = slice(64 * g, 64 * g + 64)
                        v.tensor_copy(QM6[pp, q, t, :, :, g],
                                      gqT[pp, q, P * t:P * t + P].rearrange("p (c u) -> p u c", c=2)).then_inc(S["qm"], 1)
            v.wait_ge(S["gla_a"], 4)
            for q in range(2):
                for c in range(4):
                    o = 64 * (c % 2)
                    v.tensor_tensor(QZ[:, q, c, o:o + 64], gqT[:, q, 64 * c:64 * c + 64], gt1[:, q, 64 * c:64 * c + 64],
                                    ALU.mult).then_inc(S["qz"], 1)
            v.wait_ge(S["gla_a"], 5)
            v.tensor_tensor(gt2, gt2, gkT, ALU.mult).then_inc(S["gla_v"], 1)

            def ek_mult(k):
                q, t = k // 8, (k // 4) % 2
                e4 = Ek[k % 2].rearrange("p (u c s) -> p u c s", u=16, c=2)
                v.wait_ge(S["ek_exp"], k + 1)
                v.tensor_tensor(e4, e4, bc(gkT[:, q, P * t:P * t + P].rearrange("p (c s) -> p c s", c=2), 1, 16),
                                ALU.mult).then_inc(S["ek_ready"], 1)

            for k in range(16):
                q, t, u = k // 8, (k // 4) % 2, k % 4
                e4 = Ek[k % 2].rearrange("p (u c s) -> p u c s", u=16, c=2)
                bt = bb[:, q, P * t:P * t + P].rearrange("p (c u) -> p u c", c=2)[:, 16 * u:16 * u + 16]
                bs_ = bb[:, q, P * t:P * t + P].rearrange("p (c s) -> p c s", c=2)
                if k >= 2:
                    v.wait_ge(S["attn_gla"], k - 1)
                link(v.tensor_tensor(e4, bc(bt, 3, 64), bc(bs_, 1, 16), ALU.subtract))
                v.tensor_scalar(Ek[k % 2], Ek[k % 2], 0.0, None, ALU.min).then_inc(S["ek_sub"], 1)
                if k:
                    ek_mult(k - 1)
            ek_mult(15)
            for c in range(1, 4):
                for q in range(2):
                    v.wait_ge(S["state"], 2 * (c - 1) + q + 1)
                    for g in range(2):
                        pp = slice(64 * g, 64 * g + 64)
                        ee = slice(P * g, P * g + P)
                        upd = bank[4 + q][pp, ee]
                        if c == 1:
                            v.tensor_copy(st[pp, c, q, ee], upd).then_inc(S["st"], 1)
                        else:
                            v.scalar_tensor_tensor(out=st[pp, c, q, ee], in0=st[pp, c - 1, q, ee],
                                                   scalar=gel[pp, 4 * q + c - 1:4 * q + c], in1=upd,
                                                   op0=ALU.mult, op1=ALU.add).then_inc(S["st"], 1)
                v.wait_ge(S["st"], 4 * c)
            glamask = cst("glamask").rearrange("p (c u) -> p c u", c=2)
            for t in range(NT):
                if t:
                    v.wait_ge(S["gla_o"], 1)
                for hd in range(4):
                    q, g = hd // 2, hd % 2
                    A = bank[6 + q][:, 256 * t:256 * t + 256].rearrange("p (u c g) -> p c u g", c=2, g=2)[:, :, :, g]
                    v.wait_ge(S["attn_gla"], 8 * q + 4 * t + 4)
                    v.tensor_tensor(AT[:, hd].rearrange("p (c u) -> p c u", c=2), A, glamask, ALU.mult).then_inc(S["AT"], 1)
            for t in range(NT):
                v.wait_ge(S["gla_o"], t + 1)
                v.tensor_copy(zcat[:, t], bank[t][:, :]).then_inc(S["go"], 1)
            v.wait_ge(S["go"], NT)
            go8 = zcat.rearrange("p t (g e) -> p (t g) e", g=4)
            sq = Ek[0].rearrange("p (a b) -> p a b", a=16)[:, 0:8]
            link(v.tensor_tensor(sq, go8, go8, ALU.mult))
            link(v.tensor_reduce(gso, sq, AX, ALU.add))
            v.tensor_scalar(gso, gso, 1.0 / 128, EPS, ALU.mult, ALU.add).then_inc(S["go_v"], 1)
            v.wait_ge(S["go_rt"], 1)
            link(v.reciprocal(gso, gso))
            link(v.tensor_tensor(go8, go8, bc(gso, 2, P), ALU.mult))
            link(v.tensor_tensor(zcat, zcat, bc(rw("glag"), 1, NT), ALU.mult))
            v.wait_ge(S["z_acts"], 4)
            v.tensor_tensor(zcat, zcat, z[:, :, Z_GR:Z_MA], ALU.mult).then_inc(S["go_v"], 1)
            for c in range(2):
                for t in range(NT):
                    v.wait_ge(S["branch"], 4 + 2 * c + t + 1)
                    mb = z[:, t, Z_MB + 512 * c:Z_MB + 512 * c + 512]
                    link(v.tensor_tensor(mb, bank[4 + 2 * c + t][:, :], mb, ALU.mult))
                    v.tensor_tensor(zy[:, t, 512 * c:512 * c + 512], zx[:, t, 512 * c:512 * c + 512], mb,
                                    ALU.add).then_inc(S["zy"], 1)
            add_product(x, [bank[4 + k] for k in range(4)], None, "pout2", "x_mix")
            v.wait_ge(S["x_mix"], NT * 3)
            def dense_moe():
                v.tensor_copy(stat[:, 8:9], stat[:, 6:7]).then_inc(S["hdn_made"], 2)
                with v.Fori(0, 16) as e:
                    for k in range(2):
                        for f in range(4):
                            v.wait_ge(S["sg_made"], e * 8 + (4 * k + f + 1))
                            v.wait_ge(S["moe_u"], e * 8 + (4 * k + f + 1))
                            v.tensor_tensor(hdn[:, f], sg[:, f % 2], bank[2 + f % 2][:, 0:T], ALU.mult).then_inc(S["hdn_made"], 1)
                        for i in range(4):
                            t, c = i // 2, i % 2
                            v.wait_ge(S["moe_y"], e * 8 + (4 * k + i + 1))
                            part = x[:, t, 512 * c:512 * c + 512]
                            v.scalar_tensor_tensor(out=part, in0=bank[4 + i][:, :], scalar=cmb[:, t].rearrange("p (a b) -> p b a", b=2)[:, k, bass.ds(e, 1)], in1=part,
                                                   op0=ALU.mult, op1=ALU.add).then_inc(S["moe_added"], 1)
                v.wait_ge(S["moe_added"], 4 + 128)

            g = wait_gain(v, "ffn")
            norm("nffn", x, h, g)
            v.wait_ge(S["normed"], normed("nffn", NT))
            v.tensor_copy(stat[:, 8:9], stat[:, 6:7]).then_inc(S["gain_used"], 1)
            v.wait_ge(S["router"], NT)
            for t in range(NT):
                m = lambda r, n: mst[:, r, 0:n]
                link(v.tensor_tensor(m(0, 36), bank[4 + t][:, 0:36], rw("brt"), ALU.add))
                link(v.memset(m(2, 8), NEG))
                link(v.tensor_copy(m(2, 4), m(0, 4)))
                link(v.max(m(3, 8), m(2, 8)))
                link(v.max_index(m(4, 8).bitcast(U32), m(3, 8), m(2, 8)))
                link(v.tensor_copy(m(9, 8), m(4, 8).bitcast(U32)))
                link(v.tensor_scalar(m(10, 4), cst("iota")[:, 0:4], m(9, 1), None, ALU.is_equal))
                link(v.tensor_scalar(m(11, 8), mst[:, 0, 4:12], m(10, 1), None, ALU.mult))
                for g in range(1, 4):
                    link(v.scalar_tensor_tensor(out=m(11, 8), in0=mst[:, 0, 4 + 8 * g:12 + 8 * g], scalar=mst[:, 10, g:g + 1],
                                                in1=m(11, 8), op0=ALU.mult, op1=ALU.add))
                link(v.max(m(12, 8), m(11, 8)))
                link(v.max_index(m(13, 8).bitcast(U32), m(12, 8), m(11, 8)))
                link(v.tensor_copy(m(14, 8), m(13, 8).bitcast(U32)))
                if t:
                    v.wait_ge(S["r_exp"], t)
                v.tensor_scalar(m(5, 4), m(0, 4), m(3, 1), None, ALU.subtract)
                v.tensor_tensor(mst[:, 5, 4:5], mst[:, 12, 1:2], mst[:, 12, 0:1], ALU.subtract).then_inc(S["r_sub"], 1)
                v.wait_ge(S["r_exp"], t + 1)
                link(v.tensor_reduce(m(7, 1), m(6, 4), AX, ALU.add))
                link(v.scalar_tensor_tensor(out=m(8, 1), in0=mst[:, 6, 4:5], scalar=1.0, in1=m(7, 1), op0=ALU.add,
                                            op1=ALU.mult))
                link(v.reciprocal(m(15, 1), m(8, 1)))
                link(v.tensor_tensor(mst[:, 15, 1:2], m(15, 1), mst[:, 6, 4:5], ALU.mult))
                link(v.tensor_copy(wts[:, t], mst[:, 15, 0:2]))
                for n in range(2):
                    link(v.tensor_scalar(m(1, 8), cst("iota")[:, 0:8], mst[:, 14, n:n + 1], None, ALU.is_equal))
                    for g in range(4):
                        ins = v.tensor_scalar(pick[:, t, n, 8 * g:8 * g + 8], m(1, 8), mst[:, 10, g:g + 1], None, ALU.mult)
                    link(ins)
                v.tensor_tensor(chosen[:, t], pick[:, t, 0], pick[:, t, 1], ALU.add).then_inc(S["chosen"], 1)
                link(v.tensor_scalar(cmb[:, t], pick[:, t, 0], wts[:, t, 0:1], None, ALU.mult))
                link(v.scalar_tensor_tensor(out=cmb[:, t], in0=pick[:, t, 1], scalar=wts[:, t, 1:2], in1=cmb[:, t],
                                            op0=ALU.mult, op1=ALU.add))
            link(v.memset(place, 1000.0))
            v.wait_ge(S["placed"], 3)
            for t in range(NT):
                pl = place[:, t, 0:32]
                link(v.tensor_scalar(pl, bank[6 + t][:, 0:32], 1000.0, None, ALU.add))
                link(v.scalar_tensor_tensor(out=pl, in0=chosen[:, t], scalar=-1000.0, in1=pl, op0=ALU.mult, op1=ALU.add))
                row = ptmp[:, t, 0]
                link(v.scalar_tensor_tensor(out=row, in0=cst("iota")[:, 0:32], scalar=float(CAP), in1=pl, op0=ALU.mult,
                                            op1=ALU.add))
                for n in range(2):
                    link(v.tensor_tensor(ptmp[:, t, 1], row, pick[:, t, n], ALU.mult))
                    link(v.tensor_reduce(prow[:, 2 * t + n:2 * t + n + 1], ptmp[:, t, 1], AX, ALU.add))
            link(v.tensor_copy(pidx, prow))
            link(v.tensor_reduce(prow[:, 0:1], bank[3][:, 0:32], AX, ALU.max))
            v.tensor_scalar(crowd, prow[:, 0:1], float(CAP), None, ALU.is_gt).then_inc(S["crowd"], 1)
            v.wait_ge(S["crowd"], 1)

            def select(n, k, i):
                for t in range(NT):
                    ins = v.tensor_scalar(msel[:, k, t], cst("iota"),
                                          place[:, t].rearrange("p (a b) -> p b a", b=2)[:, k, bass.ds(n, 1)],
                                          None, ALU.is_equal)
                ins.then_inc(S["selected"], 1)

            v.tensor_copy(stat[:, 9:10], stat[:, 6:7]).then_inc(S["moe_added"], 4)
            crowded = v.value_load(crowd[0:1, 0:1], min_val=0, max_val=1)
            with v.If(crowded == 0):
                select(0, 0, 0)
                select(0, 1, 0)
                with v.Fori(0, 16) as i:
                    for k in range(2):
                        v.wait_ge(S["sg_made"], i * 2 + (k + 1))
                        v.tensor_tensor(hsel[:, k].rearrange("p f c -> p (f c)"), sg[:, k], bank[2 + k][:, 256:512],
                                        ALU.mult).then_inc(S["hdn_made"], 1)
                        select(i + 1, k, i)
                for n in range(4):
                    t = n // 2
                    v.wait_ge(S[f"gathered{n}"], 16 * (PICKS * 8 // GSLOTS + 1))
                    if n % 2:
                        v.wait_ge(S["brought"], n)
                    v.scalar_tensor_tensor(out=x[:, t], in0=yback[:, n], scalar=wts[:, t, n % 2:n % 2 + 1], in1=x[:, t],
                                           op0=ALU.mult, op1=ALU.add).then_inc(S["brought"], 1)
                v.wait_ge(S["brought"], 4)
            with v.Else():
                dense_moe()
            v.tensor_copy(stat[:, 8:9], stat[:, 6:7]).then_inc(S["x_moe"], 1)
            g = wait_gain(v, "final_2")
            norm("nf2", x, h, g)
            v.wait_ge(S["normed"], normed("nf2", NT))
            v.tensor_copy(stat[:, 8:9], stat[:, 6:7]).then_inc(S["out_ready"], NT)

        @block.tensor
        def _(pe):
            def bc(ap, axis, n):
                ap = ap.unsqueeze(axis)
                shape = list(ap.shape)
                shape[axis] = n
                return ap.to_broadcast(shape)

            def accumulate(dst, pairs):
                for i, (lhsT, rhs) in enumerate(pairs):
                    ins = pe.matmul(dst, lhsT, rhs, start=i == 0, stop=i == len(pairs) - 1)
                return ins

            def tile(ap, t):
                return ap[:, P * t:P * t + P]

            def transposes(tag, src, ready, per=1):
                for g in range(4):
                    t, half = g // 2, g % 2
                    if ready in NORMS:
                        pe.wait_ge(S["normed"], normed(ready, t + 1))
                    else:
                        pe.wait_ge(S[ready], per * (t + 1))
                    for q in range(4):
                        k = 4 * half + q
                        ins = pe.transpose(bank[g][:, P * q:P * q + P], src[:, t, P * k:P * k + P], ident)
                    ins.then_inc(S["turned"], 1)

            def project(tag, first, widths, ready):
                pe.wait_ge(S["turned_ev"], turned(ready, 4))
                for k in range(2 * len(widths)):
                    c, t = k // 2, k % 2
                    if k % 2 == 0:
                        wait_weight(pe, first + c)
                    if k >= 4:
                        pe.wait_ge(S[tag + "_ev"], k - 3)
                    w = slot(first + c)
                    accumulate(bank[4 + k % 4][:, 0:widths[c]], [(tile(hT[:, i], t), w[:, i]) for i in range(KT)]).then_inc(
                        S[tag], 1)

            def modulation(l):
                pe.wait_ge(S["cB"], 2 + l)
                for c in range(12):
                    wait_weight(pe, wat[f"mod{l}"] + c)
                    if c >= 4:
                        pe.wait_ge(S["mod_ev"], 12 * l + c - 3)
                    w = slot(wat[f"mod{l}"] + c)
                    accumulate(bank[c % 4][:, :], [(cB[:, i], w[:, i]) for i in range(KT)]).then_inc(S["mod"], 1)
                    if l == 0 and c < 4:
                        accumulate(bank[4 + c][:, :], [(cB2[:, i], w[:, i]) for i in range(KT)]).then_inc(S["modc"], 1)

            modulation(0)
            pe.wait_ge(S["in_const"], 16)
            transposes("tctx", h, "nctx")
            pe.wait_ge(S["turned_ev"], turned("tctx", 4))
            wait_weight(pe, wat["in1"])
            pe.wait_ge(S["modc_ev"], 4)
            for t in range(NT):
                accumulate(bank[4 + t][:, 0:256], [(tile(hT[:, i], t), slot(wat["in1"])[:, i, 0:256]) for i in range(KT)]).then_inc(
                    S["operands"], 1)
            transposes("t1_0", h, "n1_0")
            pe.wait_ge(S["operands_ev"], operand("pctx", NT))
            project("pin1", wat["in1"], [n for _, n in INC], "t1_0")
            pe.wait_ge(S["rope1"], 1)
            for t in range(NT):
                for p in range(4):
                    ins = pe.transpose(tile(bank[t], p), tile(qk[:, t], p), ident)
                ins.then_inc(S["operands"], 1)
            for t in range(NT):
                pe.transpose(tile(bank[2], t), qk[:, t, 512:640], ident)
                ins = pe.transpose(tile(bank[2], 2 + t), kvc[:, t, 0:128], ident)
            ins.then_inc(S["operands"], 1)
            for t in range(NT):
                pe.wait_ge(S["gmlp_v"], 1 + t + 1)
                pe.wait_ge(S["pin1_ev"], 8)
                for g in range(8):
                    ins = pe.matmul(bank[4 + t][:, 64 * g:64 * g + 64], wsT[:, g], proj[:, t, 1280 + 64 * g:1344 + 64 * g],
                                    start=True, stop=True)
                ins.then_inc(S["gmlp"], 1)

            def scores1(it):
                t, j = it // 2, it % 2
                for p in range(4):
                    if it:
                        pe.wait_ge(S["a_s_ev"], 4 * (it - 1) + p + 1)
                    pe.matmul(bank[p][:, :], tile(qT[64 * j:64 * j + 64, p], t), kT[64 * j:64 * j + 64, :],
                              start=True, stop=True).then_inc(S["a_s"], 1)

            pe.wait_ge(S["operands_ev"], operand("tq1", 3))
            scores1(0)
            for it in range(4):
                t, j = it // 2, it % 2
                if it < 3:
                    scores1(it + 1)
                for p in range(4):
                    k = 4 * it + p
                    pe.wait_ge(S["a_exp"], 5 * it + p + 1)
                    if k >= 2:
                        pe.wait_ge(S["a_pt_ev"], k - 1)
                    else:
                        pe.wait_ge(S["mixed"], NT)
                    for b in range(4):
                        ins = pe.transpose(tile(bank[4 + k % 2], b), tile(sc1[:, p], b), ident)
                    ins.then_inc(S["a_pt"], 1)
                    pe.wait_ge(S["a_pt_ev"], k + 1)
                    if it >= 2:
                        pe.wait_ge(S["attn_o"], it - 1)
                    vals = [proj[:, b, 640 + 64 * j:704 + 64 * j] for b in range(NT)]
                    vals += [kvc[:, b, 128 + 64 * j:192 + 64 * j] for b in range(NT)]
                    accumulate(bank[6 + it % 2][:, 64 * p:64 * p + 64], [(pT[:, b], vals[b]) for b in range(4)]).then_inc(
                        S["a_pv"], 1)
            pe.wait_ge(S["a_s_ev"], 16)
            pe.wait_ge(S["mixed"], NT)
            transposes("tcat", mixcat, "attn_o", per=2)
            pe.wait_ge(S["attn_o"], 4)
            project("pout1", wat["out1"], [512, 512], "tcat")

            def peer(l):
                transposes(f"t2_{l}", h, f"n2_{l}")
                pe.wait_ge(S["turned_ev"], turned(f"t2_{l}", 4))
                for k in range(16):
                    i = wat[f"wq{l}"] + k // 4
                    if k % 4 == 0:
                        wait_weight(pe, i)
                    if k >= 4:
                        pe.wait_ge(S["pq_ev"], 16 * l + k - 3)
                    accumulate(bank[4 + k % 4][:, 0:T], [(tile(slot(i)[:, q], k % 4), hT[:, q]) for q in range(KT)]).then_inc(
                        S["pq"], 1)
                pe.wait_ge(S["pq_ev"], 16 * l + 16)
                for k in range(8):
                    t = k // 4
                    if k >= 4:
                        pe.wait_ge(S["ps_ev"], 8 * l + k - 3)
                    for q in range(4):
                        r = 4 * (k % 4) + q
                        ins = pe.matmul(tile(bank[k % 4], q), tile(q16[:, r], t), keysT[:, l, r % 2], start=True, stop=True)
                    ins.then_inc(S["ps"], 1)
                pe.wait_ge(S["ps_ev"], 8 * l + 8)
                for t in range(NT):
                    n0 = PICKS * (NT * l + t)

                    def pick(i, s, start, stop):
                        pe.wait_ge(S[f"gathered{s}"], i * 16 + 16 * (16 * (4 * l + 2 + t) + 1))
                        pe.wait_ge(S["diag_made"], i * GSLOTS + (n0 + s + 1))
                        for c in range(2):
                            ins = pe.matmul(bank[2 * t + c][:, :], diag[:, s % 4], G[:, s, 512 * c:512 * c + 512],
                                            start=start, stop=stop, skip_group_check=True)
                        ins.then_inc(S["up_used"], 1)

                    last = PICKS // GSLOTS - 1
                    for s in range(GSLOTS):
                        pick(0, s, s == 0, False)
                    with pe.Fori(1, last) as i:
                        for s in range(GSLOTS):
                            pick(i, s, False, False)
                    for s in range(GSLOTS):
                        pick(last, s, False, s == GSLOTS - 1)

            peer(0)
            modulation(1)
            for k in range(8):
                pe.wait_ge(S["normed"], normed("n1_1", NT))
                if k >= 4:
                    pe.wait_ge(S["operands_ev"], operand("ppool", k - 3))
                accumulate(bank[4 + k % 4][:, 0:T], [(tile(h[:, i], k), band[:, i, k // 2]) for i in range(NT)]).then_inc(
                    S["operands"], 1)
            pe.wait_ge(S["operands_ev"], operand("ppool", 8))
            wait_weight(pe, wat["pool"])
            for k in range(4):
                c, t = k // 2, k % 2
                for g in (2 * c, 2 * c + 1):
                    ins = accumulate(bank[k][:, 256 * (g % 2):256 * (g % 2) + 256],
                                     [(tile(hT[:, 2 * g + i], t), slot(wat["pool"])[:, 2 * g + i]) for i in range(2)])
                ins.then_inc(S["py_pool"], 1)
            peer(1)
            transposes("tmix", h, "nmix")
            project("pin2", wat["in2"], [n for _, n in ZC], "tmix")
            pe.wait_ge(S["pin2_ev"], 20)
            for kv in range(2):
                for g in range(2):
                    for t in range(NT):
                        pe.wait_ge(S["kcd"], t + 1)
                        ins = pe.transpose(tile(bank[kv], 2 * g + t), kcd[:, t, 2 * kv + g], ident)
                ins.then_inc(S["operands"], 1)
            pe.wait_ge(S["windows"], 16)
            for kv in range(2):
                i = wat["w1k"] + kv
                wait_weight(pe, i)
                accumulate(bank[3][0:64, 256 * kv:256 * kv + 256], [(X[:, kv, k], slot(i)[:, k]) for k in range(16)]).then_inc(
                    S["hid"], 1)
            pe.wait_ge(S["h1_gelu"], 1)
            for kv in range(2):
                for k in range(2):
                    q = 2 * kv + k
                    ins = pe.transpose(bank[2][:, 64 * q:64 * q + 64], H1[0:64, kv, P * k:P * k + P], ident[0:64, 0:64])
            ins.then_inc(S["operands"], 1)
            pe.wait_ge(S["operands_ev"], operand("th1", 1))
            for kv in range(2):
                w2 = col("w2k" if kv == 0 else "w2v").rearrange("p (k n) -> p k n", k=2)
                accumulate(bank[kv][0:64, 0:64], [(H1T[:, kv, k], w2[:, k]) for k in range(2)]).then_inc(S["cmp"], 1)
            for t in range(NT):
                pe.wait_ge(S["rope2"], t + 1)
                for p in range(4):
                    ins = pe.transpose(tile(bank[4 + t], p), tile(qr[:, t], p), ident)
                ins.then_inc(S["operands"], 1)
            for t in range(NT):
                pe.transpose(tile(bank[6], t), qr[:, t, 512:640], ident)
                ins = pe.transpose(tile(bank[6], 2 + t), qr[:, t, 640:768], ident)
            ins.then_inc(S["operands"], 1)
            pe.wait_ge(S["cmp_v"], 2)
            pe.transpose(bank[7][:, 0:64], kc2[0:64, 0:128], ident[0:64, 0:64]).then_inc(S["operands"], 1)

            def scores2(it):
                t, j = it // 2, it % 2
                for p in range(4):
                    if it:
                        pe.wait_ge(S["b_s_ev"], 4 * (it - 1) + p + 1)
                    pe.matmul(bank[p][:, :], tile(nqT[64 * j:64 * j + 64, p], t), kswT[64 * j:64 * j + 64, :],
                              start=True, stop=True).then_inc(S["b_s"], 1)

            pe.wait_ge(S["operands_ev"], operand("tq2", 4))
            pe.wait_ge(S["cmp_v"], 5)
            for t in range(NT):
                if t:
                    pe.wait_ge(S["b_pt_ev"], 8)
                for p in range(4):
                    ins = pe.matmul(bank[5][:, 64 * p:64 * p + 64], tile(nqT[:, p], t), kcT, start=True, stop=True)
                ins.then_inc(S["c_s"], 1)
                scores2(2 * t)
                pe.wait_ge(S["c_p"], t + 1)
                for p in range(4):
                    ins = pe.transpose(bank[6][0:64, P * p:P * p + P], pcm[:, p], ident)
                ins.then_inc(S["c_pt"], 1)
                scores2(2 * t + 1)
                for it in (2 * t, 2 * t + 1):
                    j = it % 2
                    for p in range(4):
                        k = 4 * it + p
                        pe.wait_ge(S["b_p"], it + 1)
                        if k >= 2:
                            pe.wait_ge(S["b_pt_ev"], k - 1)
                        blocks = [(br, b) for br in range(2) for b in range(t + 1)]
                        for n, (br, b) in enumerate(blocks):
                            ins = pe.transpose(tile(bank[4 + k % 2], n), tile(psc[:, 2 * p + br], b), ident)
                        ins.then_inc(S["b_pt"], 1)
                        pe.wait_ge(S["b_pt_ev"], k + 1)
                        pe.wait_ge(S["c_pt_ev"], t + 1)
                        if t:
                            pe.wait_ge(S["nsa_o"], 1)
                        pairs = [(pcT[0:64, p], vcz[0:64, j])]
                        for n, (br, b) in enumerate(blocks):
                            a0 = (Z_VS, Z_VW)[br] + 64 * j
                            pairs.append((npT[:, n], z[:, b, a0:a0 + 64]))
                        hd = 4 * j + p
                        accumulate(bank[7][:, 64 * hd:64 * hd + 64], pairs).then_inc(S["b_pv"], 1)
            pe.wait_ge(S["b_s_ev"], 16)
            for t in range(NT):
                pe.wait_ge(S["nsa_o"], t + 1)
                for k in range(4):
                    ins = pe.transpose(tile(bank[t], k), tile(zcat[:, t], k), ident)
                ins.then_inc(S["operands"], 1)

            def project4(weight, ready):
                i = wat[weight]
                wait_weight(pe, i)
                pe.wait_ge(S["operands_ev"], operand(ready, NT))
                for k in range(4):
                    c, t = k // 2, k % 2
                    accumulate(bank[4 + k][:, :], [(tile(zT[:, q], t), slot(i)[:, q, 512 * c:512 * c + 512]) for q in range(4)]
                               ).then_inc(S["branch"], 1)

            project4("nsa", "tnsa")
            for n, (c0, width) in enumerate(((Z_GQ, 128), (Z_GK, 128), (Z_GA, 16))):
                for q in range(2 if n < 2 else 1):
                    for t in range(NT):
                        ins = pe.transpose(bank[n][0:width, 256 * q + P * t:256 * q + P * t + P],
                                           z[:, t, c0 + P * q:c0 + P * q + width], ident)
                ins.then_inc(S["operands"], 1)
            pe.wait_ge(S["operands_ev"], operand("tgla", 3))
            for q in range(2):
                ins = pe.matmul(bank[3][:, 256 * q:256 * q + 256], tile(col("wa2")[0:16], q), gaT[0:16, :], start=True, stop=True)
            ins.then_inc(S["gla_x"], 1)
            pe.wait_ge(S["gla_v"], 4)
            for q in range(2):
                for t in range(NT):
                    ins = pe.transpose(tile(bank[q], t), tile(gt2[:, q], t), ident)
                ins.then_inc(S["operands"], 1)
            pe.wait_ge(S["ya"], 4)
            pe.wait_ge(S["qm"], 8)
            for k in range(16):
                q, t, u = k // 8, (k // 4) % 2, k % 4
                pe.wait_ge(S["ek_ready"], k + 1)
                for i in range(16):
                    n = 16 * u + i
                    ins = pe.matmul(bank[6 + q][:, 256 * t + 4 * n:256 * t + 4 * n + 4], tile(Ek[k % 2], i),
                                    QM[:, q, t, 4 * n:4 * n + 4], start=True, stop=True)
                ins.then_inc(S["attn_gla"], 1)
            pe.wait_ge(S["operands_ev"], operand("tkd", 2))
            for c in range(1, 4):
                for q in range(2):
                    t, o = (c - 1) // 2, 64 * ((c - 1) % 2)
                    if c >= 2:
                        pe.wait_ge(S["st"], 4 * (c - 2) + 2 * q + 2)
                    pe.matmul(bank[4 + q][:, 0:256], kdn[o:o + 64, t, P * q:P * q + P],
                              z[o:o + 64, t, Z_GV + 256 * q:Z_GV + 256 * q + 256], start=True, stop=True).then_inc(S["state"], 1)
            pe.wait_ge(S["st"], 12)
            pe.wait_ge(S["qz"], 8)
            for t in range(NT):
                pe.wait_ge(S["AT"], 4 * (t + 1))
                for q in range(2):
                    for c in (2 * t, 2 * t + 1):
                        if c:
                            pe.matmul(bank[t][:, 256 * q:256 * q + 256], QZ[:, q, c], st[:, c, q], start=c in (1, 2), stop=False,
                                      skip_group_check=True)
                    for hd in (2 * q, 2 * q + 1):
                        ins = pe.matmul(tile(bank[t], hd), AT[:, hd], z[:, t, Z_GV + P * hd:Z_GV + P * hd + P], start=False,
                                        stop=True, skip_group_check=True)
                ins.then_inc(S["gla_o"], 1)
            pe.wait_ge(S["go_v"], 2)
            for t in range(NT):
                for k in range(4):
                    ins = pe.transpose(tile(bank[t], k), tile(zcat[:, t], k), ident)
                ins.then_inc(S["operands"], 1)
            project4("gla", "tgo")
            pe.wait_ge(S["zy"], 4)
            transposes("tzy", zy, "zy")
            project("pout2", wat["out2"], [512, 512], "tzy")
            transposes("tffn", h, "nffn")
            pe.wait_ge(S["turned_ev"], turned("tffn", 4))
            for t in range(NT):
                accumulate(bank[4 + t][:, 0:36], [(tile(hT[:, i], t), wr[:, i]) for i in range(KT)]).then_inc(S["router"], 1)
            w_k = [w_moe[i].rearrange("p (k n) -> p k n", k=8 if i % 3 < 2 else 4) for i in range(6)]
            pe.wait_ge(S["chosen"], NT)
            tri = cst("tri")
            pe.matmul(bank[6][:, 0:32], tri, chosen[:, 0], start=True, stop=True).then_inc(S["placed"], 1)
            accumulate(bank[7][:, 0:32], [(ones, chosen[:, 0]), (tri, chosen[:, 1])]).then_inc(S["placed"], 1)
            accumulate(bank[3][:, 0:32], [(ones, chosen[:, 0]), (ones, chosen[:, 1])]).then_inc(S["placed"], 1)
            pe.wait_ge(S["crowd"], 1)
            crowded = pe.value_load(crowd[0:1, 0:1], min_val=0, max_val=1)
            with pe.If(crowded == 0):
                def tokens(k, n):
                    pe.wait_ge(S["selected"], n)
                    for q in range(KT):
                        ins = accumulate(bank[k][:, CAP * q:CAP * q + CAP], [(tile(h[:, t], q), msel[:, k, t]) for t in range(NT)])
                    ins.then_inc(S["x_sel"], 1)

                tokens(0, 1)
                with pe.Fori(0, 16) as i:
                    for k in range(2):
                        pe.wait_ge(S["x_sel_ev"], i * 2 + (k + 1))
                        for j in range(2):
                            pe.wait_ge(moe_landed[3 * k + j], i * 16 + 16)
                            for f in range(4):
                                ins = accumulate(bank[2 + k][:, 256 * j + CAP * f:256 * j + CAP * f + CAP],
                                                 [(tile(w_k[3 * k + j][:, q], f), xs[:, k, q]) for q in range(KT)])
                        ins.then_inc(S["moe_u"], 4)
                        tokens(1 - k, i * 2 + (k + 2))
                        pe.wait_ge(S["hdn_made"], i * 2 + (k + 1))
                        pe.wait_ge(moe_landed[3 * k + 2], i * 16 + 16)
                        for c in range(2):
                            pe.wait_ge(S["moe_added"], i * 4 + (2 * k + c + 1))
                            accumulate(bank[4 + 2 * k + c][0:CAP, :],
                                       [(hsel[:, k, f], w_k[3 * k + 2][:, f, 512 * c:512 * c + 512]) for f in range(4)]).then_inc(
                                S["moe_y"], 2)
            with pe.Else():
                with pe.Fori(0, 16) as e:
                    for k in range(2):
                        for f in range(4):
                            pe.wait_ge(S["hdn_made"], e * 8 + (4 * k + f + 1))
                            for j in range(2):
                                if f == 0:
                                    pe.wait_ge(moe_landed[3 * k + j], e * 16 + 16)
                                accumulate(bank[f % 2 + 2 * j][:, 0:T],
                                           [(tile(w_k[3 * k + j][:, i], f), hT[:, i]) for i in range(KT)]).then_inc(
                                    S["moe_g" if j == 0 else "moe_u"], 1)
                        pe.wait_ge(S["hdn_made"], e * 8 + (4 * k + 4 + 2))
                        pe.wait_ge(moe_landed[3 * k + 2], e * 16 + 16)
                        for i in range(4):
                            t, c = i // 2, i % 2
                            pe.wait_ge(S["moe_added"], e * 8 + (4 * k + i + 1))
                            accumulate(bank[4 + i][:, :], [(tile(hdn[:, f], t), w_k[3 * k + 2][:, f, 512 * c:512 * c + 512])
                                                           for f in range(4)]).then_inc(S["moe_y"], 1)


_ROWS = {"sink": "attn_sink", "glag": "gla_norm_g_2", "b1k": "cmp_b1_k_2", "b1v": "cmp_b1_v_2", "b2k": "cmp_b2_k_2",
         "b2v": "cmp_b2_v_2"}


def kernel(**inputs):
    import concourse.bacc as bacc
    from concourse.bass_utils import run_bass_kernel_spmd

    f = {k: np.ascontiguousarray(v) for k, v in inputs.items()}

    def lane(m):
        k = m.shape[0] // P
        return m.reshape(k, P, -1).transpose(1, 0, 2).reshape(P, -1)

    def lower(m):
        out = np.zeros((P, m.shape[1]), m.dtype)
        out[:m.shape[0]] = m
        return out

    def window_rows(m):
        return m.reshape(16, 2, 64).transpose(1, 2, 0).reshape(P, 16)

    part = {
        "c": lane(f["c"].reshape(D, 1)), "cctx": lane(f["c_ctx"].reshape(D, 1)), "b_a": lane(f["gla_b_a_2"].reshape(256, 1)),
        "bs": f["gmlp_b_s"][0].T, "posk": window_rows(f["cmp_pos_k_2"][0]), "posv": window_rows(f["cmp_pos_v_2"][0]),
        "wsT": f["gmlp_w_s"][0].transpose(2, 0, 1).reshape(P, -1),
        "keysT": f["peer_sub_keys"].transpose(3, 0, 1, 2).reshape(P, -1),
        "w2k": lane(f["cmp_w2_k_2"][0]), "w2v": lane(f["cmp_w2_v_2"][0]),
        "wr": lane(np.concatenate([f["w_grp_2"][0], f["w_exp_2"][0]], 1)), "wa2": lower(f["gla_w_a2_2"][0])}
    cols = np.concatenate([part[n] for n in COL_AT], 1)
    row = {n: f[_ROWS[n]].reshape(-1) for n in _ROWS}
    row["brt"] = np.concatenate([f["b_grp_2"][0], f["b_exp_2"][0]])
    rows = np.concatenate([row[n] for n in ROW_AT])[None]
    gains = np.stack([f["norm1_g"][0], f["norm2_g"][0], f["norm1_g"][1], f["pool_scale"][0], f["norm2_g"][1], f["final_g"],
                      f["g_mix_2"][0], f["g_ffn_2"][0], f["g_final_2"]])
    pos = f["positions_2"][0]
    pos3 = np.zeros((P, 3), pos.dtype)
    pos3[:, 0:2] = pos.reshape(NT, P).T
    for g in range(2):
        pos3[32 * g:32 * g + 15, 2] = pos[31::16]
    arrays = {
        "x": f["x"][0], "ctx": f["ctx"][0], "const": shape_constants(), "cols": np.ascontiguousarray(cols), "rows": rows,
        "gains": gains, "pos3": pos3, "mod_w": f["mod_w"], "mod_b": f["mod_b"], "attn_in_w": f["attn_in_w"][0],
        "attn_out_w": f["attn_out_w"][0], "pool_w": f["pool_w"][0], "peer_w_q": f["peer_w_q"],
        "down": f["peer_down"].reshape(2 * EXPERTS, D), "up": f["peer_up"].reshape(2 * EXPERTS, D), "w_in_2": f["w_in_2"][0],
        "cmp_w1_k_2": f["cmp_w1_k_2"][0], "cmp_w1_v_2": f["cmp_w1_v_2"][0], "w_proj_nsa_2": f["w_proj_nsa_2"][0],
        "w_proj_gla_2": f["w_proj_gla_2"][0], "w_out_2": f["w_out_2"][0], "w_gate_2": f["w_gate_2"][0],
        "w_up_2": f["w_up_2"][0], "w_down_2": f["w_down_2"][0]}
    nc = bacc.Bacc("TRN2", target_bir_lowering=False, num_devices=1)
    a = {n: nc.dram_tensor(f"in_{n}", v.shape, mybir.dt.from_np(v.dtype), kind="ExternalInput").ap() for n, v in arrays.items()}
    out = nc.dram_tensor("out", (T, D), F32, kind="ExternalOutput").ap()
    program(nc, a, out)
    return run_bass_kernel_spmd(nc, [{f"in_{n}": v for n, v in arrays.items()}], core_ids=[0]).results[0]["out"].reshape(1, T, D)
```

```python
from contextlib import ExitStack

import concourse.bass as bass
import numpy as np
from concourse import mybir

F32 = mybir.dt.float32
U32 = mybir.dt.uint32
I32 = mybir.dt.int32
ALU = mybir.AluOpType
ACT = mybir.ActivationFunctionType
AX = mybir.AxisListType.X

P = 128
T = 256
NT = T // P
D = 1024
KT = D // P
NEG = -1e30
EPS = 1e-6
SLOT = 4096
RING = 4
CAP = 64
PICKS = 128
GSLOTS = 8
ROUNDS = PICKS // GSLOTS
ALONE = (6, 1)
SHARED = tuple(ROUNDS - n for n in ALONE)
EXPERTS = 16384

Z_Q, Z_KC, Z_KS, Z_VS, Z_KW, Z_VW, Z_NG = 0, 512, 768, 896, 1024, 1152, 1280
Z_GQ, Z_GK, Z_GV, Z_GA, Z_GR, Z_MA, Z_MB, Z_W = 1304, 1560, 1816, 2328, 2344, 2856, 3880, 4904


def offsets(sizes):
    at, out = 0, {}
    for name, n in sizes:
        out[name] = (at, n)
        at += n
    return out, at


CONST_AT, CONST_W = offsets([
    ("ident", 128), ("ones", 128), ("win", 512), ("causal", 512), ("cmpmask", 64), ("cmpok", 64),
    ("rope", 128), ("inv", 32), ("glamask", 128), ("reset", 256), ("iota", 64), ("tri", 128), ("band", 2048)])
COL_AT, COL_W = offsets([
    ("c", 8), ("cctx", 8), ("b_a", 2), ("bs", 8), ("posk", 16), ("posv", 16), ("wsT", 1024), ("keysT", 512),
    ("w2k", 128), ("w2v", 128), ("wr", 288), ("wa2", 256)])
ROW_AT, ROW_W = offsets([
    ("sink", 8), ("glag", 512), ("brt", 36), ("b1k", 256), ("b1v", 256), ("b2k", 64), ("b2v", 64)])
G_NAMES = ["norm1_0", "norm2_0", "norm1_1", "pool", "norm2_1", "final_1", "mix", "ffn", "final_2"]


NORMS = ["nctx", "n1_0", "n2_0", "n1_1", "n2_1", "nf1", "nmix", "nffn", "nf2"]
TURNS = ["tctx", "t1_0", "tcat", "t2_0", "t2_1", "tmix", "tzy", "tffn"]


def normed(tag, n):
    return NT * NORMS.index(tag) + n


def turned(tag, n):
    return 4 * TURNS.index(tag) + n


OPERANDS = {"pctx": 2, "tq1": 3, "ppool": 8, "tkc": 2, "th1": 1, "tq2": 4, "tnsa": 2, "tgla": 3, "tkd": 2, "tgo": 2}


def mod_part(l, c, of_context):
    return 16 * l + c + (0 if l else min(c, 4)) + of_context


MOD_PARTS = [[(c, ctx) for c in range(12) for ctx in range(2 if l == 0 and c < 4 else 1)] for l in range(2)]


def diagonals(l, t):
    passes = NT * l + t
    return (PICKS - SHARED[0]) * ((passes + 1) // 2) + (PICKS - SHARED[1]) * (passes // 2)


def added_before(l, t):
    return sum(SHARED) * l + SHARED[0] * t


def operand(tag, n):
    names = list(OPERANDS)
    return sum(OPERANDS[name] for name in names[:names.index(tag)]) + n


def shape_constants():
    c = np.zeros((P, CONST_W), np.float32)

    def put(name, a):
        at, n = CONST_AT[name]
        c[:, at:at + n] = np.asarray(a, np.float32).reshape(P, n)

    t = np.arange(T)
    tile = t.reshape(NT, P)
    put("ident", np.eye(P))
    put("ones", np.ones((P, P)))
    near = np.abs(tile[:, :, None] - t[None, None, :]) <= 128
    put("win", np.where(near, 0, NEG).transpose(1, 0, 2))
    put("causal", np.where(t[None, None, :] <= tile[:, :, None], 0, NEG).transpose(1, 0, 2))
    n = np.arange(32)
    ok = (16 * n + 31)[None, None, :] <= tile[:, :, None]
    ok = ok & (n < 15)[None, None, :]
    put("cmpmask", np.where(ok, 0, NEG).transpose(1, 0, 2))
    put("cmpok", ok.transpose(1, 0, 2))
    inv = np.power(np.float32(10000.0), -np.arange(16, dtype=np.float32) / np.float32(16)).astype(np.float32)
    row, col = (t // 64).astype(np.float32), (t % 64).astype(np.float32)
    ang = np.stack([row[:, None] * inv, col[:, None] * inv], 1)
    rope = np.stack([np.cos(ang), np.sin(ang)], 1)
    put("rope", rope.reshape(NT, P, 64).transpose(1, 0, 2))
    inv2 = (np.float32(1.0) / np.power(np.float32(10000.0), np.arange(32, dtype=np.float32) / np.float32(32)))
    put("inv", np.broadcast_to(inv2, (P, 32)))
    cs, ct = np.arange(P), np.arange(P)
    put("glamask", (cs[:, None] // 64 == ct[None, :] // 64) & (cs[:, None] % 64 <= ct[None, :] % 64))
    put("reset", np.broadcast_to((t % 64 != 0), (P, T)))
    put("iota", np.broadcast_to(np.arange(64), (P, 64)))
    put("tri", cs[:, None] < ct[None, :])
    band = np.zeros((4, T, T), np.float32)
    for g, w in enumerate((2, 4, 8, 16)):
        for i in range(T):
            lo, hi = max(i - w // 2, 0), min(i + w // 2, T)
            band[g, lo:hi, i] += np.float32(1.0) / np.float32(hi - lo)
            band[g, i, i] -= 1.0
    put("band", band.reshape(4, NT, P, T).transpose(2, 1, 0, 3))
    return c


class Chain:

    def __init__(self, eng, sem):
        self.eng, self.sem, self.n = eng, sem, 0

    def __call__(self, ins):
        ins.then_inc(self.sem, 1)
        self.n += 1
        self.eng.wait_ge(self.sem, self.n)


def program(nc, a, out):
    ctx = ExitStack()
    with ctx:
        def sb(name, shape, dt=F32):
            return ctx.enter_context(nc.sbuf_tensor(name, shape, dt))

        class Sems(dict):

            def __missing__(self, name):
                self[name] = ctx.enter_context(nc.semaphore(name))
                return self[name]

        S = Sems()
        moe_rows = nc.dram_tensor("moe_rows", (64 * CAP, D // 2), F32).ap()

        const = sb("const", [P, CONST_W])
        cols = sb("cols", [P, COL_W])
        rows = sb("rows", [P, ROW_W])
        gvec = sb("gvec", [P, 2, D])
        ring = sb("ring", [P, RING, SLOT])
        x = sb("x", [P, NT, D])
        h = sb("h", [P, NT, D])
        hT = sb("hT", [P, KT, T])
        posi = sb("posi", [P, 3], I32)
        stat = sb("stat", [P, 64])
        ARENA = 20480
        arena = sb("arena", [P, ARENA])
        bank = [ctx.enter_context(nc.psum_tensor(f"bank{i}", [P, 512], F32)) for i in range(8)]

        class Carve:

            def __init__(self, at):
                self.at = at

            def __call__(self, *shape):
                n = int(np.prod(shape))
                assert self.at + n <= ARENA, (self.at, n)
                ap = arena[:, self.at:self.at + n]
                self.at += n
                if len(shape) == 2:
                    return ap.rearrange("p (a b) -> p a b", a=shape[0])
                if len(shape) == 3:
                    return ap.rearrange("p (a b c) -> p a b c", a=shape[0], b=shape[1])
                if len(shape) == 4:
                    return ap.rearrange("p (a b c d) -> p a b c d", a=shape[0], b=shape[1], c=shape[2])
                return ap

        def cst(name):
            at, n = CONST_AT[name]
            return const[:, at:at + n]

        def col(name):
            at, n = COL_AT[name]
            return cols[:, at:at + n]

        def rw(name):
            at, n = ROW_AT[name]
            return rows[:, at:at + n]

        ident = cst("ident")
        ones = cst("ones")
        band = cst("band").rearrange("p (k g t) -> p k g t", k=NT, g=4)
        wsT = col("wsT").rearrange("p (g q) -> p g q", g=8)
        keysT = col("keysT").rearrange("p (l s n) -> p l s n", l=2, s=2)
        wr = col("wr").rearrange("p (k n) -> p k n", k=KT)

        cv = Carve(0)
        mod = cv(6, D)
        m1 = Carve(cv.at)
        hflat = hT.rearrange("p a b -> p (a b)")
        cB, cB2 = (hflat[:, 256 * i:256 * i + 256].rearrange("p (a b) -> p a b", a=KT) for i in range(2))
        mpart = hflat[:, 512:1536].rearrange("p (a b) -> p a b", a=2)
        modc = m1(2, D)
        ctxn = m1(NT, D)
        m1 = Carve(cv.at)
        proj = m1(NT, 1792)
        mixcat = m1(NT, D)
        qk = m1(NT, 640)
        qT = m1(4, T)
        kT = m1(512)
        kvc = m1(NT, 256)
        scs = [m1(4, 512), h[:, :, :].rearrange("p a (b c) -> p (a b) c", b=2)]
        pT = m1(2, 4, P)
        tmp1 = m1(NT * 320)
        gst = m1(5, NT * 8)
        asts = [m1(6, 4) for _ in range(2)]
        pe_ = Carve(cv.at)
        G = pe_(GSLOTS, D)
        idx_all = pe_(NT, PICKS).bitcast(U32)
        gate = pe_(NT, PICKS)
        act = pe_(NT, PICKS)
        diag = pe_(4, P)
        gt = arena[:, ARENA - 1024:ARENA].rearrange("p (a b) -> p a b", a=2)
        idxb = pe_(GSLOTS).bitcast(U32)
        at_topk = pe_.at
        q16 = Carve(cv.at)(16, T)
        s16 = [Carve(cv.at + 4096)(16, P), hT.rearrange("p a b -> p (a b)").rearrange("p (a b) -> p a b", b=P)]
        pk = Carve(at_topk)
        gsum = pk(2, 8)
        usum = Carve(pk.at)(NT, D)
        v16 = pk(8, 2, 16)
        i16 = pk(16, 16).bitcast(U32)
        i16f = pk(8, 2, 16)
        bv = pk(8, 16)
        bp = pk(8, 16).bitcast(U32)
        ab = pk(2, PICKS).bitcast(U32)
        abf = pk(2, PICKS)
        sel = pk(2, PICKS)
        cand = pk(8, 256)
        onehot = [s16[i].rearrange("p a (b c) -> p (a b) c", c=16) for i in range(NT)]

        def kn(w, c0, n):
            return w.rearrange("(k p) n -> p k n", p=P)[:, :, c0:c0 + n]

        loads, freed, wat = [], [], {}

        def stream(tag, aps, used):
            wat[tag] = len(loads)
            loads.extend(aps)
            freed.extend(used(c) for c in range(len(aps)))

        stream("mod0", [kn(a["mod_w"][0], 512 * c, 512) for c in range(12)], lambda c: ("modp", mod_part(0, c, c < 4) + 1))
        INC = [(512, 512), (0, 512), (1024, 512), (1536, 256)]
        stream("in1", [kn(a["attn_in_w"], c0, n) for c0, n in INC], lambda c: ("pin1", 2 * c + 2))
        stream("out1", [kn(a["attn_out_w"], 512 * c, 512) for c in range(2)], lambda c: ("pout1", 2 * c + 2))
        stream("wq0", [kn(a["peer_w_q"][0], 512 * c, 512) for c in range(4)], lambda c: ("pq", 4 * c + 4))
        stream("mod1", [kn(a["mod_w"][1], 512 * c, 512) for c in range(12)], lambda c: ("modp", mod_part(1, c, 0) + 1))
        stream("pool", [a["pool_w"].rearrange("g (k p) e -> p (g k) e", p=P)], lambda c: ("py_pool", 4))
        stream("wq1", [kn(a["peer_w_q"][1], 512 * c, 512) for c in range(4)], lambda c: ("pq", 16 + 4 * c + 4))
        ZC = [(512 * c, min(512, Z_W - 512 * c)) for c in range(10)]
        stream("in2", [kn(a["w_in_2"], c0, n) for c0, n in ZC], lambda c: ("pin2", 2 * c + 2))
        stream("w1k", [a["cmp_w1_k_2"].rearrange("(k p) n -> p k n", p=P)], lambda c: ("hid", 1))
        stream("w1v", [a["cmp_w1_v_2"].rearrange("(k p) n -> p k n", p=P)], lambda c: ("hid", 2))
        stream("nsa", [a["w_proj_nsa_2"].rearrange("(k p) n -> p k n", p=P)], lambda c: ("branch", 4))
        stream("gla", [a["w_proj_gla_2"].rearrange("(k p) n -> p k n", p=P)], lambda c: ("branch", 8))
        stream("out2", [kn(a["w_out_2"], 512 * c, 512) for c in range(2)], lambda c: ("pout2", 2 * c + 2))

        def slot(i):
            _, k, n = loads[i].shape
            return ring[:, i % RING, 0:k * n].rearrange("p (k n) -> p k n", k=k)

        w_landed = [S[f"w_landed{i}"] for i in range(RING)]

        def wait_weight(eng, i):
            eng.wait_ge(w_landed[i % RING], 16 * (i // RING + 1))

        g_landed = [S[f"g_landed{i}"] for i in range(2)]

        def wait_gain(eng, name):
            i = G_NAMES.index(name)
            eng.wait_ge(g_landed[i % 2], 16 * (i // 2 + 1))
            return gvec[:, i % 2, :]

        mo = Carve(0)
        w_moe = [ring[:, i, :] for i in range(RING)] + [mo(SLOT) for _ in range(2)]
        moe_landed = [S[f"moe_landed{i}"] for i in range(6)]
        hdn = mo(4, T)
        sg = mo(2, T)
        cmb = mo(NT, 32)
        mst = mo(16, 36)
        pick = mo(NT, 2, 32)
        chosen = mo(NT, 32)
        place = mo(NT, 34)
        wts = mo(NT, 2)
        ptmp = mo(NT, 2, 32)
        prow = mo(NT * 2)
        pidx = mo(NT * 2, 2).bitcast(U32)
        crowd = mo(1).bitcast(I32)
        msel = mo(NT, 2 * CAP)
        xs = mo(KT, 2 * CAP)
        hsel = mo(2, 4, CAP)
        ysb = mo(2, 512)
        yback = ring[:, 0, :].rearrange("p (n d) -> p n d", n=4)

        b2 = Carve(0)
        z = b2(NT, Z_W)
        zcat = b2(NT, 512)
        zT = b2(4, T)
        zy = h
        at_b2 = b2.at
        trig = b2(3, 2, 32)
        tang = b2(6, 32)
        qr = b2(NT, 768)
        kcd = b2(NT, 4, P)
        rtmp = b2(384)
        kdT = Carve(b2.at)(4, T)
        X = Carve(b2.at + 1024)(2, 16, 64)
        nq = Carve(b2.at)
        nqT = nq(4, T)
        kswT = nq(512)
        kcT = nq(64)
        vcz = nq(2, 64)
        c2 = Carve(nq.at)
        H1 = c2(2, 256)
        H1T = c2(2, 2, 64)
        kc2 = c2(128)
        ctmp = c2(128)
        ns = Carve(nq.at)
        pscs = [ns(8, T), h[:, :, :].rearrange("p a (b c) -> p (a b) c", c=T)]
        nst = ns(8, 8)
        gsig = ns(NT, 24)
        npT = [Carve(at_b2 + 192 + 192 + n)(4, P) for n in (0, 1312)]
        pcm = Carve(at_b2 + 192 + 192 + 512)(4, 64)
        pcT = Carve(at_b2 + 192 + 192 + 768)(4, P)
        cmp_stats = Carve(at_b2 + 192 + 192 + 1280)(4, 8)

        gl = Carve(at_b2)
        gqT = gl(2, T)
        gkT = gl(2, T)
        gaT = gl(T)
        bb = gl(2, T)
        gt1 = gl(2, T)
        gt2 = gl(2, T)
        kdn = gl(NT, 256)
        QZ = gl(2, 4, P)
        QM = gl(2, 2, 256)
        zx = z[:, :, Z_MA:Z_MB]
        Ek = [h[:, :, :].rearrange("p a b -> p (a b)"), hT[:, :, :].rearrange("p a b -> p (a b)")]
        AT = gl(4, P)
        st = gl(4, 2, 256)
        gel = gl(8)
        gso = gl(8)

        def flat(ap):
            return ap.rearrange("p a b -> p (a b)")

        block = ctx.enter_context(nc.Block())

        @block.sync
        def _(sp):
            sp.dma_start(cols[:, :], a["cols"]).then_inc(S["in_cols"], 16)
            sp.dma_start(x[:, :, :], a["x"].rearrange("(t p) d -> p t d", p=P)).then_inc(S["in_x"], 16)
            sp.dma_start(ctxn, a["ctx"].rearrange("(t p) d -> p t d", p=P)).then_inc(S["in_ctx"], 16)
            sp.dma_start(posi[:, :], a["pos3"]).then_inc(S["in_pos"], 16)
            sp.dma_start(const[:, :], a["const"]).then_inc(S["in_const"], 16)
            sp.dma_start(rows[:, :], a["rows"].to_broadcast([P, ROW_W])).then_inc(S["in_rows"], 16)

            def load_mod_bias(l):
                sp.dma_start(flat(mod), a["mod_b"][l:l + 1, :].to_broadcast([P, 6 * D])).then_inc(S["in_modb"], 16)
                if l == 0:
                    sp.dma_start(flat(modc), a["mod_b"][0:1, 0:2 * D].to_broadcast([P, 2 * D])).then_inc(S["in_modcb"], 16)

            def load_gain(i):
                if i >= 2:
                    sp.wait_ge(S["gain_used"], i - 1)
                sp.dma_start(gvec[:, i % 2, :], a["gains"][i:i + 1, :].to_broadcast([P, D])).then_inc(g_landed[i % 2], 16)

            def load_weight(i):
                if i >= RING:
                    sem, value = freed[i - RING]
                    sp.wait_ge(S[sem], value)
                sp.dma_start(slot(i), loads[i]).then_inc(w_landed[i % RING], 16)

            def load_weights(tag, n):
                for i in range(wat[tag], wat[tag] + n):
                    load_weight(i)

            load_mod_bias(0)
            load_gain(0)
            load_gain(1)
            load_weights("mod0", 12)
            load_weights("in1", 4)
            load_weights("out1", 2)
            load_weights("wq0", 4)
            load_gain(2)
            sp.wait_ge(S["x_peer"], NT)
            load_mod_bias(1)
            load_weights("mod1", 12)
            load_gain(3)
            load_weights("pool", 1)
            load_gain(4)
            load_weights("wq1", 4)
            load_gain(5)
            load_gain(6)
            load_weights("in2", 10)
            load_weights("w1k", 1)
            load_weights("w1v", 1)
            load_weights("nsa", 1)
            load_gain(7)
            load_weights("gla", 1)
            load_weights("out2", 2)
            load_gain(8)
            sp.wait_ge(S["x_mix"], NT * 3)

            def load_expert(i, k, first):
                for j, w in enumerate(("w_gate_2", "w_up_2", "w_down_2")):
                    if not first:
                        sp.wait_ge(S["moe_u" if j < 2 else "moe_y"], i * 8 + (4 * k - 4))
                    kk = 8 if j < 2 else 4
                    src = a[w].rearrange("(e b) k n -> e b k n", b=2)[bass.ds(i, 1), k]
                    src = src.rearrange("e (k p) n -> p (e k) n", p=P)
                    sp.dma_start(w_moe[3 * k + j].rearrange("p (k n) -> p k n", k=kk), src).then_inc(
                        moe_landed[3 * k + j], 16)

            load_expert(0, 0, True)
            load_expert(0, 1, True)
            with sp.Fori(1, 16) as i:
                for k in range(2):
                    load_expert(i, k, False)

            sp.wait_ge(S["out_ready"], NT)
            sp.dma_start(out.rearrange("(t p) d -> p t d", p=P), h[:, :, :]).then_inc(S["stored"], 16)
            sp.wait_ge(S["stored"], 16)

        @block.gpsimd
        def _(pool):
            def gather_pass(l, n):
                tile = n // 2
                table = a["up" if n % 2 else "down"]
                done = 4 * l + n

                def group(i, s, first, shared=0):
                    if first:
                        if n % 2:
                            pool.wait_ge(S["down_used"], PICKS * (2 * l + tile + 1) - GSLOTS + s + 4)
                        elif n == 2:
                            pool.wait_ge(S["up_used"], 4 + PICKS * (2 * l + 1) - GSLOTS + s + 4)
                    else:
                        used = S["up_used" if n % 2 else "down_used"]
                        pool.wait_ge(used, i * GSLOTS + (PICKS * (2 * l + tile) - GSLOTS + s + 4 + 4 * (n % 2)))
                    if shared:
                        pool.wait_ge(S["up_added"], i + (added_before(l, tile) - ALONE[tile] + 1))
                    elif first and s and n == 2:
                        pool.wait_ge(S["up_added"], added_before(l, 1) + 1)
                    turn = done * 32 + 2 * i + s // 4
                    src = idx_all[:, tile, bass.ds(i * GSLOTS + s, 4)]
                    pool.tensor_copy(idxb[:, s:s + 4], src).then_inc(S["idx_copied"], 1)
                    pool.wait_ge(S["idx_copied"], turn + 1)
                    pool.sem_inc(S["idx_seen"], 1)
                    for q in range(s, s + 4):
                        pool.indirect_dma_start(
                            out=G[:, q, :], out_offset=None, in_=table,
                            in_offset=bass.IndirectOffsetOnAxis(ap=idxb[:, q:q + 1], axis=0)).then_inc(S[f"gathered{q}"], 16)

                if n % 2 == 0:
                    pool.wait_ge(S["idx_ready"], 2 * l + tile + 1)
                for s in (0, 4):
                    group(0, s, True)
                alone = ALONE[tile] + 1 if n % 2 else ROUNDS
                if alone > 2:
                    with pool.Fori(1, alone) as i:
                        for s in (0, 4):
                            group(i, s, False)
                else:
                    for s in (0, 4):
                        group(1, s, False)
                if n % 2:
                    with pool.Fori(alone, ROUNDS) as i:
                        for s in (0, 4):
                            group(i, s, False, shared=s)

            for l in range(2):
                for n in range(4):
                    gather_pass(l, n)
            pool.wait_ge(S["crowd"], 1)
            crowded = pool.value_load(crowd[0:1, 0:1], min_val=0, max_val=1)
            with pool.If(crowded == 0):
                for k in range(2):
                    pool.wait_ge(S[f"rows_stored{k}"], 16 * 17)
                for n in range(4):
                    for c in range(2):
                        pool.indirect_dma_start(out=yback[:, n, 512 * c:512 * c + 512], out_offset=None, in_=moe_rows,
                                                in_offset=bass.IndirectOffsetOnAxis(ap=pidx[:, n, c:c + 1], axis=0)).then_inc(
                            S[f"gathered{n}"], 16)

        @block.scalar
        def _(act_):
            link = Chain(act_, S["act_chain"])

            def evac(tag, dsts, banks, before=0):
                for k, (dst, src) in enumerate(zip(dsts, banks)):
                    if tag in OPERANDS:
                        act_.wait_ge(S["operands"], operand(tag, k + 1))
                    else:
                        act_.wait_ge(S[tag], before + k + 1)
                    act_.activation(dst, src, ACT.Copy).then_inc(S["operands_ev" if tag in OPERANDS else tag + "_ev"], 1)

            def norm(tag, src, junk):
                for t in range(NT):
                    act_.activation(junk[:, t], src[:, t], ACT.Square, accum_out=stat[:, t:t + 1]).then_inc(S["norm_sum"], 1)
                act_.wait_ge(S["norm_mean"], NORMS.index(tag) + 1)
                act_.activation(stat[:, 4:6], stat[:, 2:4], ACT.Sqrt).then_inc(S["norm_root"], 1)

            def transposes_out(tag):
                for g in range(4):
                    act_.wait_ge(S["turned"], turned(tag, g + 1))
                    act_.activation(hT[:, 4 * (g % 2):4 * (g % 2) + 4, P * (g // 2):P * (g // 2) + P],
                                    bank[g][:, :].rearrange("p (k t) -> p k t", k=4), ACT.Copy).then_inc(S["turned_ev"], 1)

            act_.sem_inc(S["rows_stored0"], 16)
            act_.sem_inc(S["rows_stored1"], 16)
            act_.wait_ge(S["in_cols"], 16)
            act_.activation(cols[:, 0:16], cols[:, 0:16], ACT.Silu).then_inc(S["silu_c"], 1)
            act_.wait_ge(S["in_ctx"], 16)
            norm("nctx", ctxn, h)
            transposes_out("tctx")
            evac("pctx", [kvc[:, t, :] for t in range(NT)], [bank[4 + t][:, 0:256] for t in range(NT)])
            act_.wait_ge(S["in_x"], 16)
            act_.wait_ge(S["turned"], turned("tctx", 4))
            norm("n1_0", x, h)
            transposes_out("t1_0")
            evac("pin1", [proj[:, t, c0:c0 + n] for c0, n in INC for t in range(NT)],
                 [bank[4 + k % 4][:, 0:INC[k // 2][1]] for k in range(8)])
            act_.wait_ge(S["pin1_ev"], 8)
            for t in range(NT):
                act_.activation(proj[:, t, 768:1792], proj[:, t, 768:1792], ACT.Gelu_apprx_tanh).then_inc(S["gelu1"], 1)
            act_.wait_ge(S["gmlp_v"], 1)
            act_.activation(gst[:, 2], gst[:, 1], ACT.Sqrt).then_inc(S["g_rt"], 1)
            evac("tq1", [qT[:, :, 0:P], qT[:, :, P:T], kT[:, 0:512]],
                 [bank[0][:, :].rearrange("p (k t) -> p k t", k=4), bank[1][:, :].rearrange("p (k t) -> p k t", k=4), bank[2][:, :]])
            for it in range(4):
                sc1, ast = scs[it % 2], asts[it % 2]
                act_.wait_ge(S["a_negm"], it + 1)
                for p in range(4):
                    act_.activation(sc1[:, p], sc1[:, p], ACT.Exp, bias=ast[:, 2, p:p + 1],
                                    accum_out=ast[:, 4, p:p + 1]).then_inc(S["a_exp"], 1)
                act_.activation(ast[:, 3], ast[:, 3], ACT.Exp).then_inc(S["a_exp"], 1)
                for p in range(4):
                    k = 4 * it + p
                    act_.wait_ge(S["a_pt"], k + 1)
                    if k >= 2:
                        act_.wait_ge(S["a_pv"], k - 1)
                    act_.activation(flat(pT[:, k % 2]), bank[4 + k % 2][:, :], ACT.Copy).then_inc(S["a_pt_ev"], 1)
            transposes_out("tcat")

            def peer(l):
                act_.wait_ge(S["x_mix"], NT * (l + 1))
                norm(f"n2_{l}", x, h)
                transposes_out(f"t2_{l}")
                evac("pq", [q16[:, k, :] for k in range(16)], [bank[4 + k % 4][:, 0:T] for k in range(16)], 16 * l)
                evac("ps", [s16[k // 4][:, 4 * (k % 4):4 * (k % 4) + 4, :] for k in range(8)],
                     [bank[k % 4][:, :].rearrange("p (a b) -> p a b", a=4) for k in range(8)], 8 * l)
                for t in range(NT):
                    act_.wait_ge(S["gate_in"], NT * l + t + 1)
                    act_.activation(gate[:, t], gate[:, t], ACT.Exp).then_inc(S["gate_exp"], 1)
                    act_.wait_ge(S["down_used"], PICKS * (2 * l + t + 1))
                    act_.activation(act[:, t], act[:, t], ACT.Gelu_apprx_tanh).then_inc(S["peer_gelu"], 1)
                    act_.wait_ge(S["peer_w"], NT * l + t + 1)
                    n0 = PICKS * (NT * l + t)

                    def diagonal(i, s):
                        act_.wait_ge(S["up_used"], i * GSLOTS + (n0 + s + 1))
                        act_.activation(diag[:, s % 4], ident, ACT.Copy,
                                        scale=act[:, t, bass.ds(i * GSLOTS + s, 1)]).then_inc(S["diag_made"], 1)

                    if ALONE[t] > 1:
                        with act_.Fori(0, ALONE[t]) as i:
                            for s in range(GSLOTS):
                                diagonal(i, s)
                    else:
                        for s in range(GSLOTS):
                            diagonal(0, s)
                    with act_.Fori(ALONE[t], ROUNDS) as i:
                        for s in range(GSLOTS - 1):
                            diagonal(i, s)

            peer(0)
            act_.wait_ge(S["x_peer"], NT)
            act_.wait_ge(S["up_used"], 4 + 2 * PICKS)
            norm("n1_1", x, h)
            evac("ppool", [hT[:, k, :] for k in range(8)], [bank[4 + k % 4][:, 0:T] for k in range(8)])
            peer(1)
            act_.wait_ge(S["x_peer"], 2 * NT)
            norm("nf1", x, h)
            act_.wait_ge(S["x_block1"], NT)
            norm("nmix", x, h)
            transposes_out("tmix")
            evac("pin2", [z[:, t, c0:c0 + n] for c0, n in ZC for t in range(NT)],
                 [bank[4 + k % 4][:, 0:ZC[k // 2][1]] for k in range(20)])
            act_.wait_ge(S["angles"], 1)
            act_.activation(trig[:, :, 1, :], tang[:, 0:3, :], ACT.Sin).then_inc(S["trig"], 1)
            act_.activation(trig[:, :, 0, :], tang[:, 3:6, :], ACT.Sin).then_inc(S["trig"], 1)
            evac("tkc", [kdT[:, 2 * g:2 * g + 2, :] for g in range(2)],
                 [bank[g][:, :].rearrange("p (k t) -> p k t", k=2) for g in range(2)])
            act_.wait_ge(S["cmp_v"], 1)
            act_.activation(flat(H1)[0:64], flat(H1)[0:64], ACT.Gelu_apprx_tanh).then_inc(S["h1_gelu"], 1)
            evac("th1", [H1T.rearrange("p a b c -> p (a b c)")], [bank[2][:, 0:256]])
            evac("tq2", [nqT[:, :, 0:P], nqT[:, :, P:T], kswT[:, 0:512]],
                 [bank[4][:, :].rearrange("p (k t) -> p k t", k=4), bank[5][:, :].rearrange("p (k t) -> p k t", k=4),
                  bank[6][:, :]])
            act_.wait_ge(S["operands"], operand("tq2", 4))
            act_.wait_ge(S["cmp_v"], 3)
            act_.activation(kcT[0:64, 0:32], bank[7][0:64, 0:32], ACT.Copy)
            act_.activation(kcT[64:128, 32:64], bank[7][64:128, 32:64], ACT.Copy).then_inc(S["operands_ev"], 1)
            act_.activation(gsig, z[:, :, Z_NG:Z_NG + 24], ACT.Sigmoid).then_inc(S["z_acts"], 1)
            for t in range(NT):
                act_.wait_ge(S["c_sub"], t + 1)
                act_.activation(pcm, pcm, ACT.Exp).then_inc(S["c_exp"], 1)
                act_.wait_ge(S["c_pt"], t + 1)
                act_.activation(pcT[0:64], bank[6][0:64, :].rearrange("p (k t) -> p k t", k=4), ACT.Copy).then_inc(S["c_pt_ev"], 1)
                for j in range(2):
                    it = 2 * t + j
                    psc = pscs[j]
                    act_.wait_ge(S["b_negm"], it + 1)
                    for q in range(8):
                        act_.activation(psc[:, q], psc[:, q], ACT.Exp, bias=nst[:, 1, q:q + 1],
                                        accum_out=nst[:, 2, q:q + 1]).then_inc(S["b_exp"], 1)
                    for p in range(4):
                        k = 4 * it + p
                        act_.wait_ge(S["b_pt"], k + 1)
                        if k >= 2:
                            act_.wait_ge(S["b_pv"], k - 1)
                        nb = 2 * (t + 1)
                        act_.activation(npT[k % 2][:, 0:nb], bank[4 + k % 2][:, 0:P * nb].rearrange("p (k t) -> p k t", k=nb),
                                        ACT.Copy).then_inc(S["b_pt_ev"], 1)
                act_.wait_ge(S["b_pv"], 4 * (2 * t + 2))
                act_.activation(zcat[:, t], bank[7][:, :], ACT.Copy).then_inc(S["nsa_o"], 1)
            evac("tnsa", [zT[:, :, P * t:P * t + P] for t in range(NT)],
                 [bank[t][:, :].rearrange("p (k t) -> p k t", k=4) for t in range(NT)])
            for t in range(NT):
                act_.activation(z[:, t, Z_MA:Z_W], z[:, t, Z_MA:Z_W], ACT.Sigmoid).then_inc(S["z_acts"], 1)
            evac("tgla", [gqT, gkT, gaT[0:16]],
                 [bank[0][:, :].rearrange("p (k t) -> p k t", k=2), bank[1][:, :].rearrange("p (k t) -> p k t", k=2),
                  bank[2][0:16, 0:256]])
            act_.wait_ge(S["gla_v"], 1)
            act_.activation(gt2, gt2, ACT.Exp, scale=-1.0).then_inc(S["gla_a"], 1)
            act_.wait_ge(S["gla_a"], 1)
            act_.activation(gt2, gt2, ACT.Ln, bias=1.0).then_inc(S["gla_a"], 1)
            act_.wait_ge(S["gla_v"], 2)
            act_.activation(gt1, bb, ACT.Exp).then_inc(S["gla_a"], 1)
            act_.activation(gel.rearrange("p (a c) -> p a c", a=2),
                            bb.rearrange("p a (c s) -> p a c s", s=64)[:, :, :, 63], ACT.Exp).then_inc(S["gla_a"], 1)
            act_.wait_ge(S["gla_v"], 3)
            act_.activation(gt2, gt2, ACT.Exp).then_inc(S["gla_a"], 1)
            evac("tkd", [kdn.rearrange("p t (a b) -> p a t b", a=2)[:, k] for k in range(2)],
                 [bank[k][:, 0:256].rearrange("p (t b) -> p t b", t=2) for k in range(2)])
            for k in range(16):
                act_.wait_ge(S["ek_sub"], k + 1)
                act_.activation(Ek[k % 2], Ek[k % 2], ACT.Exp).then_inc(S["ek_exp"], 1)
            act_.wait_ge(S["go_v"], 1)
            act_.activation(gso, gso, ACT.Sqrt).then_inc(S["go_rt"], 1)
            act_.activation(z[:, :, Z_GR:Z_MA], z[:, :, Z_GR:Z_MA], ACT.Silu).then_inc(S["z_acts"], 1)
            evac("tgo", [zT[:, :, P * t:P * t + P] for t in range(NT)],
                 [bank[t][:, :].rearrange("p (k t) -> p k t", k=4) for t in range(NT)])
            transposes_out("tzy")
            act_.wait_ge(S["x_mix"], NT * 3)
            norm("nffn", x, h)
            transposes_out("tffn")
            for t in range(NT):
                act_.wait_ge(S["r_sub"], t + 1)
                act_.activation(mst[:, 6, 0:5], mst[:, 5, 0:5], ACT.Exp).then_inc(S["r_exp"], 1)
            act_.wait_ge(S["crowd"], 1)
            crowded = act_.value_load(crowd[0:1, 0:1], min_val=0, max_val=1)
            with act_.If(crowded == 0):
                def tokens(pairs):
                    for half in range(2):
                        act_.wait_ge(S["x_sel"], pairs)
                        act_.activation(xs[:, 4 * half:4 * half + 4].rearrange("p a b -> p (a b)"), bank[half][:, :],
                                        ACT.Copy).then_inc(S["x_sel_ev"], 1)

                def rows(i, k):
                    act_.wait_ge(S["moe_y"], i * 8 + (4 * k + 4))
                    act_.wait_ge(S[f"rows_stored{k}"], i * 16 + 16)
                    act_.activation(ysb[:, k], bank[4 + k][:, :], ACT.Copy).then_inc(S["moe_added"], 1)
                    act_.wait_ge(S["moe_added"], i * 2 + (4 + k + 1))
                    dst = moe_rows.rearrange("(e b r) d -> e b r d", b=2, r=2 * CAP)[bass.ds(i, 1), k]
                    act_.dma_start(dst.rearrange("e r d -> (e r) d"), ysb[:, k]).then_inc(S[f"rows_stored{k}"], 16)

                tokens(1)
                with act_.Fori(0, 16) as i:
                    for k in range(2):
                        act_.wait_ge(S["moe_u"], i * 8 + (4 * k + 4))
                        act_.activation(sg[:, k], bank[2 + k][:, 0:256], ACT.Silu).then_inc(S["sg_made"], 1)
                    rows(i, 0)
                    tokens(i + 2)
                    rows(i, 1)
            with act_.Else():
                with act_.Fori(0, 16) as e:
                    for k in range(2):
                        for f in range(4):
                            act_.wait_ge(S["moe_g"], e * 8 + (4 * k + f + 1))
                            act_.wait_ge(S["hdn_made"], e * 8 + (4 * k + f + 1))
                            act_.activation(sg[:, f % 2], bank[f % 2][:, 0:T], ACT.Silu).then_inc(S["sg_made"], 1)
            act_.wait_ge(S["x_moe"], 1)
            norm("nf2", x, h)

        @block.vector
        def _(v):
            link = Chain(v, S["dve_chain"])

            def bc(ap, axis, n):
                ap = ap.unsqueeze(axis)
                shape = list(ap.shape)
                shape[axis] = n
                return ap.to_broadcast(shape)

            def norm(tag, src, dst, scale, shift=None):
                v.wait_ge(S["norm_sum"], normed(tag, NT))
                v.tensor_scalar(stat[:, 2:4], stat[:, 0:2], 1.0 / D, EPS, ALU.mult, ALU.add).then_inc(S["norm_mean"], 1)
                v.wait_ge(S["norm_root"], NORMS.index(tag) + 1)
                link(v.reciprocal(stat[:, 6:8], stat[:, 4:6]))
                for t in range(NT):
                    ins = v.scalar_tensor_tensor(out=dst[:, t], in0=src[:, t], scalar=stat[:, 6 + t:7 + t], in1=scale,
                                                 op0=ALU.mult, op1=ALU.mult)
                    if shift is not None:
                        link(ins)
                        ins = v.tensor_tensor(dst[:, t], dst[:, t], shift, ALU.add)
                    ins.then_inc(S["normed"], 1)

            def modulation(l):
                v.wait_ge(S["in_modb"], 16 * (l + 1))
                def out_part(c, ctx):
                    n = mod_part(l, c, ctx)
                    if ctx and c == 0:
                        v.wait_ge(S["in_modcb"], 16)
                    v.wait_ge(S["mod"], n + 1)
                    part = flat(modc if ctx else mod)[:, 512 * c:512 * c + 512]
                    v.tensor_tensor(part, part, bank[2 + n % 2][:, :], ALU.add).then_inc(S["mod_ev"], 1)

                for i, (c, ctx) in enumerate(MOD_PARTS[l]):
                    n = mod_part(l, c, ctx)
                    v.wait_ge(S["modp"], n + 1)
                    if i >= 2:
                        v.wait_ge(S["mod"], n - 1)
                    v.tensor_scalar(mpart[:, n % 2], bank[n % 2][:, :], 1.0 / 32, None, ALU.mult).then_inc(S["modp_ev"], 1)
                    if i:
                        out_part(*MOD_PARTS[l][i - 1])
                out_part(*MOD_PARTS[l][-1])
                v.wait_ge(S["mod_ev"], mod_part(l, 12, 0))

            def gain_into(scale, name):
                g = wait_gain(v, name)
                return v.scalar_tensor_tensor(out=scale, in0=scale, scalar=1.0, in1=g, op0=ALU.add, op1=ALU.mult)

            def top16(values, indices, scores, n):
                for r in range(n):
                    ins = v.max(values(r)[:, 0:8], scores(r))
                link(ins)
                for r in range(n):
                    ins = v.max_index(indices(r)[:, 0:8], values(r)[:, 0:8], scores(r))
                link(ins)
                for r in range(n):
                    ins = v.match_replace(scores(r), values(r)[:, 0:8], scores(r), NEG)
                link(ins)
                for r in range(n):
                    ins = v.max(values(r)[:, 8:16], scores(r))
                link(ins)
                for r in range(n):
                    ins = v.max_index(indices(r)[:, 8:16], values(r)[:, 8:16], scores(r))
                link(ins)

            def add_product(dst, products, gain, tag, done):
                for k in range(4):
                    c, t = k // 2, k % 2
                    v.wait_ge(S[tag], k + 1)
                    part = dst[:, t, 512 * c:512 * c + 512]
                    if gain is None:
                        ins = v.tensor_tensor(part, part, products[k][:, :], ALU.add)
                    else:
                        link(v.tensor_tensor(gt[:, k % 2], products[k][:, :], gain[:, 512 * c:512 * c + 512], ALU.mult))
                        ins = v.tensor_tensor(part, part, gt[:, k % 2], ALU.add)
                    if c == 1:
                        ins.then_inc(S[done], 1)
                    else:
                        link(ins)

            v.wait_ge(S["silu_c"], 1)
            v.tensor_copy(cB, bc(cols[:, 0:8], 2, 32)).then_inc(S["cB"], 1)
            v.tensor_copy(cB2, bc(cols[:, 8:16], 2, 32)).then_inc(S["cB"], 1)
            v.memset(stat[:, 16:17], 0.0).then_inc(S["up_used"], 4)
            v.memset(stat[:, 17:18], 0.0).then_inc(S["up_added"], 1)
            modulation(0)
            link(gain_into(modc[:, 1], "norm1_0"))
            link(gain_into(mod[:, 1], "norm1_0"))
            ins = gain_into(mod[:, 4], "norm2_0")
            ins.then_inc(S["gain_used"], 2)
            v.wait_ge(S["gain_used"], 2)
            norm("nctx", ctxn, h, modc[:, 1], modc[:, 0])
            v.wait_ge(S["in_x"], 16)
            v.wait_ge(S["norm_sum"], normed("n1_0", NT))
            norm("n1_0", x, h, mod[:, 1], mod[:, 0])

            v.wait_ge(S["pin1_ev"], 8)
            v.wait_ge(S["in_const"], 16)
            rope = cst("rope").rearrange("p (t f) -> p t f", t=NT)
            for t in range(NT):
                for n, src, dst in (
                        (4, proj[:, t, 0:512].rearrange("p (j a f) -> p j a f", j=2, a=4),
                         qk[:, t, 0:512].rearrange("p (a j f) -> p j a f", a=4, j=2)),
                        (1, proj[:, t, 512:640].rearrange("p (j a f) -> p j a f", j=2, a=1),
                         qk[:, t, 512:640].rearrange("p (a j f) -> p j a f", a=1, j=2))):
                    tmp = tmp1[:, 0:64 * n].rearrange("p (j a f) -> p j a f", j=2, a=n)
                    for axis in range(2):
                        x1, x2 = (src[:, :, :, 32 * axis + 16 * i:32 * axis + 16 * i + 16] for i in range(2))
                        o1, o2 = (dst[:, :, :, 32 * axis + 16 * i:32 * axis + 16 * i + 16] for i in range(2))
                        u1, u2 = tmp[:, :, :, 0:16], tmp[:, :, :, 16:32]
                        cos = bc(bc(rope[:, t, 16 * axis:16 * axis + 16], 1, n), 1, 2)
                        sin = bc(bc(rope[:, t, 32 + 16 * axis:48 + 16 * axis], 1, n), 1, 2)
                        v.tensor_tensor(u1, x2, sin, ALU.mult)
                        v.tensor_tensor(u2, x2, cos, ALU.mult)
                        v.tensor_tensor(o1, x1, cos, ALU.mult)
                        link(v.tensor_tensor(o2, x1, sin, ALU.mult))
                        v.tensor_tensor(o1, o1, u1, ALU.subtract)
                        link(v.tensor_tensor(o2, o2, u2, ALU.add))
            v.tensor_copy(stat[:, 8:9], stat[:, 6:7]).then_inc(S["rope1"], 1)

            v.wait_ge(S["gelu1"], NT)
            va = proj[:, :, 1280:1792].rearrange("p t (g d) -> p t g d", g=8)
            mu = gst[:, 0].rearrange("p (t g) -> p t g", t=NT)
            var = gst[:, 1].rearrange("p (t g) -> p t g", t=NT)
            sq = mixcat[:, 0, 0:512].rearrange("p (g d) -> p g d", g=8)
            for t in range(NT):
                link(v.tensor_reduce(mu[:, t], va[:, t], AX, ALU.add))
            link(v.tensor_scalar(gst[:, 0], gst[:, 0], 1.0 / 64, None, ALU.mult))
            for t in range(NT):
                link(v.tensor_tensor(va[:, t], va[:, t], bc(mu[:, t], 2, 64), ALU.subtract))
                link(v.tensor_tensor(sq, va[:, t], va[:, t], ALU.mult))
                link(v.tensor_reduce(var[:, t], sq, AX, ALU.add))
            v.tensor_scalar(gst[:, 1], gst[:, 1], 1.0 / 64, EPS, ALU.mult, ALU.add).then_inc(S["gmlp_v"], 1)
            v.wait_ge(S["g_rt"], 1)
            link(v.reciprocal(gst[:, 3], gst[:, 2]))
            for t in range(NT):
                v.tensor_tensor(va[:, t], va[:, t], bc(gst[:, 3, 8 * t:8 * t + 8], 2, 64), ALU.mult).then_inc(S["gmlp_v"], 1)
            bs = col("bs")
            for t in range(NT):
                v.wait_ge(S["gmlp"], t + 1)
                mg = mixcat[:, t, 512:1024].rearrange("p (g d) -> p g d", g=8)
                link(v.tensor_tensor(mg, bank[4 + t][:, :].rearrange("p (g d) -> p g d", g=8), bc(bs, 2, 64), ALU.add))
                v.tensor_tensor(mixcat[:, t, 512:1024], mixcat[:, t, 512:1024], proj[:, t, 768:1280], ALU.mult).then_inc(
                    S["mixed"], 1)

            v.wait_ge(S["in_rows"], 16)
            win = cst("win").rearrange("p (t k) -> p t k", t=NT)

            def softmax1(it):
                t, j = it // 2, it % 2
                sc1, ast = scs[it % 2], asts[it % 2]
                sink = rw("sink")[:, 4 * j:4 * j + 4]
                if it >= 2:
                    v.wait_ge(S["a_pt"], 4 * (it - 1))
                for p in range(4):
                    v.wait_ge(S["a_s"], 4 * it + p + 1)
                    v.scalar_tensor_tensor(out=sc1[:, p, 0:256], in0=bank[p][:, 0:256], scalar=0.125, in1=win[:, t],
                                           op0=ALU.mult, op1=ALU.add)
                    v.tensor_scalar(sc1[:, p, 256:512], bank[p][:, 256:512], 0.125, None, ALU.mult).then_inc(S["a_s_ev"], 1)
                v.wait_ge(S["a_s_ev"], 4 * it + 4)
                link(v.tensor_reduce(ast[:, 0], sc1, AX, ALU.max))
                link(v.tensor_tensor(ast[:, 0], ast[:, 0], sink, ALU.max))
                v.tensor_tensor(ast[:, 3], sink, ast[:, 0], ALU.subtract)
                v.tensor_scalar(ast[:, 2], ast[:, 0], -1.0, None, ALU.mult).then_inc(S["a_negm"], 1)

            def out1(it):
                t, j = it // 2, it % 2
                ast = asts[it % 2]
                v.wait_ge(S["a_exp"], 5 * it + 5)
                link(v.tensor_tensor(ast[:, 4], ast[:, 4], ast[:, 3], ALU.add))
                link(v.reciprocal(ast[:, 5], ast[:, 4]))
                v.wait_ge(S["a_pv"], 4 * it + 4)
                v.tensor_tensor(mixcat[:, t, 256 * j:256 * j + 256].rearrange("p (g d) -> p g d", g=4),
                                bank[6 + it % 2][:, 0:256].rearrange("p (g d) -> p g d", g=4),
                                bc(ast[:, 5], 2, 64), ALU.mult).then_inc(S["attn_o"], 1)

            softmax1(0)
            for it in range(4):
                if it < 3:
                    softmax1(it + 1)
                out1(it)
            v.wait_ge(S["attn_o"], 4)

            add_product(x, [bank[4 + k] for k in range(4)], mod[:, 2], "pout1", "x_mix")

            def peer(l):
                v.wait_ge(S["x_mix"], NT * (l + 1))
                norm(f"n2_{l}", x, h, mod[:, 4], mod[:, 3])
                v.wait_ge(S["ps_ev"], 8 * l + 8)

                def top_k(t):
                    top16(lambda r: v16[:, r // 2, r % 2], lambda r: i16[:, r], lambda r: s16[t][:, r], 16)
                    for hh in range(8):
                        ins = v.tensor_tensor(cand[:, hh].rearrange("p (a b) -> p a b", a=16),
                                              bc(v16[:, hh, 0], 2, 16), bc(v16[:, hh, 1], 1, 16), ALU.add)
                    link(ins)
                    top16(lambda r: bv[:, r], lambda r: bp[:, r], lambda r: cand[:, r], 8)
                    v.tensor_tensor(gate[:, t].rearrange("p (g k) -> p g k", g=8), bv, bc(bv[:, :, 0], 2, 16),
                                    ALU.subtract).then_inc(S["gate_in"], 1)
                    v.tensor_single_scalar(ab[:, 0], flat(bp), 4, ALU.logical_shift_right)
                    link(v.tensor_single_scalar(ab[:, 1], flat(bp), 15, ALU.bitwise_and))
                    v.tensor_copy(abf, ab)
                    link(v.tensor_copy(i16f.rearrange("p a b c -> p (a b c)"), flat(i16)))
                    oh = onehot[t]
                    for s in range(2):
                        link(v.tensor_tensor(oh, bc(cst("iota")[:, 0:16], 1, PICKS), bc(abf[:, s], 2, 16), ALU.is_equal))
                        link(v.tensor_tensor(oh.rearrange("p (g k) c -> p g k c", g=8),
                                             oh.rearrange("p (g k) c -> p g k c", g=8),
                                             bc(i16f[:, :, s], 2, 16), ALU.mult))
                        link(v.tensor_reduce(sel[:, s], oh, AX, ALU.add))
                    link(v.scalar_tensor_tensor(out=sel[:, 0], in0=sel[:, 0], scalar=128.0, in1=sel[:, 1],
                                                op0=ALU.mult, op1=ALU.add))
                    v.tensor_scalar(idx_all[:, t], sel[:, 0], float(l * EXPERTS), None, ALU.add).then_inc(S["idx_ready"], 1)

                def gates(t):
                    v.wait_ge(S["gate_exp"], NT * l + t + 1)
                    g3 = gate[:, t].rearrange("p (g k) -> p g k", g=8)
                    link(v.tensor_reduce(gsum[:, 0], g3, AX, ALU.add))
                    link(v.reciprocal(gsum[:, 1], gsum[:, 0]))
                    link(v.tensor_tensor(g3, g3, bc(gsum[:, 1], 2, 16), ALU.mult))

                def down(t):
                    with v.Fori(0, PICKS // GSLOTS) as i:
                        for s in range(GSLOTS):
                            v.wait_ge(S[f"gathered{s}"], i * 16 + 16 * (16 * (4 * l + 2 * t) + 1))
                            v.scalar_tensor_tensor(out=G[:, s], in0=G[:, s], scalar=1.0, in1=h[:, t], op0=ALU.mult,
                                                   op1=ALU.mult, accum_out=act[:, t, bass.ds(i * GSLOTS + s, 1)]).then_inc(
                                S["down_used"], 1)
                    v.wait_ge(S["peer_gelu"], NT * l + t + 1)
                    v.tensor_tensor(act[:, t], act[:, t], gate[:, t], ALU.mult).then_inc(S["peer_w"], 1)


                def up(t):
                    with v.Fori(ALONE[t], ROUNDS) as i:
                        v.wait_ge(S[f"gathered{GSLOTS - 1}"], i * 16 + 16 * (16 * (4 * l + 2 * t + 1) + 1))
                        v.wait_ge(S["up_added"], i + (added_before(l, t) - ALONE[t] + 1))
                        v.scalar_tensor_tensor(out=usum[:, t], in0=G[:, GSLOTS - 1],
                                               scalar=act[:, t, bass.ds(i * GSLOTS + (GSLOTS - 1), 1)], in1=usum[:, t],
                                               op0=ALU.mult, op1=ALU.add).then_inc(S["up_added"], 1)

                top_k(0)
                gates(0)
                down(0)
                top_k(1)
                v.wait_ge(S["idx_ready"], NT * l + 2)
                link(v.memset(usum, 0.0))
                v.wait_ge(S["peer_w"], NT * l + 1)
                up(0)
                gates(1)
                down(1)
                v.wait_ge(S["peer_w"], NT * l + 2)
                up(1)
                v.wait_ge(S["up_added"], added_before(l + 1, 0) + 1)
                for t in range(NT):
                    v.wait_ge(S["up_used"], 4 + PICKS * (NT * l + t + 1))
                    if t:
                        v.wait_ge(S["x_peer"], NT * l + t)
                    for c in range(2):
                        link(v.tensor_tensor(gt[:, c], bank[2 * t + c][:, :], usum[:, t, 512 * c:512 * c + 512], ALU.add))
                        link(v.tensor_tensor(gt[:, c], gt[:, c], mod[:, 5, 512 * c:512 * c + 512], ALU.mult))
                    v.tensor_tensor(x[:, t], x[:, t], gt.rearrange("p a b -> p (a b)"), ALU.add).then_inc(S["x_peer"], 1)
                v.wait_ge(S["x_peer"], NT * (l + 1))

            peer(0)
            v.tensor_copy(cB, bc(cols[:, 0:8], 2, 32)).then_inc(S["cB"], 1)
            modulation(1)
            link(gain_into(mod[:, 1], "norm1_1"))
            v.tensor_copy(stat[:, 8:9], stat[:, 6:7]).then_inc(S["gain_used"], 1)
            norm("n1_1", x, h, mod[:, 1], mod[:, 0])
            g = wait_gain(v, "pool")
            v.tensor_tensor(mod[:, 2], mod[:, 2], g, ALU.mult).then_inc(S["gain_used"], 1)
            v.wait_ge(S["gain_used"], 4)
            gain_into(mod[:, 4], "norm2_1").then_inc(S["gain_used"], 1)
            v.wait_ge(S["gain_used"], 5)
            add_product(x, [bank[k] for k in range(4)], mod[:, 2], "py_pool", "x_mix")
            peer(1)
            g = wait_gain(v, "final_1")
            norm("nf1", x, x, g)
            v.wait_ge(S["normed"], normed("nf1", NT))
            v.tensor_copy(stat[:, 8:10], stat[:, 6:8]).then_inc(S["x_block1"], NT)
            v.tensor_copy(stat[:, 10:11], stat[:, 6:7]).then_inc(S["gain_used"], 1)
            g = wait_gain(v, "mix")
            norm("nmix", x, h, g)
            v.wait_ge(S["normed"], normed("nmix", NT))
            v.tensor_copy(stat[:, 8:9], stat[:, 6:7]).then_inc(S["gain_used"], 1)

            posf = stat[:, 12:15]
            v.wait_ge(S["in_pos"], 16)
            link(v.tensor_copy(posf, posi[:, :]))
            ang = tang[:, 0:3]
            for i in range(3):
                link(v.tensor_scalar(ang[:, i], cst("inv"), posf[:, i:i + 1], None, ALU.mult))
            turns = tang[:, 3:6]
            link(v.tensor_scalar(turns, ang, float(np.float32(1 / (2 * np.pi))), 12582912.0, ALU.mult, ALU.add))
            link(v.tensor_scalar(turns, turns, -12582912.0, None, ALU.add))
            parts, rest = [], 2 * np.pi
            for bits in (7, 10):
                e = 2.0 ** (bits - 3)
                parts.append(np.floor(rest * e) / e if not parts else np.floor(rest * 2.0 ** 17) / 2.0 ** 17)
                rest -= parts[-1]
            parts.append(rest)
            for part in parts:
                link(v.scalar_tensor_tensor(out=ang, in0=turns, scalar=-float(part), in1=ang, op0=ALU.mult, op1=ALU.add))
            PI = 3.1415925
            link(v.tensor_scalar(ang, ang, PI, -PI, ALU.min, ALU.max))
            link(v.scalar_tensor_tensor(out=turns, in0=ang, scalar=-1.0, in1=ang, op0=ALU.mult, op1=ALU.max))
            v.tensor_scalar(turns, turns, -1.0, float(np.pi / 2), ALU.mult, ALU.add).then_inc(S["angles"], 1)

            def rope2(dst, src, tmp, n, row):
                np_ = src.shape[0]
                j = 2 if src.shape[1] > 64 else 1
                src = src.rearrange("p (j a f) -> p j a f", j=j, a=n)
                dst = dst.rearrange("p (a j f) -> p j a f", j=j, a=n)
                u = tmp.rearrange("p (j a f) -> p j a f", j=j, a=n)
                cos, sin = (bc(bc(trig[0:np_, row, i, :], 1, n), 1, j) for i in range(2))
                link(v.tensor_tensor(u, src[:, :, :, 32:64], sin, ALU.mult))
                link(v.tensor_tensor(dst[:, :, :, 0:32], src[:, :, :, 0:32], cos, ALU.mult))
                link(v.tensor_tensor(dst[:, :, :, 0:32], dst[:, :, :, 0:32], u, ALU.subtract))
                link(v.tensor_tensor(u, src[:, :, :, 32:64], cos, ALU.mult))
                link(v.tensor_tensor(dst[:, :, :, 32:64], src[:, :, :, 0:32], sin, ALU.mult))
                return v.tensor_tensor(dst[:, :, :, 32:64], dst[:, :, :, 32:64], u, ALU.add)

            v.wait_ge(S["pin2_ev"], 20)
            for t in range(NT):
                v.tensor_copy(kcd[:, t].rearrange("p a (b d) -> p a b d", b=2),
                              bc(z[:, t, Z_KC:Z_KS].rearrange("p (a d) -> p a d", a=4), 2, 2)).then_inc(S["kcd"], 1)
            v.wait_ge(S["trig"], 2)
            link(v.memset(X, 0.0))
            v.wait_ge(S["operands_ev"], operand("tkc", 2))
            X5 = X.rearrange("p v k (g n) -> p v k g n", g=2)
            for kv in range(2):
                pos = col("posk" if kv == 0 else "posv")
                for g in range(2):
                    raw = kdT[:, 2 * kv + g].rearrange("p (n m b) -> p m n b", m=8, b=2)
                    for b in range(2):
                        q = slice(64 * b, 64 * b + 64)
                        for half in range(2):
                            ins = v.tensor_tensor(X5[q, kv, 8 * half:8 * half + 8, g, 0:15], raw[q, :, half:half + 15, b],
                                                  bc(pos[q, 8 * half:8 * half + 8], 2, 15), ALU.add)
                            ins.then_inc(S["windows"], 1)
            for t in range(NT):
                link(rope2(qr[:, t, 0:512], z[:, t, Z_Q:Z_Q + 512], rtmp[:, 0:256], 4, t))
                link(rope2(qr[:, t, 512:640], z[:, t, Z_KS:Z_KS + 128], rtmp[:, 256:320], 1, t))
                rope2(qr[:, t, 640:768], z[:, t, Z_KW:Z_KW + 128], rtmp[:, 320:384], 1, t).then_inc(S["rope2"], 1)
            v.wait_ge(S["hid"], 2)
            b1 = rows[0:64, ROW_AT["b1k"][0]:ROW_AT["b1k"][0] + 512]
            v.tensor_tensor(flat(H1)[0:64], bank[3][0:64, :], b1, ALU.add).then_inc(S["cmp_v"], 1)
            v.wait_ge(S["cmp"], 2)
            b2k = rows[0:64, ROW_AT["b2k"][0]:ROW_AT["b2k"][0] + 64]
            b2v = rows[0:64, ROW_AT["b2v"][0]:ROW_AT["b2v"][0] + 64]
            link(v.tensor_tensor(ctmp[0:64, 0:64], bank[0][0:64, 0:64], b2k, ALU.add))
            link(rope2(kc2[0:64, 0:64], ctmp[0:64, 0:64], ctmp[0:64, 64:96], 1, 2))
            v.tensor_copy(kc2[0:64, 64:128], kc2[0:64, 0:64]).then_inc(S["cmp_v"], 1)
            v.memset(kcT, 0.0).then_inc(S["cmp_v"], 1)
            link(v.memset(vcz, 0.0))
            for g in range(2):
                q = slice(32 * g, 32 * g + 32)
                v.tensor_tensor(vcz[q, g], bank[1][q, 0:64], rows[q, ROW_AT["b2v"][0]:ROW_AT["b2v"][0] + 64],
                                ALU.add).then_inc(S["cmp_v"], 1)
            cmpmask = cst("cmpmask").rearrange("p (t n) -> p t n", t=NT)
            cmpok = cst("cmpok").rearrange("p (t n) -> p t n", t=NT)
            causal = cst("causal").rearrange("p (t n) -> p t n", t=NT)
            v.wait_ge(S["z_acts"], 1)
            v.wait_ge(S["operands_ev"], operand("tq2", 4))
            for t in range(NT):
                v.wait_ge(S["c_s"], t + 1)
                if t:
                    v.wait_ge(S["c_pt"], t)
                pc4 = pcm.rearrange("p a (j n) -> p a j n", j=2)
                for p in range(4):
                    ins = v.scalar_tensor_tensor(
                        out=pc4[:, p], in0=bank[5][:, 64 * p:64 * p + 64].rearrange("p (j n) -> p j n", j=2),
                        scalar=0.125, in1=bc(cmpmask[:, t], 1, 2), op0=ALU.mult, op1=ALU.add)
                link(ins)
                c8 = cmp_stats.rearrange("p a b -> p (a b)")
                link(v.tensor_reduce(c8[:, 0:8], flat(pcm).rearrange("p (a n) -> p a n", a=8), AX, ALU.max))
                p8 = flat(pcm).rearrange("p (a n) -> p a n", a=8)
                v.tensor_tensor(p8, p8, bc(c8[:, 0:8], 2, 32), ALU.subtract).then_inc(S["c_sub"], 1)
                v.wait_ge(S["c_exp"], t + 1)
                link(v.tensor_reduce(c8[:, 8:16], p8, AX, ALU.add))
                link(v.reciprocal(c8[:, 16:24], c8[:, 8:16]))
                gs3 = gsig[:, t].rearrange("p (j a b) -> p a j b", j=2, a=4)
                link(v.tensor_tensor(c8[:, 16:24].rearrange("p (a j) -> p a j", a=4),
                                     c8[:, 16:24].rearrange("p (a j) -> p a j", a=4), gs3[:, :, :, 0], ALU.mult))
                link(v.tensor_tensor(p8, p8, bc(c8[:, 16:24], 2, 32), ALU.mult))
                v.tensor_tensor(p8, p8, bc(cmpok[:, t], 1, 8), ALU.mult).then_inc(S["c_p"], 1)
                for j in range(2):
                    it = 2 * t + j
                    psc = pscs[j]
                    if it >= 2:
                        v.wait_ge(S["b_pt"], 4 * (it - 1))
                    for p in range(4):
                        v.wait_ge(S["b_s"], 4 * it + p + 1)
                        v.scalar_tensor_tensor(out=psc[:, 2 * p:2 * p + 2], in0=bank[p][:, :].rearrange("p (a k) -> p a k", a=2),
                                               scalar=0.125, in1=bc(causal[:, t], 1, 2), op0=ALU.mult,
                                               op1=ALU.add).then_inc(S["b_s_ev"], 1)
                    v.wait_ge(S["b_s_ev"], 4 * it + 4)
                    link(v.tensor_reduce(nst[:, 0], psc, AX, ALU.max))
                    v.tensor_scalar(nst[:, 1], nst[:, 0], -1.0, None, ALU.mult).then_inc(S["b_negm"], 1)
                    v.wait_ge(S["b_exp"], 8 * it + 8)
                    link(v.reciprocal(nst[:, 3], nst[:, 2]))
                    gs = gsig[:, t, 12 * j:12 * j + 12].rearrange("p (a b) -> p a b", a=4)[:, :, 1:3]
                    n3 = nst[:, 3].rearrange("p (a b) -> p a b", a=4)
                    link(v.tensor_tensor(n3, n3, gs, ALU.mult))
                    v.tensor_tensor(psc, psc, bc(nst[:, 3], 2, T), ALU.mult).then_inc(S["b_p"], 1)
            v.wait_ge(S["z_acts"], 1 + NT)
            for c in range(2):
                for t in range(NT):
                    v.wait_ge(S["branch"], 2 * c + t + 1)
                    v.tensor_tensor(zx[:, t, 512 * c:512 * c + 512], bank[4 + 2 * c + t][:, :],
                                    z[:, t, Z_MA + 512 * c:Z_MA + 512 * c + 512], ALU.mult).then_inc(S["ya"], 1)

            v.wait_ge(S["operands_ev"], operand("tgla", 3))
            v.wait_ge(S["gla_x"], 1)
            ba = col("b_a")
            for q in range(2):
                link(v.tensor_scalar(gt1[:, q], bank[3][:, 256 * q:256 * q + 256], ba[:, q:q + 1], None, ALU.add))
            v.scalar_tensor_tensor(out=gt2, in0=gt1, scalar=-1.0, in1=gt1, op0=ALU.mult, op1=ALU.max).then_inc(S["gla_v"], 1)
            v.wait_ge(S["gla_a"], 2)
            link(v.scalar_tensor_tensor(out=gt1, in0=gt1, scalar=0.0, in1=gt2, op0=ALU.min, op1=ALU.subtract))
            link(v.tensor_scalar(gt1, gt1, 1.0 / 16, None, ALU.mult))
            for q in range(2):
                ins = v.tensor_tensor_scan(bb[:, q], cst("reset"), gt1[:, q], 0.0, ALU.mult, ALU.add)
            ins.then_inc(S["gla_v"], 1)
            v.wait_ge(S["gla_v"], 2)
            b4 = bb.rearrange("p a (c s) -> p a c s", s=64)
            last = b4[:, :, :, 63]
            for q in range(2):
                ins = v.tensor_tensor(gt2[:, q].rearrange("p (c s) -> p c s", s=64), bc(last[:, q], 2, 64), b4[:, q], ALU.subtract)
            ins.then_inc(S["gla_v"], 1)
            link(v.tensor_scalar(gqT, gqT, 0.125, None, ALU.mult))
            v.memset(QM, 0.0)
            v.memset(st, 0.0)
            link(v.memset(QZ, 0.0))
            QM6 = QM.rearrange("p q t (u c g) -> p q t u c g", c=2, g=2)
            for q in range(2):
                for t in range(NT):
                    for g in range(2):
                        pp = slice(64 * g, 64 * g + 64)
                        v.tensor_copy(QM6[pp, q, t, :, :, g],
                                      gqT[pp, q, P * t:P * t + P].rearrange("p (c u) -> p u c", c=2)).then_inc(S["qm"], 1)
            v.wait_ge(S["gla_a"], 4)
            for q in range(2):
                for c in range(4):
                    o = 64 * (c % 2)
                    v.tensor_tensor(QZ[:, q, c, o:o + 64], gqT[:, q, 64 * c:64 * c + 64], gt1[:, q, 64 * c:64 * c + 64],
                                    ALU.mult).then_inc(S["qz"], 1)
            v.wait_ge(S["gla_a"], 5)
            v.tensor_tensor(gt2, gt2, gkT, ALU.mult).then_inc(S["gla_v"], 1)

            def ek_mult(k):
                q, t = k // 8, (k // 4) % 2
                e4 = Ek[k % 2].rearrange("p (u c s) -> p u c s", u=16, c=2)
                v.wait_ge(S["ek_exp"], k + 1)
                v.scalar_tensor_tensor(out=e4, in0=e4, scalar=1.0, in1=bc(
                    gkT[:, q, P * t:P * t + P].rearrange("p (c s) -> p c s", c=2), 1, 16), op0=ALU.min,
                    op1=ALU.mult).then_inc(S["ek_ready"], 1)

            for k in range(16):
                q, t, u = k // 8, (k // 4) % 2, k % 4
                e4 = Ek[k % 2].rearrange("p (u c s) -> p u c s", u=16, c=2)
                bt = bb[:, q, P * t:P * t + P].rearrange("p (c u) -> p u c", c=2)[:, 16 * u:16 * u + 16]
                bs_ = bb[:, q, P * t:P * t + P].rearrange("p (c s) -> p c s", c=2)
                if k >= 2:
                    ek_mult(k - 1)
                    v.wait_ge(S["attn_gla"], k - 1)
                v.tensor_tensor(e4, bc(bt, 3, 64), bc(bs_, 1, 16), ALU.subtract).then_inc(S["ek_sub"], 1)
                if k == 1:
                    ek_mult(0)
            ek_mult(15)
            for c in range(1, 4):
                for q in range(2):
                    v.wait_ge(S["state"], 2 * (c - 1) + q + 1)
                    for g in range(2):
                        pp = slice(64 * g, 64 * g + 64)
                        ee = slice(P * g, P * g + P)
                        upd = bank[4 + q][pp, ee]
                        if c == 1:
                            v.tensor_copy(st[pp, c, q, ee], upd).then_inc(S["st"], 1)
                        else:
                            v.scalar_tensor_tensor(out=st[pp, c, q, ee], in0=st[pp, c - 1, q, ee],
                                                   scalar=gel[pp, 4 * q + c - 1:4 * q + c], in1=upd,
                                                   op0=ALU.mult, op1=ALU.add).then_inc(S["st"], 1)
                v.wait_ge(S["st"], 4 * c)
            glamask = cst("glamask").rearrange("p (c u) -> p c u", c=2)
            for t in range(NT):
                if t:
                    v.wait_ge(S["gla_o"], 1)
                for hd in range(4):
                    q, g = hd // 2, hd % 2
                    A = bank[6 + q][:, 256 * t:256 * t + 256].rearrange("p (u c g) -> p c u g", c=2, g=2)[:, :, :, g]
                    v.wait_ge(S["attn_gla"], 8 * q + 4 * t + 4)
                    v.tensor_tensor(AT[:, hd].rearrange("p (c u) -> p c u", c=2), A, glamask, ALU.mult).then_inc(S["AT"], 1)
            for t in range(NT):
                v.wait_ge(S["gla_o"], t + 1)
                v.tensor_copy(zcat[:, t], bank[t][:, :]).then_inc(S["go"], 1)
            v.wait_ge(S["go"], NT)
            go8 = zcat.rearrange("p t (g e) -> p (t g) e", g=4)
            sq = Ek[0].rearrange("p (a b) -> p a b", a=16)[:, 0:8]
            link(v.tensor_tensor(sq, go8, go8, ALU.mult))
            link(v.tensor_reduce(gso, sq, AX, ALU.add))
            v.tensor_scalar(gso, gso, 1.0 / 128, EPS, ALU.mult, ALU.add).then_inc(S["go_v"], 1)
            v.wait_ge(S["go_rt"], 1)
            link(v.reciprocal(gso, gso))
            link(v.tensor_tensor(go8, go8, bc(gso, 2, P), ALU.mult))
            link(v.tensor_tensor(zcat, zcat, bc(rw("glag"), 1, NT), ALU.mult))
            v.wait_ge(S["z_acts"], 4)
            v.tensor_tensor(zcat, zcat, z[:, :, Z_GR:Z_MA], ALU.mult).then_inc(S["go_v"], 1)
            for c in range(2):
                for t in range(NT):
                    v.wait_ge(S["branch"], 4 + 2 * c + t + 1)
                    mb = z[:, t, Z_MB + 512 * c:Z_MB + 512 * c + 512]
                    link(v.tensor_tensor(mb, bank[4 + 2 * c + t][:, :], mb, ALU.mult))
                    v.tensor_tensor(zy[:, t, 512 * c:512 * c + 512], zx[:, t, 512 * c:512 * c + 512], mb,
                                    ALU.add).then_inc(S["zy"], 1)
            add_product(x, [bank[4 + k] for k in range(4)], None, "pout2", "x_mix")
            v.wait_ge(S["x_mix"], NT * 3)
            def dense_moe():
                v.tensor_copy(stat[:, 8:9], stat[:, 6:7]).then_inc(S["hdn_made"], 2)
                with v.Fori(0, 16) as e:
                    for k in range(2):
                        for f in range(4):
                            v.wait_ge(S["sg_made"], e * 8 + (4 * k + f + 1))
                            v.wait_ge(S["moe_u"], e * 8 + (4 * k + f + 1))
                            v.tensor_tensor(hdn[:, f], sg[:, f % 2], bank[2 + f % 2][:, 0:T], ALU.mult).then_inc(S["hdn_made"], 1)
                        for i in range(4):
                            t, c = i // 2, i % 2
                            v.wait_ge(S["moe_y"], e * 8 + (4 * k + i + 1))
                            part = x[:, t, 512 * c:512 * c + 512]
                            v.scalar_tensor_tensor(out=part, in0=bank[4 + i][:, :], scalar=cmb[:, t].rearrange("p (a b) -> p b a", b=2)[:, k, bass.ds(e, 1)], in1=part,
                                                   op0=ALU.mult, op1=ALU.add).then_inc(S["moe_added"], 1)
                v.wait_ge(S["moe_added"], 4 + 128)

            g = wait_gain(v, "ffn")
            norm("nffn", x, h, g)
            v.wait_ge(S["normed"], normed("nffn", NT))
            v.tensor_copy(stat[:, 8:9], stat[:, 6:7]).then_inc(S["gain_used"], 1)
            v.wait_ge(S["router"], NT)
            for t in range(NT):
                m = lambda r, n: mst[:, r, 0:n]
                link(v.tensor_tensor(m(0, 36), bank[4 + t][:, 0:36], rw("brt"), ALU.add))
                link(v.memset(m(2, 8), NEG))
                link(v.tensor_copy(m(2, 4), m(0, 4)))
                link(v.max(m(3, 8), m(2, 8)))
                link(v.max_index(m(4, 8).bitcast(U32), m(3, 8), m(2, 8)))
                link(v.tensor_copy(m(9, 8), m(4, 8).bitcast(U32)))
                link(v.tensor_scalar(m(10, 4), cst("iota")[:, 0:4], m(9, 1), None, ALU.is_equal))
                link(v.tensor_scalar(m(11, 8), mst[:, 0, 4:12], m(10, 1), None, ALU.mult))
                for g in range(1, 4):
                    link(v.scalar_tensor_tensor(out=m(11, 8), in0=mst[:, 0, 4 + 8 * g:12 + 8 * g], scalar=mst[:, 10, g:g + 1],
                                                in1=m(11, 8), op0=ALU.mult, op1=ALU.add))
                link(v.max(m(12, 8), m(11, 8)))
                link(v.max_index(m(13, 8).bitcast(U32), m(12, 8), m(11, 8)))
                link(v.tensor_copy(m(14, 8), m(13, 8).bitcast(U32)))
                if t:
                    v.wait_ge(S["r_exp"], t)
                v.tensor_scalar(m(5, 4), m(0, 4), m(3, 1), None, ALU.subtract)
                v.tensor_tensor(mst[:, 5, 4:5], mst[:, 12, 1:2], mst[:, 12, 0:1], ALU.subtract).then_inc(S["r_sub"], 1)
                v.wait_ge(S["r_exp"], t + 1)
                link(v.tensor_reduce(m(7, 1), m(6, 4), AX, ALU.add))
                link(v.scalar_tensor_tensor(out=m(8, 1), in0=mst[:, 6, 4:5], scalar=1.0, in1=m(7, 1), op0=ALU.add,
                                            op1=ALU.mult))
                link(v.reciprocal(m(15, 1), m(8, 1)))
                link(v.tensor_tensor(mst[:, 15, 1:2], m(15, 1), mst[:, 6, 4:5], ALU.mult))
                link(v.tensor_copy(wts[:, t], mst[:, 15, 0:2]))
                for n in range(2):
                    link(v.tensor_scalar(m(1, 8), cst("iota")[:, 0:8], mst[:, 14, n:n + 1], None, ALU.is_equal))
                    for g in range(4):
                        ins = v.tensor_scalar(pick[:, t, n, 8 * g:8 * g + 8], m(1, 8), mst[:, 10, g:g + 1], None, ALU.mult)
                    link(ins)
                v.tensor_tensor(chosen[:, t], pick[:, t, 0], pick[:, t, 1], ALU.add).then_inc(S["chosen"], 1)
                link(v.tensor_scalar(cmb[:, t], pick[:, t, 0], wts[:, t, 0:1], None, ALU.mult))
                link(v.scalar_tensor_tensor(out=cmb[:, t], in0=pick[:, t, 1], scalar=wts[:, t, 1:2], in1=cmb[:, t],
                                            op0=ALU.mult, op1=ALU.add))
            link(v.memset(place, 1000.0))
            v.wait_ge(S["placed"], 3)
            for t in range(NT):
                pl = place[:, t, 0:32]
                link(v.tensor_scalar(pl, bank[6 + t][:, 0:32], 1000.0, None, ALU.add))
                link(v.scalar_tensor_tensor(out=pl, in0=chosen[:, t], scalar=-1000.0, in1=pl, op0=ALU.mult, op1=ALU.add))
                row = ptmp[:, t, 0]
                link(v.scalar_tensor_tensor(out=row, in0=cst("iota")[:, 0:32], scalar=2.0 * CAP, in1=pl, op0=ALU.mult,
                                            op1=ALU.add))
                for n in range(2):
                    link(v.tensor_tensor(ptmp[:, t, 1], row, pick[:, t, n], ALU.mult))
                    link(v.tensor_reduce(prow[:, 2 * t + n:2 * t + n + 1], ptmp[:, t, 1], AX, ALU.add))
            link(v.tensor_copy(pidx[:, :, 0], prow))
            link(v.tensor_scalar(prow, prow, float(CAP), None, ALU.add))
            link(v.tensor_copy(pidx[:, :, 1], prow))
            link(v.tensor_reduce(prow[:, 0:1], bank[3][:, 0:32], AX, ALU.max))
            v.tensor_scalar(crowd, prow[:, 0:1], float(CAP), None, ALU.is_gt).then_inc(S["crowd"], 1)
            v.wait_ge(S["crowd"], 1)

            def select(n):
                for k in range(2):
                    for t in range(NT):
                        ins = v.tensor_scalar(msel[:, t, CAP * k:CAP * k + CAP], cst("iota"),
                                              place[:, t].rearrange("p (a b) -> p b a", b=2)[:, k, bass.ds(n, 1)],
                                              None, ALU.is_equal)
                ins.then_inc(S["selected"], 1)

            v.tensor_copy(stat[:, 9:10], stat[:, 6:7]).then_inc(S["moe_added"], 4)
            crowded = v.value_load(crowd[0:1, 0:1], min_val=0, max_val=1)
            with v.If(crowded == 0):
                select(0)
                with v.Fori(0, 16) as i:
                    for k in range(2):
                        v.wait_ge(S["sg_made"], i * 2 + (k + 1))
                        v.tensor_tensor(hsel[:, k].rearrange("p f c -> p (f c)"), sg[:, k], bank[2 + k][:, 256:512],
                                        ALU.mult).then_inc(S["hdn_made"], 1)
                        if k == 0:
                            select(i + 1)
                for n in range(4):
                    t = n // 2
                    v.wait_ge(S[f"gathered{n}"], 16 * (PICKS * 8 // GSLOTS + 2))
                    if n % 2:
                        v.wait_ge(S["brought"], n)
                    v.scalar_tensor_tensor(out=x[:, t], in0=yback[:, n], scalar=wts[:, t, n % 2:n % 2 + 1], in1=x[:, t],
                                           op0=ALU.mult, op1=ALU.add).then_inc(S["brought"], 1)
                v.wait_ge(S["brought"], 4)
            with v.Else():
                dense_moe()
            v.tensor_copy(stat[:, 8:9], stat[:, 6:7]).then_inc(S["x_moe"], 1)
            g = wait_gain(v, "final_2")
            norm("nf2", x, h, g)
            v.wait_ge(S["normed"], normed("nf2", NT))
            v.tensor_copy(stat[:, 8:9], stat[:, 6:7]).then_inc(S["out_ready"], NT)

        @block.tensor
        def _(pe):
            def bc(ap, axis, n):
                ap = ap.unsqueeze(axis)
                shape = list(ap.shape)
                shape[axis] = n
                return ap.to_broadcast(shape)

            def accumulate(dst, pairs):
                for i, (lhsT, rhs) in enumerate(pairs):
                    ins = pe.matmul(dst, lhsT, rhs, start=i == 0, stop=i == len(pairs) - 1)
                return ins

            def tile(ap, t):
                return ap[:, P * t:P * t + P]

            def transposes(tag, src, ready, per=1):
                for g in range(4):
                    t, half = g // 2, g % 2
                    if ready in NORMS:
                        pe.wait_ge(S["normed"], normed(ready, t + 1))
                    else:
                        pe.wait_ge(S[ready], per * (t + 1))
                    for q in range(4):
                        k = 4 * half + q
                        ins = pe.transpose(bank[g][:, P * q:P * q + P], src[:, t, P * k:P * k + P], ident)
                    ins.then_inc(S["turned"], 1)

            def project(tag, first, widths, ready):
                pe.wait_ge(S["turned_ev"], turned(ready, 4))
                for k in range(2 * len(widths)):
                    c, t = k // 2, k % 2
                    if k % 2 == 0:
                        wait_weight(pe, first + c)
                    if k >= 4:
                        pe.wait_ge(S[tag + "_ev"], k - 3)
                    w = slot(first + c)
                    accumulate(bank[4 + k % 4][:, 0:widths[c]], [(tile(hT[:, i], t), w[:, i]) for i in range(KT)]).then_inc(
                        S[tag], 1)

            def modulation(l):
                pe.wait_ge(S["cB"], 2 + l)

                def total(c, ctx):
                    n = mod_part(l, c, ctx)
                    pe.wait_ge(S["modp_ev"], n + 1)
                    if n >= 2:
                        pe.wait_ge(S["mod_ev"], n - 1)
                    pe.matmul(bank[2 + n % 2][:, :], ones, mpart[:, n % 2], start=True, stop=True).then_inc(S["mod"], 1)

                for i, (c, ctx) in enumerate(MOD_PARTS[l]):
                    n = mod_part(l, c, ctx)
                    wait_weight(pe, wat[f"mod{l}"] + c)
                    if n >= 2:
                        pe.wait_ge(S["modp_ev"], n - 1)
                    w = slot(wat[f"mod{l}"] + c)
                    for k in range(2):
                        for j in range(4):
                            ins = pe.matmul(bank[n % 2][32 * j:32 * j + 32, :], (cB2 if ctx else cB)[:, 2 * j + k],
                                            w[:, 2 * j + k], start=k == 0, stop=k == 1, skip_group_check=True)
                    ins.then_inc(S["modp"], 1)
                    if i:
                        total(*MOD_PARTS[l][i - 1])
                total(*MOD_PARTS[l][-1])

            pe.wait_ge(S["in_const"], 16)
            modulation(0)
            pe.wait_ge(S["in_const"], 16)
            transposes("tctx", h, "nctx")
            pe.wait_ge(S["turned_ev"], turned("tctx", 4))
            wait_weight(pe, wat["in1"])
            for t in range(NT):
                accumulate(bank[4 + t][:, 0:256], [(tile(hT[:, i], t), slot(wat["in1"])[:, i, 0:256]) for i in range(KT)]).then_inc(
                    S["operands"], 1)
            transposes("t1_0", h, "n1_0")
            pe.wait_ge(S["operands_ev"], operand("pctx", NT))
            project("pin1", wat["in1"], [n for _, n in INC], "t1_0")
            pe.wait_ge(S["rope1"], 1)
            for t in range(NT):
                for p in range(4):
                    ins = pe.transpose(tile(bank[t], p), tile(qk[:, t], p), ident)
                ins.then_inc(S["operands"], 1)
            for t in range(NT):
                pe.transpose(tile(bank[2], t), qk[:, t, 512:640], ident)
                ins = pe.transpose(tile(bank[2], 2 + t), kvc[:, t, 0:128], ident)
            ins.then_inc(S["operands"], 1)
            for t in range(NT):
                pe.wait_ge(S["gmlp_v"], 1 + t + 1)
                pe.wait_ge(S["pin1_ev"], 8)
                for g in range(8):
                    ins = pe.matmul(bank[4 + t][:, 64 * g:64 * g + 64], wsT[:, g], proj[:, t, 1280 + 64 * g:1344 + 64 * g],
                                    start=True, stop=True)
                ins.then_inc(S["gmlp"], 1)

            def scores1(it):
                t, j = it // 2, it % 2
                for p in range(4):
                    if it:
                        pe.wait_ge(S["a_s_ev"], 4 * (it - 1) + p + 1)
                    pe.matmul(bank[p][:, :], tile(qT[64 * j:64 * j + 64, p], t), kT[64 * j:64 * j + 64, :],
                              start=True, stop=True).then_inc(S["a_s"], 1)

            pe.wait_ge(S["operands_ev"], operand("tq1", 3))
            scores1(0)

            def turn1(k):
                it, p = k // 4, k % 4
                pe.wait_ge(S["a_exp"], 5 * it + p + 1)
                if k >= 2:
                    pe.wait_ge(S["a_pt_ev"], k - 1)
                else:
                    pe.wait_ge(S["mixed"], NT)
                for b in range(4):
                    ins = pe.transpose(tile(bank[4 + k % 2], b), tile(scs[it % 2][:, p], b), ident)
                ins.then_inc(S["a_pt"], 1)

            for it in range(4):
                t, j = it // 2, it % 2
                if it < 3:
                    scores1(it + 1)
                turn1(4 * it)
                for p in range(4):
                    k = 4 * it + p
                    if p < 3:
                        turn1(k + 1)
                    pe.wait_ge(S["a_pt_ev"], k + 1)
                    if it >= 2:
                        pe.wait_ge(S["attn_o"], it - 1)
                    vals = [proj[:, b, 640 + 64 * j:704 + 64 * j] for b in range(NT)]
                    vals += [kvc[:, b, 128 + 64 * j:192 + 64 * j] for b in range(NT)]
                    accumulate(bank[6 + it % 2][:, 64 * p:64 * p + 64], [(pT[:, k % 2, b], vals[b]) for b in range(4)]).then_inc(
                        S["a_pv"], 1)
            pe.wait_ge(S["a_s_ev"], 16)
            pe.wait_ge(S["mixed"], NT)
            transposes("tcat", mixcat, "attn_o", per=2)
            pe.wait_ge(S["attn_o"], 4)
            project("pout1", wat["out1"], [512, 512], "tcat")

            def peer(l):
                transposes(f"t2_{l}", h, f"n2_{l}")
                pe.wait_ge(S["turned_ev"], turned(f"t2_{l}", 4))
                for k in range(16):
                    i = wat[f"wq{l}"] + k // 4
                    if k % 4 == 0:
                        wait_weight(pe, i)
                    if k >= 4:
                        pe.wait_ge(S["pq_ev"], 16 * l + k - 3)
                    accumulate(bank[4 + k % 4][:, 0:T], [(tile(slot(i)[:, q], k % 4), hT[:, q]) for q in range(KT)]).then_inc(
                        S["pq"], 1)
                pe.wait_ge(S["pq_ev"], 16 * l + 16)
                for k in range(8):
                    t = k // 4
                    if k >= 4:
                        pe.wait_ge(S["ps_ev"], 8 * l + k - 3)
                    for q in range(4):
                        r = 4 * (k % 4) + q
                        ins = pe.matmul(tile(bank[k % 4], q), tile(q16[:, r], t), keysT[:, l, r % 2], start=True, stop=True)
                    ins.then_inc(S["ps"], 1)
                pe.wait_ge(S["ps_ev"], 8 * l + 8)
                for t in range(NT):
                    n0 = diagonals(l, t)

                    def pick(i, s, start, stop, shared=0):
                        pe.wait_ge(S[f"gathered{s}"], i * 16 + 16 * (16 * (4 * l + 2 * t + 1) + 1))
                        n = GSLOTS - shared
                        pe.wait_ge(S["diag_made"], i * n + (n0 + ALONE[t] * shared + s + 1))
                        for c in range(2):
                            ins = pe.matmul(bank[2 * t + c][:, :], diag[:, s % 4], G[:, s, 512 * c:512 * c + 512],
                                            start=start, stop=stop, skip_group_check=True)
                        ins.then_inc(S["up_used"], 1 + (shared and s == n - 1))

                    for s in range(GSLOTS):
                        pick(0, s, s == 0, False)
                    if ALONE[t] > 1:
                        with pe.Fori(1, ALONE[t]) as i:
                            for s in range(GSLOTS):
                                pick(i, s, False, False)
                    last = ROUNDS - 1
                    with pe.Fori(ALONE[t], last) as i:
                        for s in range(GSLOTS - 1):
                            pick(i, s, False, False, 1)
                    for s in range(GSLOTS - 1):
                        pick(last, s, False, s == GSLOTS - 2, 1)

            peer(0)
            modulation(1)
            for k in range(8):
                pe.wait_ge(S["normed"], normed("n1_1", NT))
                if k >= 4:
                    pe.wait_ge(S["operands_ev"], operand("ppool", k - 3))
                accumulate(bank[4 + k % 4][:, 0:T], [(tile(h[:, i], k), band[:, i, k // 2]) for i in range(NT)]).then_inc(
                    S["operands"], 1)
            pe.wait_ge(S["operands_ev"], operand("ppool", 8))
            wait_weight(pe, wat["pool"])
            for k in range(4):
                c, t = k // 2, k % 2
                for g in (2 * c, 2 * c + 1):
                    ins = accumulate(bank[k][:, 256 * (g % 2):256 * (g % 2) + 256],
                                     [(tile(hT[:, 2 * g + i], t), slot(wat["pool"])[:, 2 * g + i]) for i in range(2)])
                ins.then_inc(S["py_pool"], 1)
            peer(1)
            transposes("tmix", h, "nmix")
            project("pin2", wat["in2"], [n for _, n in ZC], "tmix")
            pe.wait_ge(S["pin2_ev"], 20)
            for kv in range(2):
                for g in range(2):
                    for t in range(NT):
                        pe.wait_ge(S["kcd"], t + 1)
                        ins = pe.transpose(tile(bank[kv], 2 * g + t), kcd[:, t, 2 * kv + g], ident)
                ins.then_inc(S["operands"], 1)
            pe.wait_ge(S["windows"], 16)
            for kv in range(2):
                i = wat["w1k"] + kv
                wait_weight(pe, i)
                accumulate(bank[3][0:64, 256 * kv:256 * kv + 256], [(X[:, kv, k], slot(i)[:, k]) for k in range(16)]).then_inc(
                    S["hid"], 1)
            pe.wait_ge(S["h1_gelu"], 1)
            for kv in range(2):
                for k in range(2):
                    q = 2 * kv + k
                    ins = pe.transpose(bank[2][:, 64 * q:64 * q + 64], H1[0:64, kv, P * k:P * k + P], ident[0:64, 0:64])
            ins.then_inc(S["operands"], 1)
            pe.wait_ge(S["operands_ev"], operand("th1", 1))
            for kv in range(2):
                w2 = col("w2k" if kv == 0 else "w2v").rearrange("p (k n) -> p k n", k=2)
                accumulate(bank[kv][0:64, 0:64], [(H1T[:, kv, k], w2[:, k]) for k in range(2)]).then_inc(S["cmp"], 1)
            for t in range(NT):
                pe.wait_ge(S["rope2"], t + 1)
                for p in range(4):
                    ins = pe.transpose(tile(bank[4 + t], p), tile(qr[:, t], p), ident)
                ins.then_inc(S["operands"], 1)
            for t in range(NT):
                pe.transpose(tile(bank[6], t), qr[:, t, 512:640], ident)
                ins = pe.transpose(tile(bank[6], 2 + t), qr[:, t, 640:768], ident)
            ins.then_inc(S["operands"], 1)
            pe.wait_ge(S["cmp_v"], 2)
            pe.transpose(bank[7][:, 0:64], kc2[0:64, 0:128], ident[0:64, 0:64]).then_inc(S["operands"], 1)

            def scores2(it):
                t, j = it // 2, it % 2
                for p in range(4):
                    if it:
                        pe.wait_ge(S["b_s_ev"], 4 * (it - 1) + p + 1)
                    pe.matmul(bank[p][:, :], tile(nqT[64 * j:64 * j + 64, p], t), kswT[64 * j:64 * j + 64, :],
                              start=True, stop=True).then_inc(S["b_s"], 1)

            pe.wait_ge(S["operands_ev"], operand("tq2", 4))
            pe.wait_ge(S["cmp_v"], 5)
            for t in range(NT):
                if t:
                    pe.wait_ge(S["b_pt_ev"], 8)
                for p in range(4):
                    ins = pe.matmul(bank[5][:, 64 * p:64 * p + 64], tile(nqT[:, p], t), kcT, start=True, stop=True)
                ins.then_inc(S["c_s"], 1)
                scores2(2 * t)
                pe.wait_ge(S["c_p"], t + 1)
                for p in range(4):
                    ins = pe.transpose(bank[6][0:64, P * p:P * p + P], pcm[:, p], ident)
                ins.then_inc(S["c_pt"], 1)
                scores2(2 * t + 1)
                blocks = [(br, b) for br in range(2) for b in range(t + 1)]

                def turn2(it, p):
                    k = 4 * it + p
                    pe.wait_ge(S["b_p"], it + 1)
                    if k >= 2:
                        pe.wait_ge(S["b_pt_ev"], k - 1)
                    for n, (br, b) in enumerate(blocks):
                        ins = pe.transpose(tile(bank[4 + k % 2], n), tile(pscs[it % 2][:, 2 * p + br], b), ident)
                    ins.then_inc(S["b_pt"], 1)

                for it in (2 * t, 2 * t + 1):
                    j = it % 2
                    turn2(it, 0)
                    for p in range(4):
                        k = 4 * it + p
                        if p < 3:
                            turn2(it, p + 1)
                        pe.wait_ge(S["b_pt_ev"], k + 1)
                        pe.wait_ge(S["c_pt_ev"], t + 1)
                        if t:
                            pe.wait_ge(S["nsa_o"], 1)
                        pairs = [(pcT[0:64, p], vcz[0:64, j])]
                        for n, (br, b) in enumerate(blocks):
                            a0 = (Z_VS, Z_VW)[br] + 64 * j
                            pairs.append((npT[k % 2][:, n], z[:, b, a0:a0 + 64]))
                        hd = 4 * j + p
                        accumulate(bank[7][:, 64 * hd:64 * hd + 64], pairs).then_inc(S["b_pv"], 1)
            pe.wait_ge(S["b_s_ev"], 16)
            for t in range(NT):
                pe.wait_ge(S["nsa_o"], t + 1)
                for k in range(4):
                    ins = pe.transpose(tile(bank[t], k), tile(zcat[:, t], k), ident)
                ins.then_inc(S["operands"], 1)

            def project4(weight, ready):
                i = wat[weight]
                wait_weight(pe, i)
                pe.wait_ge(S["operands_ev"], operand(ready, NT))
                for k in range(4):
                    c, t = k // 2, k % 2
                    accumulate(bank[4 + k][:, :], [(tile(zT[:, q], t), slot(i)[:, q, 512 * c:512 * c + 512]) for q in range(4)]
                               ).then_inc(S["branch"], 1)

            project4("nsa", "tnsa")
            for n, (c0, width) in enumerate(((Z_GQ, 128), (Z_GK, 128), (Z_GA, 16))):
                for q in range(2 if n < 2 else 1):
                    for t in range(NT):
                        ins = pe.transpose(bank[n][0:width, 256 * q + P * t:256 * q + P * t + P],
                                           z[:, t, c0 + P * q:c0 + P * q + width], ident)
                ins.then_inc(S["operands"], 1)
            pe.wait_ge(S["operands_ev"], operand("tgla", 3))
            for q in range(2):
                ins = pe.matmul(bank[3][:, 256 * q:256 * q + 256], tile(col("wa2")[0:16], q), gaT[0:16, :], start=True, stop=True)
            ins.then_inc(S["gla_x"], 1)
            pe.wait_ge(S["gla_v"], 4)
            for q in range(2):
                for t in range(NT):
                    ins = pe.transpose(tile(bank[q], t), tile(gt2[:, q], t), ident)
                ins.then_inc(S["operands"], 1)
            pe.wait_ge(S["ya"], 4)
            pe.wait_ge(S["qm"], 8)
            for k in range(16):
                q, t, u = k // 8, (k // 4) % 2, k % 4
                pe.wait_ge(S["ek_ready"], k + 1)
                for i in range(16):
                    n = 16 * u + i
                    ins = pe.matmul(bank[6 + q][:, 256 * t + 4 * n:256 * t + 4 * n + 4], tile(Ek[k % 2], i),
                                    QM[:, q, t, 4 * n:4 * n + 4], start=True, stop=True)
                ins.then_inc(S["attn_gla"], 1)
            pe.wait_ge(S["operands_ev"], operand("tkd", 2))
            for c in range(1, 4):
                for q in range(2):
                    t, o = (c - 1) // 2, 64 * ((c - 1) % 2)
                    if c >= 2:
                        pe.wait_ge(S["st"], 4 * (c - 2) + 2 * q + 2)
                    pe.matmul(bank[4 + q][:, 0:256], kdn[o:o + 64, t, P * q:P * q + P],
                              z[o:o + 64, t, Z_GV + 256 * q:Z_GV + 256 * q + 256], start=True, stop=True).then_inc(S["state"], 1)
            pe.wait_ge(S["st"], 12)
            pe.wait_ge(S["qz"], 8)
            for t in range(NT):
                pe.wait_ge(S["AT"], 4 * (t + 1))
                for q in range(2):
                    for c in (2 * t, 2 * t + 1):
                        if c:
                            pe.matmul(bank[t][:, 256 * q:256 * q + 256], QZ[:, q, c], st[:, c, q], start=c in (1, 2), stop=False,
                                      skip_group_check=True)
                    for hd in (2 * q, 2 * q + 1):
                        ins = pe.matmul(tile(bank[t], hd), AT[:, hd], z[:, t, Z_GV + P * hd:Z_GV + P * hd + P], start=False,
                                        stop=True, skip_group_check=True)
                ins.then_inc(S["gla_o"], 1)
            pe.wait_ge(S["go_v"], 2)
            for t in range(NT):
                for k in range(4):
                    ins = pe.transpose(tile(bank[t], k), tile(zcat[:, t], k), ident)
                ins.then_inc(S["operands"], 1)
            project4("gla", "tgo")
            pe.wait_ge(S["zy"], 4)
            transposes("tzy", zy, "zy")
            project("pout2", wat["out2"], [512, 512], "tzy")
            transposes("tffn", h, "nffn")
            pe.wait_ge(S["turned_ev"], turned("tffn", 4))
            for t in range(NT):
                accumulate(bank[4 + t][:, 0:36], [(tile(hT[:, i], t), wr[:, i]) for i in range(KT)]).then_inc(S["router"], 1)

            def keep_warm(n):
                for _ in range(n):
                    pe.matmul(bank[2][:, :], ones, cst("causal"), start=True, stop=True)

            keep_warm(10)
            w_k = [w_moe[i].rearrange("p (k n) -> p k n", k=8 if i % 3 < 2 else 4) for i in range(6)]
            pe.wait_ge(S["chosen"], NT)
            tri = cst("tri")
            pe.matmul(bank[6][:, 0:32], tri, chosen[:, 0], start=True, stop=True).then_inc(S["placed"], 1)
            accumulate(bank[7][:, 0:32], [(ones, chosen[:, 0]), (tri, chosen[:, 1])]).then_inc(S["placed"], 1)
            accumulate(bank[3][:, 0:32], [(ones, chosen[:, 0]), (ones, chosen[:, 1])]).then_inc(S["placed"], 1)
            keep_warm(5)
            pe.wait_ge(S["crowd"], 1)
            crowded = pe.value_load(crowd[0:1, 0:1], min_val=0, max_val=1)
            with pe.If(crowded == 0):
                def tokens(pairs):
                    pe.wait_ge(S["selected"], pairs)
                    for q in range(KT):
                        ins = accumulate(tile(bank[q // 4], q % 4), [(tile(h[:, t], q), msel[:, t]) for t in range(NT)])
                    ins.then_inc(S["x_sel"], 1)

                def gate_up(i, k):
                    for j in range(2):
                        pe.wait_ge(moe_landed[3 * k + j], i * 16 + 16)
                        for f in range(4):
                            ins = accumulate(bank[2 + k][:, 256 * j + CAP * f:256 * j + CAP * f + CAP],
                                             [(tile(w_k[3 * k + j][:, q], f), xs[:, q, CAP * k:CAP * k + CAP])
                                              for q in range(KT)])
                    ins.then_inc(S["moe_u"], 4)

                def down(i, k):
                    pe.wait_ge(S["hdn_made"], i * 2 + (k + 1))
                    pe.wait_ge(moe_landed[3 * k + 2], i * 16 + 16)
                    pe.wait_ge(S["moe_added"], i * 2 + (k + 3))
                    for f in range(4):
                        for c in range(2):
                            ins = pe.matmul(bank[4 + k][CAP * c:CAP * c + CAP, :], hsel[:, k, f],
                                            w_k[3 * k + 2][:, f, 512 * c:512 * c + 512], start=f == 0, stop=f == 3)
                    ins.then_inc(S["moe_y"], 4)

                tokens(1)
                with pe.Fori(0, 16) as i:
                    pe.wait_ge(S["x_sel_ev"], i * 2 + 2)
                    gate_up(i, 0)
                    gate_up(i, 1)
                    down(i, 0)
                    tokens(i + 2)
                    down(i, 1)
            with pe.Else():
                with pe.Fori(0, 16) as e:
                    for k in range(2):
                        for f in range(4):
                            pe.wait_ge(S["hdn_made"], e * 8 + (4 * k + f + 1))
                            for j in range(2):
                                if f == 0:
                                    pe.wait_ge(moe_landed[3 * k + j], e * 16 + 16)
                                accumulate(bank[f % 2 + 2 * j][:, 0:T],
                                           [(tile(w_k[3 * k + j][:, i], f), hT[:, i]) for i in range(KT)]).then_inc(
                                    S["moe_g" if j == 0 else "moe_u"], 1)
                        pe.wait_ge(S["hdn_made"], e * 8 + (4 * k + 4 + 2))
                        pe.wait_ge(moe_landed[3 * k + 2], e * 16 + 16)
                        for i in range(4):
                            t, c = i // 2, i % 2
                            pe.wait_ge(S["moe_added"], e * 8 + (4 * k + i + 1))
                            accumulate(bank[4 + i][:, :], [(tile(hdn[:, f], t), w_k[3 * k + 2][:, f, 512 * c:512 * c + 512])
                                                           for f in range(4)]).then_inc(S["moe_y"], 1)


_ROWS = {"sink": "attn_sink", "glag": "gla_norm_g_2", "b1k": "cmp_b1_k_2", "b1v": "cmp_b1_v_2", "b2k": "cmp_b2_k_2",
         "b2v": "cmp_b2_v_2"}


def kernel(**inputs):
    import concourse.bacc as bacc
    from concourse.bass_utils import run_bass_kernel_spmd

    f = {k: np.ascontiguousarray(v) for k, v in inputs.items()}

    def lane(m):
        k = m.shape[0] // P
        return m.reshape(k, P, -1).transpose(1, 0, 2).reshape(P, -1)

    def lower(m):
        out = np.zeros((P, m.shape[1]), m.dtype)
        out[:m.shape[0]] = m
        return out

    def window_rows(m):
        return m.reshape(16, 2, 64).transpose(1, 2, 0).reshape(P, 16)

    part = {
        "c": lane(f["c"].reshape(D, 1)), "cctx": lane(f["c_ctx"].reshape(D, 1)), "b_a": lane(f["gla_b_a_2"].reshape(256, 1)),
        "bs": f["gmlp_b_s"][0].T, "posk": window_rows(f["cmp_pos_k_2"][0]), "posv": window_rows(f["cmp_pos_v_2"][0]),
        "wsT": f["gmlp_w_s"][0].transpose(2, 0, 1).reshape(P, -1),
        "keysT": f["peer_sub_keys"].transpose(3, 0, 1, 2).reshape(P, -1),
        "w2k": lane(f["cmp_w2_k_2"][0]), "w2v": lane(f["cmp_w2_v_2"][0]),
        "wr": lane(np.concatenate([f["w_grp_2"][0], f["w_exp_2"][0]], 1)), "wa2": lower(f["gla_w_a2_2"][0])}
    cols = np.concatenate([part[n] for n in COL_AT], 1)
    row = {n: f[_ROWS[n]].reshape(-1) for n in _ROWS}
    row["brt"] = np.concatenate([f["b_grp_2"][0], f["b_exp_2"][0]])
    rows = np.concatenate([row[n] for n in ROW_AT])[None]
    gains = np.stack([f["norm1_g"][0], f["norm2_g"][0], f["norm1_g"][1], f["pool_scale"][0], f["norm2_g"][1], f["final_g"],
                      f["g_mix_2"][0], f["g_ffn_2"][0], f["g_final_2"]])
    pos = f["positions_2"][0]
    pos3 = np.zeros((P, 3), pos.dtype)
    pos3[:, 0:2] = pos.reshape(NT, P).T
    for g in range(2):
        pos3[32 * g:32 * g + 15, 2] = pos[31::16]
    arrays = {
        "x": f["x"][0], "ctx": f["ctx"][0], "const": shape_constants(), "cols": np.ascontiguousarray(cols), "rows": rows,
        "gains": gains, "pos3": pos3, "mod_w": f["mod_w"], "mod_b": f["mod_b"], "attn_in_w": f["attn_in_w"][0],
        "attn_out_w": f["attn_out_w"][0], "pool_w": f["pool_w"][0], "peer_w_q": f["peer_w_q"],
        "down": f["peer_down"].reshape(2 * EXPERTS, D), "up": f["peer_up"].reshape(2 * EXPERTS, D), "w_in_2": f["w_in_2"][0],
        "cmp_w1_k_2": f["cmp_w1_k_2"][0], "cmp_w1_v_2": f["cmp_w1_v_2"][0], "w_proj_nsa_2": f["w_proj_nsa_2"][0],
        "w_proj_gla_2": f["w_proj_gla_2"][0], "w_out_2": f["w_out_2"][0], "w_gate_2": f["w_gate_2"][0],
        "w_up_2": f["w_up_2"][0], "w_down_2": f["w_down_2"][0]}
    nc = bacc.Bacc("TRN2", target_bir_lowering=False, num_devices=1)
    a = {n: nc.dram_tensor(f"in_{n}", v.shape, mybir.dt.from_np(v.dtype), kind="ExternalInput").ap() for n, v in arrays.items()}
    out = nc.dram_tensor("out", (T, D), F32, kind="ExternalOutput").ap()
    program(nc, a, out)
    return run_bass_kernel_spmd(nc, [{f"in_{n}": v for n, v in arrays.items()}], core_ids=[0]).results[0]["out"].reshape(1, T, D)
```
